# Optimizing a Trainium2 kernel written in Bass

```python
import jax, jax.numpy as jnp
from jax import lax
import numpy as np

D_MODEL = 1024
BATCH = 1
SEQ = 1024
DEPTH = 1

CHUNK = 64
Q_BLOCK = 128
EPS = 1e-6

POOL_WIDTH = D_MODEL // 4
POOL_WINDOWS = (2, 4, 8, 16)
POOL_GROUPS = len(POOL_WINDOWS)
POOL_GROUP = POOL_WIDTH // POOL_GROUPS
GLA_WIDTH = D_MODEL // 4
GLA_HEADS = 4
GLA_HEAD_DIM = GLA_WIDTH // GLA_HEADS
GLA_GATE_RANK = 16
GLA_TAU = 16.0
FOX_WIDTH = D_MODEL - POOL_WIDTH - GLA_WIDTH
FOX_HEAD_DIM = 64
FOX_HEADS = FOX_WIDTH // FOX_HEAD_DIM
D_FF = ((-(-8 * D_MODEL // 3)) + 255) // 256 * 256

IN_SIZES = (POOL_WIDTH,
            GLA_WIDTH, GLA_WIDTH, GLA_WIDTH, GLA_WIDTH,
            GLA_GATE_RANK,
            FOX_WIDTH, FOX_WIDTH, FOX_WIDTH,
            FOX_HEADS)
IN_WIDTH = sum(IN_SIZES)


def _split_points():
    pts, acc = [], 0
    for s in IN_SIZES[:-1]:
        acc += s
        pts.append(acc)
    return pts

def rmsnorm(x, g):
    x32 = x.astype(jnp.float32)
    y = x32 * lax.rsqrt(jnp.mean(x32 * x32, axis=-1, keepdims=True) + EPS) * g.astype(jnp.float32)
    return y.astype(x.dtype)

def pool_mixer(u, w_pool, pool_scale):
    B, T, _ = u.shape
    u32 = u.astype(jnp.float32)
    cs = jnp.cumsum(u32, axis=1)
    cs_pad = jnp.concatenate([jnp.zeros((B, 1, POOL_WIDTH), jnp.float32), cs], axis=1)
    t1 = jnp.arange(1, T + 1)
    means = []
    for gi, w in enumerate(POOL_WINDOWS):
        lo, hi = gi * POOL_GROUP, (gi + 1) * POOL_GROUP
        lagged = jnp.concatenate([jnp.zeros((B, w - 1, POOL_GROUP), jnp.float32),
                                  cs_pad[:, :T - w + 1, lo:hi]], axis=1)
        cnt = jnp.minimum(t1, w).astype(jnp.float32)
        means.append((cs[:, :, lo:hi] - lagged) / cnt[None, :, None])
    d = (jnp.concatenate(means, axis=-1) - u32).astype(u.dtype)
    d = d.reshape(B, T, POOL_GROUPS, POOL_GROUP)
    y = jnp.einsum('btgc,gcd->btgd', d, w_pool).reshape(B, T, POOL_WIDTH)
    return y * pool_scale

def gla_mixer(q, k, v, g, a_low, w_a_up, b_a, gla_gn):
    B, T, _ = q.shape
    H, Dh, C = GLA_HEADS, GLA_HEAD_DIM, CHUNK
    NC = T // C

    def heads(z):
        return z.astype(jnp.float32).reshape(B, NC, C, H, Dh).transpose(0, 3, 1, 2, 4)

    log_a = jax.nn.log_sigmoid(jnp.einsum('btr,rd->btd', a_low.astype(jnp.float32),
                                          w_a_up.astype(jnp.float32)) + b_a.astype(jnp.float32)) / GLA_TAU
    qh = heads(q) * (Dh ** -0.5)
    kh, vh, la = heads(k), heads(v), heads(log_a)
    bcum = jnp.cumsum(la, axis=3)
    b_last = bcum[:, :, :, -1:, :]
    ref = bcum[:, :, :, C // 2 - 1:C // 2, :]

    q_in = qh * jnp.exp(bcum - ref)
    k_in = kh * jnp.exp(ref - bcum)
    causal = jnp.tril(jnp.ones((C, C), dtype=bool))
    att = jnp.where(causal, jnp.einsum('bhncd,bhnsd->bhncs', q_in, k_in), 0.0)
    o_intra = jnp.einsum('bhncs,bhnse->bhnce', att, vh)

    kv = jnp.einsum('bhncd,bhnce->bhnde', kh * jnp.exp(b_last - bcum), vh)
    dec = jnp.exp(b_last[:, :, :, 0, :])

    def step(S, inp):
        kv_n, dec_n = inp
        return dec_n[..., None] * S + kv_n, S

    S0 = jnp.zeros((B, H, Dh, Dh), jnp.float32)
    _, S_prev = lax.scan(step, S0, (kv.transpose(2, 0, 1, 3, 4), dec.transpose(2, 0, 1, 3)))
    S_prev = S_prev.transpose(1, 2, 0, 3, 4)
    o_inter = jnp.einsum('bhncd,bhnde->bhnce', qh * jnp.exp(bcum), S_prev)

    o = o_intra + o_inter
    o = o * lax.rsqrt(jnp.mean(o * o, axis=-1, keepdims=True) + EPS)
    o = o.transpose(0, 2, 3, 1, 4).reshape(B, T, GLA_WIDTH) * gla_gn.astype(jnp.float32)
    return (o * jax.nn.silu(g.astype(jnp.float32))).astype(q.dtype)

def fox_mixer(q, k, v, f_logit, b_f):
    B, T, _ = q.shape
    H, Dh = FOX_HEADS, FOX_HEAD_DIM
    nb = T // Q_BLOCK

    def heads(z):
        return z.astype(jnp.float32).reshape(B, T, H, Dh).transpose(0, 2, 1, 3)

    qh = heads(q) * (Dh ** -0.5)
    kh, vh = heads(k), heads(v)
    logf = jax.nn.log_sigmoid(f_logit.astype(jnp.float32) + b_f.astype(jnp.float32))
    F = jnp.cumsum(logf, axis=1).transpose(0, 2, 1)
    q_blocks = qh.reshape(B, H, nb, Q_BLOCK, Dh).transpose(2, 0, 1, 3, 4)
    F_blocks = F.reshape(B, H, nb, Q_BLOCK).transpose(2, 0, 1, 3)
    kpos = jnp.arange(T)

    def block(args):
        qb, Fb, i = args
        s = jnp.einsum('bhqd,bhkd->bhqk', qb, kh) + Fb[..., None] - F[:, :, None, :]
        qpos = i * Q_BLOCK + jnp.arange(Q_BLOCK)
        s = jnp.where(kpos[None, :] <= qpos[:, None], s, -jnp.inf)
        p = jax.nn.softmax(s, axis=-1)
        return jnp.einsum('bhqk,bhkd->bhqd', p, vh)

    o = lax.map(block, (q_blocks, F_blocks, jnp.arange(nb)))
    return o.transpose(1, 0, 3, 2, 4).reshape(B, T, FOX_WIDTH).astype(q.dtype)

def first_inputs(seed: int = 0) -> dict:
    key = jax.random.key(seed)
    ks = jax.random.split(key, 16)
    f32 = jnp.float32
    nrm = lambda k, shape: jax.random.normal(k, shape, f32)
    return {
        "x": nrm(ks[0], (BATCH, SEQ, D_MODEL)),
        "ln1": 1.0 + 0.02 * nrm(ks[1], (DEPTH, D_MODEL)),
        "w_in": nrm(ks[2], (DEPTH, D_MODEL, IN_WIDTH)) * D_MODEL ** -0.5,
        "w_pool": nrm(ks[3], (DEPTH, POOL_GROUPS, POOL_GROUP, POOL_GROUP)) * POOL_GROUP ** -0.5,
        "pool_scale": 0.5 + 0.1 * nrm(ks[4], (DEPTH, POOL_WIDTH)),
        "w_a_up": nrm(ks[5], (DEPTH, GLA_GATE_RANK, GLA_WIDTH)) * GLA_GATE_RANK ** -0.5,
        "b_a": 0.1 * nrm(ks[6], (DEPTH, GLA_WIDTH)),
        "gla_gn": 1.0 + 0.02 * nrm(ks[7], (DEPTH, GLA_WIDTH)),
        "b_f": 3.0 + 0.5 * nrm(ks[8], (DEPTH, FOX_HEADS)),
        "w_o": nrm(ks[9], (DEPTH, D_MODEL, D_MODEL)) * D_MODEL ** -0.5,
        "ln2": 1.0 + 0.02 * nrm(ks[10], (DEPTH, D_MODEL)),
        "w_gu": nrm(ks[11], (DEPTH, D_MODEL, 2 * D_FF)) * D_MODEL ** -0.5,
        "w_down": nrm(ks[12], (DEPTH, D_FF, D_MODEL)) * D_FF ** -0.5,
        "ln_f": 1.0 + 0.02 * nrm(ks[13], (D_MODEL,)),
    }

def first_block(x, ln1, w_in, w_pool, pool_scale, w_a_up, b_a, gla_gn, b_f, w_o, ln2, w_gu, w_down, ln_f):
    pts = _split_points()
    for l in range(DEPTH):
        h = rmsnorm(x, ln1[l])
        z = jnp.einsum('btd,de->bte', h, w_in[l])
        u_pool, gq, gk, gv, gg, ga, fq, fk, fv, ff = jnp.split(z, pts, axis=-1)
        y_pool = pool_mixer(u_pool, w_pool[l], pool_scale[l])
        y_gla = gla_mixer(gq, gk, gv, gg, ga, w_a_up[l], b_a[l], gla_gn[l])
        y_fox = fox_mixer(fq, fk, fv, ff, b_f[l])
        mix = jnp.concatenate([y_pool.astype(x.dtype), y_gla.astype(x.dtype), y_fox.astype(x.dtype)], axis=-1)
        x = x + jnp.einsum('btd,de->bte', mix, w_o[l])
        h = rmsnorm(x, ln2[l])
        gate, up = jnp.split(jnp.einsum('btd,df->btf', h, w_gu[l]), 2, axis=-1)
        x = x + jnp.einsum('btf,fd->btd', jax.nn.silu(gate) * up, w_down[l])
    return rmsnorm(x, ln_f)


N_MIXERS = 3
PLE_DIM = 256
MLA_HEADS = 16
MLA_Q_LORA = 384
MLA_KV_LORA = 256
MLA_NOPE = 64
MLA_ROPE = 32
MLA_V = 64
MLA_WIDTH = MLA_HEADS * MLA_V
MLA_IN = MLA_Q_LORA + MLA_KV_LORA + MLA_ROPE + MLA_WIDTH
ROPE_THETA = 10000.0
CONV_WIDTH = 3
CONV_DIM = D_MODEL
CONV_IN = 4 * CONV_DIM
MLSTM_HEADS = 4
MLSTM_INNER = 2 * D_MODEL
MLSTM_DV = MLSTM_INNER // MLSTM_HEADS
MLSTM_DK = MLSTM_DV // 2
MLSTM_IN = 2 * MLSTM_HEADS * MLSTM_DK + 3 * MLSTM_INNER + 2 * MLSTM_HEADS


def rmsnorm_2(x, g=None):
    xf = x.astype(jnp.float32)
    y = xf * lax.rsqrt(jnp.mean(xf * xf, axis=-1, keepdims=True) + EPS)
    if g is not None:
        y = y * g.astype(jnp.float32)
    return y.astype(x.dtype)

def rope_cos_sin(positions, dim, dtype):
    inv = ROPE_THETA ** (-jnp.arange(0, dim, 2, dtype=jnp.float32) / dim)
    ang = positions.astype(jnp.float32)[..., None] * inv
    return jnp.cos(ang).astype(dtype), jnp.sin(ang).astype(dtype)

def apply_rope(x, cos, sin):
    x1, x2 = jnp.split(x, 2, axis=-1)
    return jnp.concatenate([x1 * cos - x2 * sin, x1 * sin + x2 * cos], axis=-1)

def mla_mixer(h, cos, sin, w_in, q_norm, w_q_b, kv_norm, w_kv_b, w_out):
    B, S, _ = h.shape
    u = h @ w_in
    c_q, c_kv, k_rope, z = jnp.split(
        u, [MLA_Q_LORA, MLA_Q_LORA + MLA_KV_LORA, MLA_Q_LORA + MLA_KV_LORA + MLA_ROPE], axis=-1)
    q = (rmsnorm_2(c_q, q_norm) @ w_q_b).reshape(B, S, MLA_HEADS, MLA_NOPE + MLA_ROPE)
    q_nope = q[..., :MLA_NOPE]
    q_rope = apply_rope(q[..., MLA_NOPE:], cos[:, :, None], sin[:, :, None])
    kv = (rmsnorm_2(c_kv, kv_norm) @ w_kv_b).reshape(B, S, MLA_HEADS, MLA_NOPE + MLA_V)
    k_nope, v = kv[..., :MLA_NOPE], kv[..., MLA_NOPE:]
    k_rope = apply_rope(k_rope, cos, sin)
    scale = (MLA_NOPE + MLA_ROPE) ** -0.5
    outs = []
    for blk in range(S // Q_BLOCK):
        q0, q1 = blk * Q_BLOCK, (blk + 1) * Q_BLOCK
        s = (jnp.einsum('bqhd,bkhd->bhqk', q_nope[:, q0:q1], k_nope[:, :q1])
             + jnp.einsum('bqhd,bkd->bhqk', q_rope[:, q0:q1], k_rope[:, :q1])).astype(jnp.float32) * scale
        q_chunk = (q0 + jnp.arange(Q_BLOCK)) // CHUNK
        k_chunk = jnp.arange(q1) // CHUNK
        s = jnp.where(k_chunk[None, :] <= q_chunk[:, None], s, -jnp.inf)
        prob = jax.nn.softmax(s, axis=-1).astype(v.dtype)
        outs.append(jnp.einsum('bhqk,bkhd->bqhd', prob, v[:, :q1]))
    o = jnp.concatenate(outs, axis=1).reshape(B, S, MLA_WIDTH)
    return (o * jax.nn.silu(z)) @ w_out

def shortconv_mixer(h, w_in, conv_w, w_out):
    b_gate, c_gate, hx, z = jnp.split(h @ w_in, 4, axis=-1)
    y = lax.conv_general_dilated(
        c_gate * hx, conv_w[:, None, :].astype(hx.dtype), window_strides=(1,),
        padding=[(CONV_WIDTH - 1, 0)], dimension_numbers=('NWC', 'WIO', 'NWC'),
        feature_group_count=CONV_DIM)
    return (b_gate * y * jax.nn.silu(z)) @ w_out

def mlstm_chunk_step(carry, xs):
    C, n, m = carry
    q, k, v, ig, lf = xs
    L = q.shape[2]
    b = jnp.cumsum(lf, axis=-1)
    causal = jnp.tril(jnp.ones((L, L), dtype=bool))
    d_log = jnp.where(causal, b[..., :, None] - b[..., None, :] + ig[..., None, :], -jnp.inf)
    g = b + m[..., None]
    m_t = jnp.maximum(g, jnp.max(d_log, axis=-1))
    w_intra = jnp.exp(d_log - m_t[..., None])
    w_inter = jnp.exp(g - m_t)
    s = jnp.einsum('bhtd,bhsd->bhts', q, k) * w_intra
    num = (w_inter[..., None] * jnp.einsum('bhtd,bhdv->bhtv', q, C)
           + jnp.einsum('bhts,bhsv->bhtv', s, v))
    den = w_inter * jnp.einsum('bhtd,bhd->bht', q, n) + jnp.sum(s, axis=-1)
    h = num / jnp.maximum(jnp.abs(den), jnp.exp(-m_t))[..., None]
    b_last = b[..., -1]
    d_state = b_last[..., None] - b + ig
    m_new = jnp.maximum(b_last + m, jnp.max(d_state, axis=-1))
    w_s = jnp.exp(d_state - m_new[..., None])
    decay = jnp.exp(b_last + m - m_new)
    C = decay[..., None, None] * C + jnp.einsum('bhs,bhsd,bhsv->bhdv', w_s, k, v)
    n = decay[..., None] * n + jnp.einsum('bhs,bhsd->bhd', w_s, k)
    return (C, n, m_new), h

def mlstm_mixer(h, w_in, b_gates, w_out):
    B, S, _ = h.shape
    H, DK, DV = MLSTM_HEADS, MLSTM_DK, MLSTM_DV
    qk = H * DK
    u = h @ w_in
    q, k, v, o, z, gates = jnp.split(
        u, [qk, 2 * qk, 2 * qk + MLSTM_INNER, 2 * qk + 2 * MLSTM_INNER, 2 * qk + 3 * MLSTM_INNER], axis=-1)
    gates = gates.astype(jnp.float32) + b_gates.astype(jnp.float32)
    ig = gates[..., :H]
    lf = jax.nn.log_sigmoid(gates[..., H:])
    nc = S // CHUNK

    def to_chunks(t, d):
        return t.astype(jnp.float32).reshape(B, nc, CHUNK, H, d).transpose(1, 0, 3, 2, 4)

    def gate_chunks(t):
        return t.reshape(B, nc, CHUNK, H).transpose(1, 0, 3, 2)

    xs = (to_chunks(q, DK), to_chunks(k, DK) * (DK ** -0.5), to_chunks(v, DV),
          gate_chunks(ig), gate_chunks(lf))
    init = (jnp.zeros((B, H, DK, DV), jnp.float32), jnp.zeros((B, H, DK), jnp.float32),
            jnp.zeros((B, H), jnp.float32))
    _, hc = lax.scan(mlstm_chunk_step, init, xs)
    hs = hc.transpose(1, 0, 3, 2, 4).reshape(B, S, MLSTM_INNER).astype(h.dtype)
    return (jax.nn.sigmoid(o) * hs * jax.nn.silu(z)) @ w_out

def second_inputs(seed: int = 0) -> dict:
    key = jax.random.key(seed)
    ks = iter(jax.random.split(key, 32))
    n_mla = max(0, (DEPTH - 0 + 2) // 3)
    n_conv = max(0, (DEPTH - 1 + 2) // 3)
    n_mlstm = max(0, (DEPTH - 2 + 2) // 3)
    res_scale = (2.0 * DEPTH) ** -0.5

    def nrm(shape, scale):
        return jax.random.normal(next(ks), shape, jnp.float32) * scale

    def gain(shape):
        return 1.0 + nrm(shape, 0.02)

    x = nrm((BATCH, SEQ, D_MODEL), 1.0)
    p = nrm((DEPTH, BATCH, SEQ, PLE_DIM), 1.0)
    offsets = jax.random.randint(next(ks), (BATCH, 1), 0, 4096, dtype=jnp.int32)
    positions = (offsets + jnp.arange(SEQ, dtype=jnp.int32)[None, :]).astype(jnp.int32)
    norm_g = gain((DEPTH, D_MODEL))
    mla_w_in = nrm((n_mla, D_MODEL, MLA_IN), D_MODEL ** -0.5)
    mla_q_norm = gain((n_mla, MLA_Q_LORA))
    mla_w_q_b = nrm((n_mla, MLA_Q_LORA, MLA_HEADS * (MLA_NOPE + MLA_ROPE)), MLA_Q_LORA ** -0.5)
    mla_kv_norm = gain((n_mla, MLA_KV_LORA))
    mla_w_kv_b = nrm((n_mla, MLA_KV_LORA, MLA_HEADS * (MLA_NOPE + MLA_V)), MLA_KV_LORA ** -0.5)
    mla_w_out = nrm((n_mla, MLA_WIDTH, D_MODEL), MLA_WIDTH ** -0.5 * res_scale)
    conv_w_in = nrm((n_conv, D_MODEL, CONV_IN), D_MODEL ** -0.5)
    conv_w = nrm((n_conv, CONV_WIDTH, CONV_DIM), CONV_WIDTH ** -0.5)
    conv_w_out = nrm((n_conv, CONV_DIM, D_MODEL), CONV_DIM ** -0.5 * res_scale)
    mlstm_w_in = nrm((n_mlstm, D_MODEL, MLSTM_IN), D_MODEL ** -0.5)
    b_in = nrm((n_mlstm, MLSTM_HEADS), 0.1)
    b_f = jnp.linspace(3.0, 6.0, MLSTM_HEADS, dtype=jnp.float32)[None, :] + nrm((n_mlstm, MLSTM_HEADS), 0.1)
    mlstm_b_gates = jnp.concatenate([b_in, b_f], axis=-1)
    mlstm_w_out = nrm((n_mlstm, MLSTM_INNER, D_MODEL), MLSTM_INNER ** -0.5 * res_scale)
    ple_proj = nrm((DEPTH, PLE_DIM, D_MODEL), PLE_DIM ** -0.5 * res_scale)
    ple_gate = nrm((DEPTH, D_MODEL, D_MODEL), D_MODEL ** -0.5)
    final_norm = gain((D_MODEL,))
    return {"x": x, "p": p, "positions": positions, "norm_g": norm_g,
            "mla_w_in": mla_w_in, "mla_q_norm": mla_q_norm, "mla_w_q_b": mla_w_q_b,
            "mla_kv_norm": mla_kv_norm, "mla_w_kv_b": mla_w_kv_b, "mla_w_out": mla_w_out,
            "conv_w_in": conv_w_in, "conv_w": conv_w, "conv_w_out": conv_w_out,
            "mlstm_w_in": mlstm_w_in, "mlstm_b_gates": mlstm_b_gates, "mlstm_w_out": mlstm_w_out,
            "ple_proj": ple_proj, "ple_gate": ple_gate, "final_norm": final_norm}

def second_block(x, p, positions, norm_g, mla_w_in, mla_q_norm, mla_w_q_b, mla_kv_norm, mla_w_kv_b,
              mla_w_out, conv_w_in, conv_w, conv_w_out, mlstm_w_in, mlstm_b_gates, mlstm_w_out,
              ple_proj, ple_gate, final_norm):
    cos, sin = rope_cos_sin(positions, MLA_ROPE, x.dtype)
    for i in range(DEPTH):
        kind, j = i % N_MIXERS, i // N_MIXERS
        h = rmsnorm_2(x, norm_g[i])
        if kind == 0:
            y = mla_mixer(h, cos, sin, mla_w_in[j], mla_q_norm[j], mla_w_q_b[j],
                          mla_kv_norm[j], mla_w_kv_b[j], mla_w_out[j])
        elif kind == 1:
            y = shortconv_mixer(h, conv_w_in[j], conv_w[j], conv_w_out[j])
        else:
            y = mlstm_mixer(h, mlstm_w_in[j], mlstm_b_gates[j], mlstm_w_out[j])
        x = x + y
        gate = jax.nn.sigmoid(rmsnorm_2(x) @ ple_gate[i])
        x = x + gate * (p[i] @ ple_proj[i])
    return rmsnorm_2(x, final_norm)


def setup_inputs(seed=0):
    out = dict(first_inputs(seed))
    for name, value in second_inputs(seed + 1).items():
        if name != "x":
            out[name + "_2"] = value
    return out


def reference(
    x, ln1, w_in, w_pool, pool_scale, w_a_up, b_a, gla_gn, b_f, w_o, ln2, w_gu, w_down, ln_f,
    p_2, positions_2, norm_g_2, mla_w_in_2, mla_q_norm_2, mla_w_q_b_2, mla_kv_norm_2,
    mla_w_kv_b_2, mla_w_out_2, conv_w_in_2, conv_w_2, conv_w_out_2, mlstm_w_in_2,
    mlstm_b_gates_2, mlstm_w_out_2, ple_proj_2, ple_gate_2, final_norm_2,
):
    x = first_block(
        x, ln1, w_in, w_pool, pool_scale, w_a_up, b_a, gla_gn, b_f, w_o, ln2, w_gu, w_down,
        ln_f,
    )
    return second_block(
        x, p_2, positions_2, norm_g_2, mla_w_in_2, mla_q_norm_2, mla_w_q_b_2, mla_kv_norm_2,
        mla_w_kv_b_2, mla_w_out_2, conv_w_in_2, conv_w_2, conv_w_out_2, mlstm_w_in_2,
        mlstm_b_gates_2, mlstm_w_out_2, ple_proj_2, ple_gate_2, final_norm_2,
    )


_drawn_inputs = setup_inputs


def setup_inputs(seed=0):
    import zlib

    import numpy as np

    out = dict(_drawn_inputs(seed))
    spreads = {}
    factors = {'ln1': 3.611,
     'b_a': 4.171,
     'gla_gn': 8.0,
     'ln2': 4.472,
     'ln_f': 2.897,
     'norm_g_2': 8.0,
     'mla_q_norm_2': 8.0,
     'mla_kv_norm_2': 8.0,
     'p_2': 4.55,
     'ple_proj_2': 4.549,
     'ple_gate_2': 8.0}
    for name, (base, spread) in spreads.items():
        noise = np.random.default_rng([zlib.crc32(name.encode()), seed]).standard_normal(out[name].shape)
        drawn = base * np.exp(spread * noise) if base else spread * noise
        out[name] = __import__('jax').numpy.asarray(drawn.astype(out[name].dtype))
    for name, factor in factors.items():
        out[name] = (out[name] * factor).astype(out[name].dtype)
    return out
```

```python
from contextlib import ExitStack

import numpy as np

import concourse.bass as bass
from concourse import mybir

F32 = mybir.dt.float32
F32R = mybir.dt.float32r
BF16 = mybir.dt.bfloat16
U32 = mybir.dt.uint32
I32 = mybir.dt.int32
ALU = mybir.AluOpType
ACT = mybir.ActivationFunctionType
AX_X = mybir.AxisListType.X

P = 128
T = 1024
D = 1024
DT = D // P
HALF = 512
EPS = 1e-6
CHUNK = 64
NCH = T // CHUNK

POOL_W = GLA_W = 256
GLA_TAU = 16.0
FOX_W = 512
FOX_H = 8
HD = 64
FF = 2816
FT = FF // P
MLP_CHUNKS = (6, 6, 5, 5)
MLA_H = 16
QL, KVL, NOPE, ROPE = 384, 256, 64, 32
MLA_SCALE = (NOPE + ROPE) ** -0.5
ROPE_THETA = 10000.0
NEG = -1.0e30

C_POOL, C_GQ, C_GK, C_GV, C_GG, C_GA = 0, 256, 512, 768, 1024, 1280
C_FQ = 1296
C_FK, C_FV, C_FF = C_FQ + FOX_W, C_FQ + 2 * FOX_W, C_FQ + 3 * FOX_W

U_SMALL = 0
U_FV = U_SMALL + 1
U_FQK = U_FV + FOX_H // 2
U_REST = U_FQK + FOX_H
N_REST = 10
U_WO = U_REST + N_REST
U_GU, U_DN = [], []
_u = U_WO + DT
for _n in MLP_CHUNKS:
    U_GU.append(_u)
    U_DN.append(_u + 2 * _n)
    _u += 2 * _n + DT
U_MIN = _u
U_Z = U_MIN + 6
U_HEAD = U_Z + DT
U_MO = U_HEAD + MLA_H
U_PLE = U_MO + DT
N_UNITS = U_PLE + 2 * DT

V_LN1, V_LN2, V_LNF, V_NG = 0, 8, 16, 24
V_GN, V_BA, V_PS, V_QN, V_KVN, V_BF, V_FN = 32, 34, 36, 38, 41, 43, 44
V_WPOOL, V_WAUP = 56, 56 + 256
N_VEC = 56 + 512

K_ID, K_ONE, K_BLK = 0, 128, 256
K_MASK = 384
K_ATT = K_MASK + 4 * 256
K_CNT = K_ATT + 128
K_FREQ, K_SIGN, K_EPS = K_CNT + 32, K_CNT + 33, K_CNT + 34
N_CONST = K_CNT + 40


def build(nc, wpack, xT, pT, vecs, consts, pos, outT, f_rows):
    with ExitStack() as ctx:
        def sem(name):
            return ctx.enter_context(nc.semaphore(name))

        base = (nc.sbuf_base + 63) // 64 * 64
        R_X = base
        R_S = R_X + 32768
        R_M = R_S + 28672
        R_H = R_M + 32768
        R_RING = R_H + 65536
        R_W = R_RING + 24576
        R_C = R_W + 20480
        top = [R_C]

        def at(name, offset, shape, dt=F32):
            return nc.alloc_sbuf_tensor_at(name, shape, dt, offset=offset)

        def const(name, shape, dt=F32):
            n = int(np.prod(shape[1:])) * mybir.dt.size(dt)
            off = top[0]
            top[0] += (n + 31) // 32 * 32
            return at(name, off, shape, dt)

        x = at("x", R_X, [P, DT, T])
        h_hi = at("h_hi", R_H, [P, DT, T], F32R)
        h_lo = at("h_lo", R_H + 32768, [P, DT, T], F32R)
        mix = at("mix", R_M, [P, DT, T])
        raw = [at(f"w_raw{s}", R_RING + 4096 * s, [P, DT, P]) for s in range(2)]
        w_hi = [at(f"w_hi{s}", R_RING + 8192 + 4096 * s, [P, DT, P], F32R) for s in range(2)]
        w_lo = [at(f"w_lo{s}", R_RING + 16384 + 4096 * s, [P, DT, P], F32R) for s in range(2)]
        ssq = at("ssq", R_W, [P, T])
        diag = at("diag", R_W + 4096, [P, T])
        tmp = [at(f"tmp{s}", R_W + 8192 + 4096 * s, [P, T]) for s in range(2)]
        sq = at("sq", R_W + 16384, [P, T])
        cos_sin = at("cos_sin", R_S, [P, T])

        vec = const("vec", [P, N_VEC])
        ident = const("ident", [P, P])
        ones = const("ones", [P, P])
        head_mean = const("head_mean", [P, P])
        small_const = const("small_const", [P, 40])
        ident_bf = const("ident_bf", [P, P], BF16)
        masks = const("masks", [P, 4, 256], BF16)
        att_mask = const("att_mask", [P, P], U32)
        rt = const("rt", [P, 16])
        rv = const("rv", [P, 16])
        mx = const("mx", [P, 8])
        zero = const("zero", [P, 1])
        c_neg = const("c_neg", [DT, P], F32R)
        assert top[0] <= nc.sbuf_usable_end, top[0]
        eps = small_const[:, K_EPS - K_CNT:K_EPS - K_CNT + 1]

        PS = ctx.enter_context(nc.psum_tensor("ps", [P, 8, HALF], F32))
        pjA, pjB = PS[:, 0:2, :], PS[:, 2:4, :]

        def flat(ap):
            return ap.rearrange("p a n -> p (a n)")

        w_loaded = [sem(f"w_loaded{s}") for s in range(2)]
        w_hi_done = sem("w_hi_done")
        w_split = sem("w_split")
        unit_done = sem("unit_done")
        consts_in, vecs_in, pos_in = sem("consts_in"), sem("vecs_in"), sem("pos_in")
        x_in = [sem(f"x_in{k}") for k in range(DT)]
        x_back = sem("x_back")
        zero_set = sem("zero_set")
        setup_done = sem("setup_done")
        rope_s = sem("rope_steps")
        rope_a = sem("rope_sines")
        out_stored = [sem(f"out_stored{s}") for s in range(2)]

        norm_sem = {k: sem(f"norm_{k}") for k in ("sq", "ssq", "ms", "rt", "rv", "diag", "bc", "h", "hi", "lo")}
        counted = dict.fromkeys(norm_sem, 0)

        class Norm:
            def __init__(self, tiles, sums, split=True):
                self.base = dict(counted)
                for k in ("sq", "h") + ("hi", "lo") * split:
                    counted[k] += tiles
                counted["ssq"] += sums
                for k in ("ms", "rt", "rv", "diag", "bc"):
                    counted[k] += 1

            def __getitem__(self, k):
                return norm_sem[k]

            def wait(self, eng, k, n):
                eng.wait_ge(norm_sem[k], n + self.base[k])

        N1, N2, NF, N3, NQ, NKV, N4, N5 = (Norm(*n) for n in ((DT, DT), (DT, DT + 1), (DT, DT + 1, False), (DT, DT), (3, 3), (2, 2), (DT, DT + 1), (DT, DT + 1)))

        def project(pe, slot, kts, hi, lo, dst, done=True, halves=(0, 1)):
            last = None
            for half in halves:
                t = slice(half * HALF, (half + 1) * HALF)
                n, total = 0, 3 * len(kts)
                for w, a in ((w_lo, hi), (w_hi, lo), (w_hi, hi)):
                    for i, kt in enumerate(kts):
                        last = nc.tensor.matmul(dst[:, half, :], w[slot][:, kt, :], a[:, i, t],
                                                start=(n == 0), stop=(n == total - 1))
                        n += 1
            if done:
                last.then_inc(unit_done, 1)
            return last

        def norm_pe(pe, s, n_ssq, col=0):
            s.wait(pe, "ssq", n_ssq)
            for b in range(DT):
                last = nc.tensor.matmul(PS[:, 7, col + b:col + b + 1], ssq[:, b * P:(b + 1) * P], ones[:, 0:1],
                                        start=True, stop=True)
            last.then_inc(s["ms"], 1)
            s.wait(pe, "diag", 1)
            for half in range(2):
                last = nc.tensor.matmul(PS[:, 4 + half, :], ones[:, :], diag[:, half * HALF:(half + 1) * HALF],
                                        start=True, stop=True)
            last.then_inc(s["bc"], 1)

        def norm_root(act, s, width, col=0):
            s.wait(act, "ms", 1)
            nc.scalar.activation(rt[:, 0:DT], PS[:, 7, col:col + DT], ACT.Sqrt, bias=eps, scale=1.0 / width)\
                .then_inc(s["rt"], 1)

        def norm_spread(dve, s):
            s.wait(dve, "rt", 1)
            nc.vector.reciprocal(rv[:, 0:DT], rt[:, 0:DT]).then_inc(s["rv"], 1)
            s.wait(dve, "rv", 1)
            for b in range(DT):
                last = nc.vector.tensor_scalar(diag[:, b * P:(b + 1) * P], ident[:, :], rv[:, b:b + 1], None, ALU.mult)
            last.then_inc(s["diag"], 1)
            s.wait(dve, "bc", 1)

        def norm_scaled(s, dst, src, gain):
            if gain is None:
                return nc.vector.tensor_tensor(dst, src, flat(PS[:, 4:6, :]), ALU.mult)
            return nc.vector.scalar_tensor_tensor(dst, src, gain, flat(PS[:, 4:6, :]), ALU.mult, ALU.mult)

        def norm_split_dve(dve, s, n, src, gain, hi, lo):
            for k in range(n + 1):
                if k < n:
                    if k >= 2:
                        s.wait(dve, "lo", k - 1)
                    norm_scaled(s, tmp[k % 2][:, :], src(k), gain(k)).then_inc(s["h"], 1)
                if k >= 1:
                    s.wait(dve, "hi", k)
                    nc.vector.tensor_tensor(lo(k - 1), tmp[(k - 1) % 2][:, :], hi(k - 1).bitcast(F32), ALU.subtract)\
                        .then_inc(s["lo"], 1)

        def norm_split_act(act, s, n, hi):
            for k in range(n):
                s.wait(act, "h", k + 1)
                nc.scalar.activation(hi(k), tmp[k % 2][:, :], ACT.Copy).then_inc(s["hi"], 1)

        def gain_of(col):
            return lambda k: vec[:, col + k:col + k + 1]

        def hi_tile(k):
            return h_hi[:, k, :]

        def lo_tile(k):
            return h_lo[:, k, :]

        def units_pe(pe, first, n, kts, hi, lo, free):
            with pe.Fori(0, n // 2) as it:
                for j, dst in enumerate((pjA, pjB)):
                    pe.wait_ge(w_split, it * 2 + (first + j + 3))
                    free(it, j)
                    project(pe, (first + j) % 2, kts, hi, lo, dst)

        def residual_dve(dve, first, added, added0, s=None, ssq_first=True):
            if s is not None:
                nc.vector.memset(ssq[:, :], 0.0).then_inc(s["ssq"], 1)
            with dve.Fori(0, DT // 2) as it:
                for j, src in enumerate((pjA, pjB)):
                    tile = flat(x[:, bass.ds(it * 2 + j, 1), :])
                    dve.wait_ge(unit_done, it * 2 + (first + j + 3))
                    nc.vector.tensor_tensor(tile, flat(src), tile, ALU.add).then_inc(added, 1)
                    if s is not None:
                        s.wait(dve, "sq", it * 2 + (j + 1))
                        s.wait(dve, "ssq", it * 2 + (j + 1))
                        nc.vector.tensor_tensor(ssq[:, :], ssq[:, :], sq[:, :], ALU.add).then_inc(s["ssq"], 1)

        def residual_squares(act, added, added0, s):
            with act.Fori(0, DT // 2) as it:
                for j in range(2):
                    act.wait_ge(added, it * 2 + (added0 + j + 3))
                    nc.scalar.activation(sq[:, :], flat(x[:, bass.ds(it * 2 + j, 1), :]), ACT.Square).then_inc(s["sq"], 1)

        class Attention:

            def __init__(self, k, heads, rows_max, rows, mask):
                self.k, self.heads, self.rows_max, self.rows, self.mask = k, heads, rows_max, rows, mask
                self.s_ready = sem(f"{k}_s_ready")
                self.exp_done = sem(f"{k}_exp_done")
                self.pv_done = sem(f"{k}_pv_done")
                self.vt_ready = sem(f"{k}_vt_ready")
                self.vT_done = sem(f"{k}_vT_done")
                self.vaug_done = sem(f"{k}_vaug_done")
                self.mp_ready = sem(f"{k}_mp_ready")
                self.max_done = sem(f"{k}_max_done")
                self.mT_ready = sem(f"{k}_mT_ready")
                self.cneg_done = sem(f"{k}_cneg_done")
                self.hi_done = sem(f"{k}_hi_done")
                self.lo_done = sem(f"{k}_lo_done")
                self.rope_done = sem(f"{k}_rope_done")
                self.ln_done = sem(f"{k}_ln_done")
                self.r0_done = sem(f"{k}_r0_done")
                self.newton = sem(f"{k}_newton")
                self.norm_done = sem(f"{k}_norm_done")
                self.mx_done = sem(f"{k}_mx_done")
                self.setup = sem(f"{k}_setup")
                self.row_in = [sem(f"{k}_row_in{b}") for b in range(2)]


        PIECES = []
        for half in range(2):
            for j in range(4 * (half + 1)):
                d = j * P - half * HALF
                PIECES.append((half, j, min(max(d, 0), 256), d))
        N_PIECES = len(PIECES)
        LAST_OF_HALF = (3, N_PIECES - 1)
        S_BANK, O_BANK = (4, 5), (6, 7)
        MAX_BANK = ((2, 0), (3, 0), (0, 0), (1, 0), (2, 2), (0, 4), (2, 5), (0, 6))
        MAX_AFTER = {3: (0,), 4: (1, 2), 5: (3,), 6: (4,), 7: (5,), 8: (6,), 9: (7,)}
        N_MAX = len(MAX_BANK)
        V_BANK, M_BANK = 2, 3
        Pt = [at(f"probs{s}", R_W + 8192 + 2048 * s, [P, HALF]) for s in range(4)]
        ln_sum = at("ln_sum", R_W, [P, HALF])
        r0 = at("r0", R_W + 2048, [P, HALF])
        newton = at("newton", R_W + 4096, [P, HALF])
        rec = at("rec", R_W + 6144, [P, HALF])

        def max_width(i):
            w = max(256, (i % 4 + 1) * P)
            return w, i // 4 * HALF + w

        def buffers(k, q_at, klo_at, vaug_at):
            q_hi = [at(f"{k}_q_hi{b}", q_at + 4096 * b, [P, T], F32R) for b in range(2)]
            q_lo = [at(f"{k}_q_lo{b}", q_at + 8192 + 4096 * b, [P, T], F32R) for b in range(2)]
            k_hi = [at(f"{k}_k_hi{b}", q_at + 16384 + 4096 * b, [P, T], F32R) for b in range(2)]
            k_lo = [at(f"{k}_k_lo{b}", klo_at + 4096 * b, [P, T], F32R) for b in range(2)]
            vaug = [at(f"{k}_vaug{b}", vaug_at + 4096 * b, [P, DT, P]) for b in range(2)]
            return q_hi, q_lo, k_hi, k_lo, vaug

        def score_pe(pe, A, n, b, g):
            q_hi, q_lo, k_hi, k_lo, vaug = A.bufs
            half, j, off, d = PIECES[g]
            bank = S_BANK[g % 2]
            out = PS[:, bank, 0:HALF - off]
            t = slice(half * HALF + off, (half + 1) * HALF)
            r = slice(0, A.rows)
            keys = slice(j * P, (j + 1) * P)
            masked = d >= 0
            nc.tensor.matmul(out, k_lo[b][r, keys], q_hi[b][r, t], start=True, stop=False)
            nc.tensor.matmul(out, k_hi[b][r, keys], q_lo[b][r, t], start=False, stop=False)
            last = nc.tensor.matmul(out, k_hi[b][r, keys], q_hi[b][r, t], start=False, stop=not masked)
            if masked:
                extra = d - off
                m = masks[:, A.mask + 1, P - extra:2 * P]
                last = nc.tensor.matmul(PS[:, bank, 0:P + extra], ident_bf[:, :], m, start=False, stop=True)
            last.then_inc(A.s_ready, 1)

        def value_pe(pe, A, n, b, g):
            half, j, off, d = PIECES[g]
            if j == 0 and not (isinstance(n, int) and n == 0):
                pe.wait_ge(A.norm_done, n * 2 + (half - 1))
            pe.wait_ge(A.exp_done, n * N_PIECES + (g + 1))
            nc.tensor.matmul(PS[:, O_BANK[half], off:HALF], A.bufs[4][b][:, j, :], Pt[g % 4][:, 0:HALF - off],
                             start=(j == 0), stop=(g in LAST_OF_HALF)).then_inc(A.pv_done, 1)

        def vtrans_pe(pe, A, n, src):
            pe.wait_ge(A.vT_done, n + 1)
            pe.wait_ge(A.max_done, n * N_MAX + 7)
            for j in range(DT):
                last = nc.tensor.matmul(PS[:, V_BANK, j * HD:(j + 1) * HD], src[0:HD, j * P:(j + 1) * P], ident[0:HD, 0:HD],
                                        start=True, stop=True)
            last.then_inc(A.vt_ready, 1)

        def max_pe(pe, A, n, b, i):
            q_hi, _, k_hi, _, _ = A.bufs
            r = slice(0, A.rows_max)
            bank, reduced = MAX_BANK[i]
            if reduced:
                pe.wait_ge(A.max_done, n * N_MAX + reduced)
            queries = q_hi[b][r, i * P:(i + 1) * P]
            if i >= 4:
                nc.tensor.matmul(PS[:, bank, :], queries, k_hi[b][r, 0:HALF], start=True, stop=True)
            w, c, d = max_width(i)[0], i // 4, i % 4 * P
            nc.tensor.matmul(PS[:, bank + c, 0:w], queries, k_hi[b][r, c * HALF:c * HALF + w], start=True, stop=False)
            nc.tensor.matmul(PS[:, bank + c, d:w], ident_bf[:, :], masks[:, A.mask, 0:w - d], start=False, stop=True)\
                .then_inc(A.mp_ready, 1)

        def max_row_pe(pe, A, n):
            pe.wait_ge(A.mx_done, n + 1)
            nc.tensor.transpose(PS[0:DT, M_BANK, 0:P], mx[:, 0:DT], ident[:, :]).then_inc(A.mT_ready, 1)

        def exp_act(act, A, n, g):
            half, j, off, d = PIECES[g]
            act.wait_ge(A.s_ready, n * N_PIECES + (g + 1))
            act.wait_ge(A.pv_done, n * N_PIECES + (g + 1))
            nc.scalar.activation(Pt[g % 4][:, 0:HALF - off], PS[:, S_BANK[g % 2], 0:HALF - off], ACT.Exp).then_inc(A.exp_done, 1)

        def rough_act(act, A, n, half):
            act.wait_ge(A.pv_done, n * N_PIECES + (LAST_OF_HALF[half] + 1 + 4))
            if half == 1 or not (isinstance(n, int) and n == 0):
                act.wait_ge(A.norm_done, n * 2 + half)
            nc.scalar.activation(ln_sum[0:HD, :], PS[HD:P, O_BANK[half], :], ACT.Ln).then_inc(A.ln_done, 1)
            act.wait_ge(A.ln_done, n * 2 + (half + 1))
            nc.scalar.activation(r0[0:HD, :], ln_sum[0:HD, :], ACT.Exp, scale=-1.0).then_inc(A.r0_done, 1)

        def norm_half_dve(dve, A, n, b, half, tile, gate):
            dve.wait_ge(A.r0_done, n * 2 + (half + 1))
            steps = 3 if gate else 2
            seq = n * (2 * steps) + half * steps
            rows = slice(HD * b, HD * b + HD)
            if half == 1 or not (isinstance(n, int) and n == 0):
                dve.wait_ge(A.newton, seq)
                dve.wait_ge(A.norm_done, n * 2 + half)
            nc.vector.tensor_tensor(newton[0:HD, :], PS[HD:P, O_BANK[half], :], r0[0:HD, :], ALU.mult).then_inc(A.newton, 1)
            dve.wait_ge(A.newton, seq + 1)
            nc.vector.scalar_tensor_tensor(rec[rows, :], newton[0:HD, :], -2.0, r0[0:HD, :], ALU.add, ALU.mult).then_inc(A.newton, 1)
            dve.wait_ge(A.newton, seq + 2)
            dst = flat(mix[rows, bass.ds(tile, 1), half * HALF:(half + 1) * HALF])
            if gate:
                nc.vector.tensor_tensor(rec[rows, :], rec[rows, :], dst, ALU.mult).then_inc(A.newton, 1)
                dve.wait_ge(A.newton, seq + 3)
            nc.vector.scalar_tensor_tensor(dst, PS[0:HD, O_BANK[half], :], -1.0, rec[rows, :], ALU.mult, ALU.mult).then_inc(A.norm_done, 1)

        def max_dve(dve, A, n, i):
            dve.wait_ge(A.mp_ready, n * N_MAX + (i + 1))
            bank = MAX_BANK[i][0]
            nc.vector.reduce_max(mx[:, i:i + 1], flat(PS[:, bank:bank + 2, :])[:, 0:max_width(i)[1]] if i >= 4 else
                                 PS[:, bank, 0:max_width(i)[1]], AX_X).then_inc(A.max_done, 1)

        def negate_dve(dve, A, n):
            dve.wait_ge(A.max_done, (n + 1) * N_MAX)
            nc.vector.tensor_scalar(mx[:, 0:8], mx[:, 0:8], -1.0, None, ALU.mult).then_inc(A.mx_done, 1)

        def vaug_dve(dve, A, n, b):
            dve.wait_ge(A.vt_ready, n + 1)
            nc.vector.tensor_copy(A.bufs[4][b][:, :, 0:HD], PS[:, V_BANK, :].rearrange("p (j e) -> p j e", e=HD)).then_inc(A.vaug_done, 1)

        def max_row_dve(dve, A, n):
            dve.wait_ge(A.mT_ready, n + 1)
            nc.vector.tensor_copy(c_neg[:, :], PS[0:DT, M_BANK, 0:P]).then_inc(A.cneg_done, 1)

        def max_row_act(act, A, n, b, turn):
            act.wait_ge(A.cneg_done, n + 1)
            act.dma_start(A.bufs[0][b][A.rows - 1:A.rows, :].bitcast(F32), c_neg[:, :].bitcast(F32)).then_inc(A.row_in[b], 16)

        fox = Attention("fox", FOX_H, HD + 1, HD + 2, 0)
        fox.bufs = buffers("fox", R_X, R_X + 24576, R_S + 8192)
        fox.f_in = [sem(f"fox_f_in{b}") for b in range(2)]
        fox_vT = at("fox_vT", R_S + 16384, [HD, T])
        mla = Attention("mla", MLA_H, NOPE + ROPE, NOPE + ROPE + 1, 2)
        mla.bufs = buffers("mla", R_H + 40960, R_S + 8192, R_S + 16384)
        mla_vT = at("mla_vT", R_W + 16384, [HD, T])

        def attend_pe(pe, A, n, b, after=()):
            for g in range(N_PIECES):
                value_pe(pe, A, n, b, g)
                if g + 2 < N_PIECES:
                    score_pe(pe, A, n, b, g + 2)
                if after:
                    after(g)

        def step_pe(pe, A, n, b, turn, project_head, vT):
            prev = None if isinstance(n, int) and n == 0 else n - 1

            def first_scores():
                if prev is not None:
                    pe.wait_ge(A.row_in[1 - b], 16 * turn if b == 0 else turn * 16 + 16)
                    score_pe(pe, A, prev, 1 - b, 0)
                    score_pe(pe, A, prev, 1 - b, 1)

            def maxima(g):
                if g == min(MAX_AFTER):
                    pe.wait_ge(A.lo_done, (n + 1) * A.n_lo)
                    pe.wait_ge(A.vT_done, n + 1)
                    if A is fox:
                        pe.wait_ge(A.f_in[b], turn * 32 + 32)
                for i in MAX_AFTER.get(g, ()):
                    max_pe(pe, A, n, b, i)
                if g == N_PIECES - 2:
                    vtrans_pe(pe, A, n, vT)
                if g == N_PIECES - 1:
                    max_row_pe(pe, A, n)

            project_head(pe, n, b, first_scores)
            if prev is not None:
                attend_pe(pe, A, prev, 1 - b, maxima)
            else:
                for g in range(N_PIECES):
                    maxima(g)

        def last_pe(pe, A):
            pe.wait_ge(A.row_in[1], 16 * (A.heads // 2))
            for g in range(2):
                score_pe(pe, A, A.heads - 1, 1, g)
            attend_pe(pe, A, A.heads - 1, 1)

        def step_act(act, A, n, b, turn, prepare):
            prev = None if isinstance(n, int) and n == 0 else n - 1
            todo = prepare(act, n, b, turn)
            for g in range(N_PIECES):
                if prev is not None:
                    exp_act(act, A, prev, g)
                if g in todo:
                    todo[g]()
                if g == 6 and prev is not None:
                    rough_act(act, A, prev, 0)
            if prev is not None:
                rough_act(act, A, prev, 1)
            max_row_act(act, A, n, b, turn)

        def last_act(act, A):
            for g in range(N_PIECES):
                exp_act(act, A, A.heads - 1, g)
                if g == 6:
                    rough_act(act, A, A.heads - 1, 0)
            rough_act(act, A, A.heads - 1, 1)

        def step_dve(dve, A, n, b, turn, prepare, tile0, gate):
            prev = None if isinstance(n, int) and n == 0 else n - 1
            prepare(dve, n, b)
            tile = turn + (tile0 - (b == 0))
            for i in range(N_MAX):
                max_dve(dve, A, n, i)
                if i == 3 and prev is not None:
                    norm_half_dve(dve, A, prev, 1 - b, 0, tile, gate)
            negate_dve(dve, A, n)
            vaug_dve(dve, A, n, b)
            max_row_dve(dve, A, n)
            if prev is not None:
                norm_half_dve(dve, A, prev, 1 - b, 1, tile, gate)

        def steps(eng, A, step):
            for b in range(2):
                step(b, b, 0)
            with eng.Fori(1, A.heads // 2) as turn:
                for b in range(2):
                    step(turn * 2 + b, b, turn)

        small_read, f_stored = sem("small_read"), sem("f_stored")
        f_y, f_log, f_sum = sem("f_y"), sem("f_log"), sem("f_sum")
        fv_read = sem("fv_read")
        restA, restB = sem("rest_read_act"), sem("rest_read_dve")
        a_low = at("a_low", R_S + 4096, [16, T])
        FR = slice(32, 32 + FOX_H)
        f_t = [at(f"f_t{i}", R_X + 4096 * i, [P, T]) for i in range(4)]
        f_hi = at("f_hi", R_X + 16384, [P, T], F32R)
        f_lo = at("f_lo", R_X + 20480, [P, T], F32R)
        f_one = at("f_one", R_X + 24576, [P, T])
        z8 = at("z8", R_X, [P, 8, T])
        zg = at("zg", R_S + 8192, [P, 2, T])
        bcum = at("bcum", R_H, [P, 2, T])
        q_in = at("q_in", R_H + 8192, [P, 2, T])
        k_in = at("k_in", R_H + 16384, [P, 2, T])
        gt = [at(f"gla_t{i}", R_H + 24576 + 8192 * i, [P, 2, T]) for i in range(5)]
        kd_tok = at("kd_tok", R_H + 24576, [P, DT, 2, P])
        attm = at("attm", R_H + 32768, [P, 4, DT, P])
        S_all = at("S_all", R_H + 49152, [P, 2, NCH, P])
        v_tok = at("v_tok", R_S + 16384, [P, DT, 2, P])
        gla_o = at("gla_o", R_H, [P, 2, T])
        gla_sq = at("gla_sq", R_H + 8192, [P, 2, T])
        gla_ln = at("gla_ln", R_H + 16384, [P, 2, T])
        gla_y = at("gla_y", R_H + 24576, [P, 2, T])
        gla_n = at("gla_n", R_H + 32768, [P, 2, T])
        dec = at("dec", R_S + 24576, [P, 2 * NCH])
        s2 = at("pool_s2", R_W, [P, 2, T])
        s4 = at("pool_s4", R_W + 8192, [P, 2, T])
        s8 = at("pool_s8", R_W + 16384, [P, T])
        pool_step, pool_d, pool_mm = sem("pool_step"), sem("pool_d"), sem("pool_mm")
        pool_out = sem("pool_out")
        g_vt, g_vtok, g_gate, g_act, g_dve = sem("g_vt"), sem("g_vtok"), sem("g_gate"), sem("g_act"), sem("g_dve")
        g_kt, g_ktok, g_att, g_attm, g_kv, g_S = sem("g_kt"), sem("g_ktok"), sem("g_att"), sem("g_attm"), sem("g_kv"), sem("g_S")
        g_mm, g_o1, g_o, g_ms = sem("g_mm"), sem("g_o1"), sem("g_o"), sem("g_ms")
        g_zero = sem("g_zero")
        m_hi, m_lo = sem("mix_hi"), sem("mix_lo")
        wo_added = sem("wo_added")

        def psflat(a, n):
            return flat(PS[:, a:a + n, :])

        def small_dve(dve):
            dve.wait_ge(unit_done, U_SMALL + 3)
            nc.vector.tensor_copy(a_low[:, :], flat(pjA)[0:16, :]).then_inc(small_read, 1)
            bf = vec[FR, V_BF:V_BF + 1]
            nc.vector.tensor_scalar(f_t[0][FR, :], flat(pjA)[FR, :], bf, 0.0, ALU.add, ALU.min).then_inc(f_y, 1)
            nc.vector.memset(f_one[FR, :], 1.0).then_inc(f_y, 1)
            dve.wait_ge(f_log, 3)
            dve.wait_ge(f_y, 2)
            nc.vector.tensor_tensor(f_t[0][FR, :], f_t[2][FR, :], f_t[0][FR, :], ALU.subtract).then_inc(f_sum, 1)
            dve.wait_ge(f_sum, 1)
            nc.vector.tensor_tensor_scan(f_t[1][FR, :], f_one[FR, :], f_t[0][FR, :], 0.0, ALU.mult, ALU.add).then_inc(f_sum, 1)
            dve.wait_ge(f_sum, 2)
            nc.vector.tensor_copy(f_hi[FR, :], f_t[1][FR, :]).then_inc(f_sum, 1)
            dve.wait_ge(f_sum, 3)
            nc.vector.tensor_tensor(f_lo[FR, :], f_t[1][FR, :], f_hi[FR, :].bitcast(F32), ALU.subtract).then_inc(f_sum, 1)

        def small_act(act):
            act.wait_ge(unit_done, U_SMALL + 3)
            bf = vec[FR, V_BF:V_BF + 1]
            act.wait_ge(f_y, 1)
            nc.scalar.activation(f_t[1][FR, :], flat(pjA)[FR, :], ACT.Abs, bias=bf).then_inc(f_log, 1)
            act.wait_ge(f_log, 1)
            nc.scalar.activation(f_t[2][FR, :], f_t[1][FR, :], ACT.Exp, scale=-1.0).then_inc(f_log, 1)
            act.wait_ge(f_log, 2)
            nc.scalar.activation(f_t[2][FR, :], f_t[2][FR, :], ACT.Ln, bias=one[FR, :]).then_inc(f_log, 1)
            act.wait_ge(f_sum, 4)
            act.dma_start(f_rows[0, :, :], f_hi[FR, :].bitcast(F32)).then_inc(f_stored, 16)
            act.dma_start(f_rows[1, :, :], f_lo[FR, :].bitcast(F32)).then_inc(f_stored, 16)

        one = small_const[:, K_EPS - K_CNT + 1:K_EPS - K_CNT + 2]

        def fox_values_pe(pe):
            pe.wait_ge(f_y, 1)
            pe.wait_ge(f_log, 1)
            units_pe(pe, U_FV, 4, range(DT), h_hi, h_lo, lambda it, j: pe.wait_ge(fv_read, it * 2 + (j + 1)))

        def fox_values_act(act):
            with act.Fori(0, 2) as it:
                for j, src in enumerate((pjA, pjB)):
                    act.wait_ge(unit_done, it * 2 + (U_FV + j + 3))
                    nc.scalar.activation(flat(mix[:, bass.ds(it * 2 + j, 1), :]), flat(src), ACT.Copy).then_inc(fv_read, 1)

        def fox_project(pe, n, b, first_scores):
            pe.wait_ge(w_split, n + (U_FQK + 3))
            project(pe, (U_FQK + b) % 2, range(DT), h_hi, h_lo, pjA, done=False, halves=(0,))
            first_scores()
            project(pe, (U_FQK + b) % 2, range(DT), h_hi, h_lo, pjA, halves=(1,))

        def fox_prepare_act(act, n, b, turn):
            q_hi, q_lo, k_hi, k_lo, vaug = fox.bufs
            src = flat(pjA)
            if isinstance(n, int) and n == 0:
                act.wait_ge(fox.setup, 1)
                act.wait_ge(f_stored, 32)
            else:
                act.wait_ge(fox.vt_ready, n)
            for part, row in ((0, k_hi[b]), (1, k_lo[b])):
                act.dma_start(row[HD:HD + 1, :].bitcast(F32), f_rows[part, bass.ds(n, 1), :]).then_inc(fox.f_in[b], 16)

            def split():
                act.wait_ge(unit_done, n + (U_FQK + 3))
                nc.scalar.activation(q_hi[b][0:HD, :], src[0:HD, :], ACT.Copy, scale=HD ** -0.5).then_inc(fox.hi_done, 1)
                nc.scalar.activation(k_hi[b][0:HD, :], src[HD:P, :], ACT.Copy).then_inc(fox.hi_done, 1)

            def values():
                nc.scalar.activation(fox_vT[:, :], flat(mix[HD * b:HD * b + HD, bass.ds(turn, 1), :]), ACT.Copy).then_inc(fox.vT_done, 1)
            return {1: split, 2: values}

        def fox_prepare_dve(dve, n, b):
            q_hi, q_lo, k_hi, k_lo, vaug = fox.bufs
            src = flat(pjA)
            dve.wait_ge(fox.hi_done, n * 2 + 1)
            nc.vector.scalar_tensor_tensor(q_lo[b][0:HD, :], src[0:HD, :], HD ** -0.5, q_hi[b][0:HD, :].bitcast(F32),
                                           ALU.mult, ALU.subtract).then_inc(fox.lo_done, 1)
            dve.wait_ge(fox.hi_done, n * 2 + 2)
            nc.vector.tensor_tensor(k_lo[b][0:HD, :], src[HD:P, :], k_hi[b][0:HD, :].bitcast(F32), ALU.subtract)\
                .then_inc(fox.lo_done, 1)

        def fox_setup_dve(dve):
            dve.wait_ge(f_stored, 32)
            q_hi, q_lo, k_hi, k_lo, vaug = fox.bufs
            for b in range(2):
                nc.vector.memset(q_hi[b][HD:HD + 2, :].bitcast(F32), 1.0)
                nc.vector.memset(q_lo[b][HD:HD + 2, :].bitcast(F32), 0.0)
                nc.vector.memset(k_hi[b][HD:HD + 2, :].bitcast(F32), 1.0)
                nc.vector.memset(k_lo[b][HD:HD + 2, :].bitcast(F32), 0.0)
                last = nc.vector.memset(vaug[b][:, :, HD:P], 1.0)
            last.then_inc(fox.setup, 1)

        fox.n_lo = 2

        def rest_pe(pe):
            units_pe(pe, U_REST, N_REST, range(DT), h_hi, h_lo,
                     lambda it, j: pe.wait_ge((restA, restB)[j], it + 1))

        def rest_act(act):
            with act.Fori(0, 4) as it:
                act.wait_ge(unit_done, it * 2 + (U_REST + 3))
                nc.scalar.activation(flat(z8[:, bass.ds(it * 2, 1), :]), flat(pjA), ACT.Copy).then_inc(restA, 1)
            act.wait_ge(unit_done, U_REST + 8 + 3)
            nc.scalar.activation(zg[:, 0, :], flat(pjA), ACT.Copy).then_inc(restA, 1)

        def rest_dve(dve):
            with dve.Fori(0, 4) as it:
                dve.wait_ge(unit_done, it * 2 + (U_REST + 4))
                nc.vector.tensor_copy(flat(z8[:, bass.ds(it * 2 + 1, 1), :]), flat(pjB)).then_inc(restB, 1)
            dve.wait_ge(unit_done, U_REST + 9 + 3)
            nc.vector.tensor_copy(zg[:, 1, :], flat(pjB)).then_inc(restB, 1)

        def pool_dve(dve):
            dve.wait_ge(restA, N_REST // 2 + 1)
            dve.wait_ge(restB, N_REST // 2 + 1)
            count = [0]

            def shifted(dst, src, w):
                nc.vector.tensor_copy(dst[:, :, 0:w], src[:, :, 0:w])
                nc.vector.tensor_tensor(dst[:, :, w:T], src[:, :, w:T], src[:, :, 0:T - w], ALU.add).then_inc(pool_step, 1)
                count[0] += 1
                dve.wait_ge(pool_step, count[0])
            u = z8[:, 0:2, :]
            shifted(s2, u, 1)
            shifted(s4, s2, 2)
            s8_ = s8[:, :].rearrange("p (a n) -> p a n", a=1)
            shifted(s8_, s4[:, 1:2, :], 4)
            shifted(s2[:, 1:2, :], s8_, 8)
            cnt = small_const[:, 0:32].rearrange("p (c n) -> p c n", c=2)
            for c, r, src, w in ((0, 0, s2[:, 0, :], 2), (0, HD, s4[:, 0, :], 4), (1, 0, s8[:, :], 8), (1, HD, s2[:, 1, :], 16)):
                rows = slice(r, r + HD)
                nc.vector.tensor_tensor(src[rows, 0:16], src[rows, 0:16], cnt[rows, c, :], ALU.mult).then_inc(pool_step, 1)
                count[0] += 1
                nc.vector.scalar_tensor_tensor(z8[rows, c, 16:T], src[rows, 16:T], 1.0 / w, z8[rows, c, 16:T],
                                               ALU.mult, ALU.subtract)
                dve.wait_ge(pool_step, count[0])
                last = nc.vector.tensor_tensor(z8[rows, c, 0:16], src[rows, 0:16], z8[rows, c, 0:16], ALU.subtract)
            last.then_inc(pool_d, 1)

        def pool_pe(pe):
            pe.wait_ge(pool_d, 1)
            pe.wait_ge(g_act, 2)
            pe.wait_ge(g_dve, 2)
            for c, dst in enumerate((pjA, pjB)):
                for half in range(2):
                    last = nc.tensor.matmul(dst[:, half, :], vec[:, V_WPOOL + P * c:V_WPOOL + P * c + P],
                                            z8[:, c, half * HALF:(half + 1) * HALF], start=True, stop=True)
            last.then_inc(pool_mm, 1)

        def pool_act(act):
            act.wait_ge(pool_mm, 1)
            for c, src in enumerate((pjA, pjB)):
                nc.scalar.activation(mix[:, c, :], flat(src), ACT.Copy, scale=vec[:, V_PS + c:V_PS + c + 1]).then_inc(pool_out, 1)

        def by_chunk(ap):
            return ap.rearrange("p c (n t) -> p (c n) t", t=CHUNK)

        def chunk_col(col):
            return by_chunk(bcum[:, :, :])[:, :, col:col + 1].to_broadcast([P, 2 * NCH, CHUNK])

        def kv_place(c, n):
            return (4 if c == 0 else 0) + n % 2 * 2 + n // 8, n // 2 % 4 * P

        def tau(t):
            return flat(t[:, :, :])

        def gla_pe(pe):
            pe.wait_ge(restA, N_REST // 2 + 1)
            pe.wait_ge(restB, N_REST // 2 + 1)
            for blk in range(DT):
                for c in range(2):
                    last = nc.tensor.transpose(PS[:, 4 + blk // 2, (blk % 2 * 2 + c) * P:(blk % 2 * 2 + c + 1) * P],
                                               z8[:, 6 + c, blk * P:(blk + 1) * P], ident[:, :])
            last.then_inc(g_vt, 1)
            for c, dst in enumerate((pjA, pjB)):
                for half in range(2):
                    last = nc.tensor.matmul(dst[:, half, :], vec[0:16, V_WAUP + P * c:V_WAUP + P * c + P],
                                            a_low[:, half * HALF:(half + 1) * HALF], start=True, stop=True)
            last.then_inc(g_gate, 1)
            pool_pe(pe)
            pe.wait_ge(pool_out, 2)
            pe.wait_ge(g_dve, 8)
            for batch in range(2):
                if batch:
                    pe.wait_ge(g_attm, 1)
                for hh in range(2):
                    hd = batch * 2 + hh
                    rows = slice(HD * hh, HD * hh + HD)
                    for pr in range(DT):
                        s = slice(pr * P, (pr + 1) * P)
                        last = nc.tensor.matmul(PS[:, hh * 2 + pr // 4, pr % 4 * P:(pr % 4 + 1) * P], k_in[rows, batch, s],
                                                q_in[rows, batch, s], start=True, stop=True)
                last.then_inc(g_att, 1)
                if batch == 0:
                    pe.wait_ge(g_dve, 10)
                    pe.wait_ge(g_vtok, 1)
                    for blk in range(DT):
                        for c in range(2):
                            last = nc.tensor.transpose(PS[:, 4 + blk // 2, (blk % 2 * 2 + c) * P:(blk % 2 * 2 + c + 1) * P],
                                                       z8[:, 4 + c, blk * P:(blk + 1) * P], ident[:, :])
                    last.then_inc(g_kt, 1)
            pe.wait_ge(g_ktok, 1)
            for c in range(2):
                if c:
                    pe.wait_ge(g_attm, 2)
                for n in range(NCH - 1):
                    rows = slice(n % 2 * CHUNK, n % 2 * CHUNK + CHUNK)
                    bank, col = kv_place(c, n)
                    last = nc.tensor.matmul(PS[:, bank, col:col + P], kd_tok[rows, n // 2, c, :],
                                            v_tok[rows, n // 2, c, :], start=True, stop=True)
                last.then_inc(g_kv, 1)
            pe.wait_ge(g_S, 4 * (NCH - 1))
            for c, dst in enumerate((pjA, pjB)):
                for n in range(NCH):
                    last = nc.tensor.matmul(dst[:, n // 8, n % 8 * CHUNK:(n % 8 + 1) * CHUNK], S_all[:, c, n, :],
                                            z8[:, 2 + c, n * CHUNK:(n + 1) * CHUNK], start=True, stop=True)
            for hd in range(4):
                rows = slice(HD * (hd % 2), HD * (hd % 2) + HD)
                for pr in range(DT):
                    last = nc.tensor.matmul(PS[rows, 4 + hd // 2 * 2 + pr // 4, pr % 4 * P:(pr % 4 + 1) * P],
                                            v_tok[:, pr, hd // 2, HD * (hd % 2):HD * (hd % 2) + HD], attm[:, hd, pr, :],
                                            start=True, stop=True)
            last.then_inc(g_mm, 1)
            pe.wait_ge(g_act, 11)
            pe.wait_ge(g_o1, 1)
            for c in range(2):
                for half in range(2):
                    last = nc.tensor.matmul(PS[:, 2 * c + half, :], head_mean[:, :], gla_sq[:, c, half * HALF:(half + 1) * HALF],
                                            start=True, stop=True)
            last.then_inc(g_ms, 1)

        def gla_act(act):
            act.wait_ge(g_vt, 1)
            nc.scalar.activation(v_tok[:, :, :, :].rearrange("p a c n -> p (a c n)"), psflat(4, 4), ACT.Copy).then_inc(g_vtok, 1)
            act.wait_ge(g_gate, 1)
            for c, src in enumerate((pjA, pjB)):
                act.wait_ge(g_dve, c + 1)
                nc.scalar.activation(gt[1][:, c, :], flat(src), ACT.Abs, bias=vec[:, V_BA + c:V_BA + c + 1]).then_inc(g_act, 1)
            act.wait_ge(g_act, 2)
            nc.scalar.activation(tau(gt[2]), tau(gt[1]), ACT.Exp, scale=-1.0).then_inc(g_act, 1)
            act.wait_ge(g_act, 3)
            nc.scalar.activation(tau(gt[1]), tau(gt[2]), ACT.Ln, bias=one).then_inc(g_act, 1)
            pool_act(act)
            act.wait_ge(g_dve, 5)
            nc.scalar.activation(tau(gt[1]), tau(gt[0]), ACT.Exp, scale=1.0 / GLA_TAU).then_inc(g_act, 1)
            nc.scalar.activation(tau(gt[2]), tau(gt[0]), ACT.Exp, scale=-1.0 / GLA_TAU).then_inc(g_act, 1)
            nc.scalar.activation(tau(gt[3]), tau(bcum), ACT.Exp, scale=1.0 / GLA_TAU).then_inc(g_act, 1)
            act.wait_ge(g_dve, 6)
            nc.scalar.activation(tau(gt[4]), tau(gt[0]), ACT.Exp, scale=1.0 / GLA_TAU).then_inc(g_act, 1)
            nc.scalar.activation(dec[:, :], by_chunk(bcum[:, :, :])[:, :, CHUNK - 1], ACT.Exp, scale=1.0 / GLA_TAU).then_inc(g_act, 1)
            act.wait_ge(g_kt, 1)
            nc.scalar.activation(kd_tok[:, :, :, :].rearrange("p a c n -> p (a c n)"), psflat(4, 4), ACT.Copy).then_inc(g_ktok, 1)
            act.wait_ge(g_mm, 1)
            nc.scalar.activation(tau(gla_o), psflat(0, 4), ACT.Copy).then_inc(g_o1, 1)
            nc.scalar.activation(tau(zg), tau(zg), ACT.Silu).then_inc(g_act, 1)
            act.wait_ge(g_o, 1)
            nc.scalar.activation(tau(gla_sq), tau(gla_o), ACT.Square).then_inc(g_act, 1)
            act.wait_ge(g_ms, 1)
            nc.scalar.activation(tau(gla_ln), psflat(0, 4), ACT.Ln, bias=eps).then_inc(g_act, 1)
            act.wait_ge(g_act, 12)
            nc.scalar.activation(tau(gla_y), tau(gla_ln), ACT.Exp, scale=-0.5).then_inc(g_act, 1)

        def gla_dve(dve):
            dve.wait_ge(g_gate, 1)
            for c, src in enumerate((pjA, pjB)):
                nc.vector.tensor_scalar(gt[0][:, c, :], flat(src), vec[:, V_BA + c:V_BA + c + 1], 0.0, ALU.add, ALU.min).then_inc(g_dve, 1)
            nc.vector.memset(tau(gt[4]), 1.0).then_inc(g_zero, 1)
            dve.wait_ge(g_zero, 1)
            nc.vector.memset(by_chunk(gt[4][:, :, :])[:, :, 0:1], 0.0).then_inc(g_zero, 1)
            dve.wait_ge(g_act, 4)
            dve.wait_ge(g_dve, 2)
            nc.vector.tensor_tensor(tau(gt[3]), tau(gt[0]), tau(gt[1]), ALU.subtract).then_inc(g_dve, 1)
            dve.wait_ge(g_dve, 3)
            dve.wait_ge(g_zero, 2)
            nc.vector.tensor_tensor_scan(tau(bcum), tau(gt[4]), tau(gt[3]), 0.0, ALU.mult, ALU.add).then_inc(g_dve, 1)
            dve.wait_ge(g_dve, 4)
            nc.vector.tensor_tensor(by_chunk(gt[0][:, :, :]), by_chunk(bcum[:, :, :]), chunk_col(CHUNK // 2 - 1), ALU.subtract).then_inc(g_dve, 1)
            dve.wait_ge(g_act, 6)
            nc.vector.tensor_tensor(by_chunk(gt[0][:, :, :]), chunk_col(CHUNK - 1), by_chunk(bcum[:, :, :]), ALU.subtract).then_inc(g_dve, 1)
            gq, gk = flat(z8[:, 2:4, :]), flat(z8[:, 4:6, :])
            nc.vector.scalar_tensor_tensor(tau(q_in), gq, HD ** -0.5, tau(gt[1]), ALU.mult, ALU.mult).then_inc(g_dve, 1)
            nc.vector.tensor_tensor(tau(k_in), gk, tau(gt[2]), ALU.mult).then_inc(g_dve, 1)
            dve.wait_ge(g_act, 7)
            dve.wait_ge(g_dve, 8)
            nc.vector.scalar_tensor_tensor(gq, gq, HD ** -0.5, tau(gt[3]), ALU.mult, ALU.mult).then_inc(g_dve, 1)
            dve.wait_ge(g_act, 8)
            nc.vector.tensor_tensor(gk, gk, tau(gt[4]), ALU.mult).then_inc(g_dve, 1)
            dve.wait_ge(g_dve, 10)
            nc.vector.memset(attm[:, :, :, :].rearrange("p h a n -> p (h a n)"), 0.0).then_inc(g_zero, 1)
            nc.vector.memset(S_all[:, :, :, :].rearrange("p c a n -> p (c a n)"), 0.0).then_inc(g_zero, 1)
            dve.wait_ge(g_zero, 4)
            m = att_mask[:, :].rearrange("p (o n) -> p o n", o=1).to_broadcast([P, 4, P])
            for batch in range(2):
                dve.wait_ge(g_att, batch + 1)
                for bank in range(4):
                    hd, a = batch * 2 + bank // 2, bank % 2 * 4
                    last = nc.vector.copy_predicated(attm[:, hd, a:a + 4, :], m, PS[:, bank, :].rearrange("p (a n) -> p a n", n=P))
                last.then_inc(g_attm, 1)
            dve.wait_ge(g_act, 9)
            dve.wait_ge(g_kv, 2)
            done = 0
            for n in range(NCH - 1):
                for c in range(2):
                    for a in range(2):
                        r = slice(HD * a, HD * a + HD)
                        bank, col = kv_place(c, n)
                        kv = PS[r, bank, col + HD * a:col + HD * a + HD]
                        if n:
                            dve.wait_ge(g_S, done - 3)
                        nc.vector.scalar_tensor_tensor(S_all[r, c, n + 1, r], S_all[r, c, n, r], dec[r, c * NCH + n:c * NCH + n + 1],
                                                       kv, ALU.mult, ALU.add).then_inc(g_S, 1)
                        done += 1
            dve.wait_ge(g_o1, 1)
            nc.vector.tensor_tensor(tau(gla_o), psflat(4, 4), tau(gla_o), ALU.add).then_inc(g_o, 1)
            dve.wait_ge(g_act, 13)
            nc.vector.tensor_tensor(tau(gla_n), tau(gla_y), tau(gla_y), ALU.mult).then_inc(g_o, 1)
            dve.wait_ge(g_o, 2)
            nc.vector.scalar_tensor_tensor(tau(gla_n), psflat(0, 4), EPS, tau(gla_n), ALU.add, ALU.mult).then_inc(g_o, 1)
            dve.wait_ge(g_o, 3)
            nc.vector.tensor_scalar(tau(gla_n), tau(gla_n), -0.5, 1.5, ALU.mult, ALU.add).then_inc(g_o, 1)
            dve.wait_ge(g_o, 4)
            nc.vector.tensor_tensor(tau(gla_y), tau(gla_y), tau(gla_n), ALU.mult).then_inc(g_o, 1)
            dve.wait_ge(g_o, 5)
            for c in range(2):
                nc.vector.scalar_tensor_tensor(gla_o[:, c, :], gla_o[:, c, :], vec[:, V_GN + c:V_GN + c + 1], gla_y[:, c, :],
                                               ALU.mult, ALU.mult).then_inc(g_o, 1)
            dve.wait_ge(g_o, 7)
            nc.vector.tensor_tensor(flat(mix[:, 2:4, :]), tau(gla_o), tau(zg), ALU.mult).then_inc(g_o, 1)

        def mix_split_act(act, hi_done):
            for k in range(DT):
                nc.scalar.activation(hi_tile(k), mix[:, k, :], ACT.Copy).then_inc(hi_done, 1)

        def mix_split_dve(dve, hi_done, lo_done):
            for k in range(DT):
                dve.wait_ge(hi_done, k + 1)
                nc.vector.tensor_tensor(lo_tile(k), mix[:, k, :], hi_tile(k).bitcast(F32), ALU.subtract).then_inc(lo_done, 1)

        gate_read, up_read, a_split_hi = sem("gate_read"), sem("up_read"), sem("a_split_hi")
        a_split_lo, dn_added = sem("a_split_lo"), sem("dn_added")
        a_hi = at("a_hi", R_M + 8192, [P, 6, T], F32R)
        a_lo = at("a_lo", R_M - 16384, [P, 6, T], F32R)
        F0 = [sum(MLP_CHUNKS[:c]) for c in range(len(MLP_CHUNKS))]

        def mlp_pe(pe):
            for c, fc in enumerate(MLP_CHUNKS):
                if c:
                    pe.wait_ge(dn_added, DT * c + 2)
                with pe.Fori(0, fc) as f:
                    for j, (dst, free) in enumerate(((pjA, gate_read), (pjB, up_read))):
                        pe.wait_ge(w_split, f * 2 + (U_GU[c] + j + 3))
                        pe.wait_ge(free, f + (F0[c] + 1))
                        project(pe, (U_GU[c] + j) % 2, range(DT), h_hi, h_lo, dst)
                pe.wait_ge(a_split_lo, F0[c] + fc + 1)
                units_pe(pe, U_DN[c], DT, range(fc), a_hi, a_lo,
                         lambda it, j, c=c: pe.wait_ge(dn_added, it * 2 + (DT * c + j + 1)))

        def mlp_act(act):
            for c, fc in enumerate(MLP_CHUNKS):
                with act.Fori(0, fc) as f:
                    act.wait_ge(unit_done, f * 2 + (U_GU[c] + 3))
                    act.wait_ge(up_read, f + (F0[c] + 1))
                    nc.scalar.activation(tmp[0][:, :], flat(pjA), ACT.Silu).then_inc(gate_read, 1)
                    act.wait_ge(up_read, f + (F0[c] + 2))
                    nc.scalar.activation(flat(a_hi[:, bass.ds(f, 1), :]), tmp[1][:, :], ACT.Copy).then_inc(a_split_hi, 1)
                if c == len(MLP_CHUNKS) - 1:
                    residual_squares(act, dn_added, DT * c, NF)

        def mlp_dve(dve):
            for c, fc in enumerate(MLP_CHUNKS):
                with dve.Fori(0, fc) as f:
                    dve.wait_ge(unit_done, f * 2 + (U_GU[c] + 4))
                    dve.wait_ge(gate_read, f + (F0[c] + 2))
                    dve.wait_ge(a_split_lo, f + (F0[c] + 1))
                    nc.vector.tensor_tensor(tmp[1][:, :], flat(pjB), tmp[0][:, :], ALU.mult).then_inc(up_read, 1)
                    dve.wait_ge(a_split_hi, f + (F0[c] + 1))
                    nc.vector.tensor_tensor(flat(a_lo[:, bass.ds(f, 1), :]), tmp[1][:, :],
                                            flat(a_hi[:, bass.ds(f, 1), :]).bitcast(F32), ALU.subtract).then_inc(a_split_lo, 1)
                last = c == len(MLP_CHUNKS) - 1
                residual_dve(dve, U_DN[c], dn_added, DT * c, NF if last else None)

        u5 = at("u5", R_S + 8192, [P, 5, T])
        k_rope = at("k_rope", R_S + 4096, [P, T])
        cq_hi, cq_lo = at("cq_hi", R_H, [P, 3, T], F32R), at("cq_lo", R_H + 12288, [P, 3, T], F32R)
        ckv_hi, ckv_lo = at("ckv_hi", R_H + 24576, [P, 2, T], F32R), at("ckv_lo", R_H + 32768, [P, 2, T], F32R)
        min_read, kr_step, z_read = sem("min_read"), sem("kr_step"), sem("z_read")
        CR, SR = slice(64, 96), slice(96, 128)

        def mla_in_pe(pe):
            for i in range(6):
                u = U_MIN + i
                pe.wait_ge(w_split, u + 3)
                if i >= 2:
                    pe.wait_ge(min_read, i - 1)
                project(pe, u % 2, range(DT), h_hi, h_lo, (pjA, pjB)[i % 2])
            pe.wait_ge(min_read, 5)
            pe.wait_ge(kr_step, 2)
            units_pe(pe, U_Z, DT, range(DT), h_hi, h_lo, lambda it, j: pe.wait_ge(z_read, it * 2 + (j + 1)))

        def mla_in_dve(dve):
            for i in range(5):
                dve.wait_ge(unit_done, U_MIN + i + 3)
                nc.vector.tensor_copy(u5[:, i, :], flat((pjA, pjB)[i % 2])).then_inc(min_read, 1)
                if i < 3:
                    NQ.wait(dve, "sq", i + 1)
                    if i == 0:
                        nc.vector.tensor_copy(ssq[:, :], sq[:, :]).then_inc(NQ["ssq"], 1)
                    else:
                        NQ.wait(dve, "ssq", i)
                        nc.vector.tensor_tensor(ssq[:, :], ssq[:, :], sq[:, :], ALU.add).then_inc(NQ["ssq"], 1)
            dve.wait_ge(unit_done, U_MIN + 5 + 3)
            ps = flat(pjB)
            nc.vector.scalar_tensor_tensor(tmp[0][CR, :], ps[CR, :], MLA_SCALE, cos_sin[CR, :], ALU.mult, ALU.mult).then_inc(kr_step, 1)
            nc.vector.scalar_tensor_tensor(tmp[1][CR, :], ps[SR, :], MLA_SCALE, cos_sin[SR, :], ALU.mult, ALU.mult).then_inc(kr_step, 1)
            dve.wait_ge(kr_step, 2)
            nc.vector.tensor_tensor(k_rope[CR, :], tmp[0][CR, :], tmp[1][CR, :], ALU.add).then_inc(kr_step, 1)

        def mla_in_act(act):
            for i in range(3):
                act.wait_ge(min_read, i + 1)
                if i:
                    NQ.wait(act, "ssq", i)
                nc.scalar.activation(sq[:, :], u5[:, i, :], ACT.Square).then_inc(NQ["sq"], 1)
            with act.Fori(0, DT // 2) as it:
                for j, src in enumerate((pjA, pjB)):
                    act.wait_ge(unit_done, it * 2 + (U_Z + j + 3))
                    nc.scalar.activation(flat(mix[:, bass.ds(it * 2 + j, 1), :]), flat(src), ACT.Silu).then_inc(z_read, 1)

        def lora_norms_pe(pe):
            norm_pe(pe, NQ, 3)
            NQ.wait(pe, "lo", 3)
            norm_pe(pe, NKV, 2, DT)

        def lora_norms_act(act):
            norm_root(act, NQ, QL)
            norm_split_act(act, NQ, 3, lambda k: cq_hi[:, k, :])
            act.wait_ge(min_read, 5)
            for i in range(2):
                if i:
                    NKV.wait(act, "ssq", 1)
                nc.scalar.activation(sq[:, :], u5[:, 3 + i, :], ACT.Square).then_inc(NKV["sq"], 1)
            norm_root(act, NKV, KVL, DT)
            norm_split_act(act, NKV, 2, lambda k: ckv_hi[:, k, :])

        def lora_norms_dve(dve):
            norm_spread(dve, NQ)
            norm_split_dve(dve, NQ, 3, lambda k: u5[:, k, :], gain_of(V_QN), lambda k: cq_hi[:, k, :], lambda k: cq_lo[:, k, :])
            NKV.wait(dve, "sq", 1)
            nc.vector.tensor_copy(ssq[:, :], sq[:, :]).then_inc(NKV["ssq"], 1)
            NKV.wait(dve, "sq", 2)
            NKV.wait(dve, "ssq", 1)
            nc.vector.tensor_tensor(ssq[:, :], ssq[:, :], sq[:, :], ALU.add).then_inc(NKV["ssq"], 1)
            norm_spread(dve, NKV)
            norm_split_dve(dve, NKV, 2, lambda k: u5[:, 3 + k, :], gain_of(V_KVN), lambda k: ckv_hi[:, k, :], lambda k: ckv_lo[:, k, :])

        mla.n_lo = 3
        rope_x = at("rope_x", R_W + 16384, [P, T])
        rope_y = at("rope_y", R_W, [P, T])

        def mla_project(pe, n, b, first_scores):
            pe.wait_ge(w_split, n + (U_HEAD + 3))
            slot = (U_HEAD + b) % 2
            project(pe, slot, (0, 1, 2), cq_hi, cq_lo, pjA, done=False).then_inc(q_ready, 1)
            if not (isinstance(n, int) and n == 0):
                pe.wait_ge(mla.vaug_done, n)
                pe.wait_ge(mla.cneg_done, n)
            project(pe, slot, (3, 4), ckv_hi, ckv_lo, pjB, done=False, halves=(0,))
            first_scores()
            project(pe, slot, (3, 4), ckv_hi, ckv_lo, pjB, halves=(1,))

        q_ready = sem("mla_q_ready")

        def mla_setup_act(act):
            act.wait_ge(mla.setup, 1)
            for b in range(2):
                nc.scalar.activation(mla.bufs[2][b][CR, :], k_rope[CR, :], ACT.Copy).then_inc(mla.setup, 1)

        def mla_setup_dve(dve):
            q_hi, q_lo, k_hi, k_lo, vaug = mla.bufs
            NKV.wait(dve, "lo", 2)
            dve.wait_ge(kr_step, 3)
            for b in range(2):
                nc.vector.memset(q_hi[b][96:97, :].bitcast(F32), 0.0)
                nc.vector.memset(q_lo[b][96:97, :].bitcast(F32), 0.0)
                nc.vector.memset(k_hi[b][96:97, :].bitcast(F32), 1.0)
                nc.vector.memset(k_lo[b][96:97, :].bitcast(F32), 0.0)
                last = nc.vector.memset(vaug[b][:, :, HD:P], 1.0)
            last.then_inc(mla.setup, 1)
            dve.wait_ge(mla.setup, 3)
            for b in range(2):
                nc.vector.tensor_tensor(k_lo[b][CR, :], k_rope[CR, :], k_hi[b][CR, :].bitcast(F32), ALU.subtract).then_inc(mla.setup, 1)

        def mla_prepare_act(act, n, b, turn):
            q_hi, q_lo, k_hi, k_lo, vaug = mla.bufs
            q, kv = flat(pjA), flat(pjB)
            act.wait_ge(q_ready, n + 1)
            nc.scalar.activation(q_hi[b][0:HD, :], q[0:HD, :], ACT.Copy, scale=MLA_SCALE).then_inc(mla.hi_done, 1)

            def keys():
                act.wait_ge(unit_done, n + (U_HEAD + 3))
                nc.scalar.activation(k_hi[b][0:HD, :], kv[0:HD, :], ACT.Copy).then_inc(mla.hi_done, 1)

            def values():
                if not (isinstance(n, int) and n == 0):
                    act.wait_ge(mla.vt_ready, n)
                nc.scalar.activation(mla_vT[:, :], kv[HD:P, :], ACT.Copy).then_inc(mla.vT_done, 1)

            def rope():
                act.wait_ge(mla.rope_done, n * 3 + 3)
                nc.scalar.activation(q_hi[b][CR, :], rope_x[CR, :], ACT.Copy).then_inc(mla.hi_done, 1)
            return {1: keys, 2: values, 3: rope}

        def mla_prepare_dve(dve, n, b):
            q_hi, q_lo, k_hi, k_lo, vaug = mla.bufs
            q, kv = flat(pjA), flat(pjB)
            dve.wait_ge(q_ready, n + 1)
            if not (isinstance(n, int) and n == 0):
                dve.wait_ge(mla.lo_done, n * 3)
            nc.vector.tensor_tensor(rope_x[CR, :], q[CR, :], cos_sin[CR, :], ALU.mult).then_inc(mla.rope_done, 1)
            nc.vector.tensor_tensor(rope_y[CR, :], q[SR, :], cos_sin[SR, :], ALU.mult).then_inc(mla.rope_done, 1)
            dve.wait_ge(mla.rope_done, n * 3 + 2)
            nc.vector.tensor_tensor(rope_x[CR, :], rope_x[CR, :], rope_y[CR, :], ALU.add).then_inc(mla.rope_done, 1)
            dve.wait_ge(mla.hi_done, n * 3 + 1)
            nc.vector.scalar_tensor_tensor(q_lo[b][0:HD, :], q[0:HD, :], MLA_SCALE, q_hi[b][0:HD, :].bitcast(F32),
                                           ALU.mult, ALU.subtract).then_inc(mla.lo_done, 1)
            dve.wait_ge(mla.hi_done, n * 3 + 2)
            nc.vector.tensor_tensor(k_lo[b][0:HD, :], kv[0:HD, :], k_hi[b][0:HD, :].bitcast(F32), ALU.subtract).then_inc(mla.lo_done, 1)
            dve.wait_ge(mla.hi_done, n * 3 + 3)
            dve.wait_ge(mla.rope_done, n * 3 + 3)
            nc.vector.tensor_tensor(q_lo[b][CR, :], rope_x[CR, :], q_hi[b][CR, :].bitcast(F32), ALU.subtract).then_inc(mla.lo_done, 1)

        m2_hi, m2_lo, mo_added = sem("mix2_hi"), sem("mix2_lo"), sem("mo_added")
        p_in, p_hi_done, p_lo_done = sem("p_in"), sem("p_hi_done"), sem("p_lo_done")
        pg_read, pp_read, ple_added = sem("ple_gate_read"), sem("ple_proj_read"), sem("ple_added")
        p_raw = at("p_raw", R_M, [P, 2, T])
        p_hi, p_lo = at("p_hi", R_M + 8192, [P, 2, T], F32R), at("p_lo", R_M + 16384, [P, 2, T], F32R)

        def ple_pe(pe):
            pe.wait_ge(mo_added, DT + 2)
            pe.wait_ge(p_lo_done, 1)
            with pe.Fori(0, DT) as e:
                pe.wait_ge(w_split, e * 2 + (U_PLE + 3))
                pe.wait_ge(pg_read, e + 1)
                project(pe, U_PLE % 2, range(DT), h_hi, h_lo, pjA)
                pe.wait_ge(w_split, e * 2 + (U_PLE + 4))
                pe.wait_ge(pp_read, e + 1)
                project(pe, (U_PLE + 1) % 2, range(2), p_hi, p_lo, pjB)

        def ple_act(act):
            with act.Fori(0, DT) as e:
                act.wait_ge(unit_done, e * 2 + (U_PLE + 3))
                act.wait_ge(pp_read, e + 1)
                nc.scalar.activation(tmp[0][:, :], flat(pjA), ACT.Sigmoid).then_inc(pg_read, 1)
                act.wait_ge(ple_added, e + 2)
                nc.scalar.activation(sq[:, :], flat(x[:, bass.ds(e, 1), :]), ACT.Square).then_inc(N5["sq"], 1)

        def ple_dve(dve):
            nc.vector.memset(ssq[:, :], 0.0).then_inc(N5["ssq"], 1)
            with dve.Fori(0, DT) as e:
                tile = flat(x[:, bass.ds(e, 1), :])
                dve.wait_ge(unit_done, e * 2 + (U_PLE + 4))
                dve.wait_ge(pg_read, e + 2)
                dve.wait_ge(ple_added, e + 1)
                nc.vector.tensor_tensor(tmp[1][:, :], flat(pjB), tmp[0][:, :], ALU.mult).then_inc(pp_read, 1)
                dve.wait_ge(pp_read, e + 2)
                nc.vector.tensor_tensor(tile, tmp[1][:, :], tile, ALU.add).then_inc(ple_added, 1)
                N5.wait(dve, "sq", e + 1)
                N5.wait(dve, "ssq", e + 1)
                nc.vector.tensor_tensor(ssq[:, :], ssq[:, :], sq[:, :], ALU.add).then_inc(N5["ssq"], 1)

        stage = at("const_stage", R_M, [P, N_CONST])
        pos_i = at("pos_i", R_S + 8192, [P, T], I32)
        ang = [at(f"ang{i}", R_S + 12288 + 4096 * i, [P, T]) for i in range(4)]

        def setup_dve(dve):
            dve.wait_ge(consts_in, 16)
            for dst, k, n in ((ident[:, :], K_ID, P), (ones[:, :], K_ONE, P), (head_mean[:, :], K_BLK, P),
                              (ident_bf[:, :], K_ID, P), (masks[:, :, :].rearrange("p a n -> p (a n)"), K_MASK, 1024),
                              (att_mask[:, :], K_ATT, P), (small_const[:, :], K_CNT, 40)):
                nc.vector.tensor_copy(dst, stage[:, k:k + n]).then_inc(setup_done, 1)

        N_SETUP = 7

        def rope_dve(dve):
            r = slice(64, 128)
            two_pi = 2 * np.pi
            c1 = 6.28125
            c2 = float(np.floor((two_pi - c1) * 2 ** 20) / 2 ** 20)
            c3 = float(two_pi - c1 - c2)
            magic = 1.5 * 2 ** 23
            k = [0]

            def step(ins):
                ins.then_inc(rope_s, 1)
                k[0] += 1
                dve.wait_ge(rope_s, k[0])
            dve.wait_ge(pos_in, 16)
            dve.wait_ge(setup_done, N_SETUP)
            freq, sign = small_const[r, 32:33], small_const[SR, 33:34]
            step(nc.vector.tensor_copy(ang[0][r, :], pos_i[r, :]))
            step(nc.vector.tensor_scalar(ang[0][r, :], ang[0][r, :], freq, None, ALU.mult))
            step(nc.vector.tensor_scalar(ang[1][r, :], ang[0][r, :], float(1 / two_pi), magic, ALU.mult, ALU.add))
            step(nc.vector.tensor_scalar(ang[1][r, :], ang[1][r, :], magic, None, ALU.subtract))
            for c in (c1, c2, c3):
                step(nc.vector.scalar_tensor_tensor(ang[0][r, :], ang[1][r, :], -c, ang[0][r, :], ALU.mult, ALU.add))
            lim = 3.14159
            step(nc.vector.tensor_scalar(ang[0][r, :], ang[0][r, :], lim, -lim, ALU.min, ALU.max))
            dve.wait_ge(rope_a, 2)
            step(nc.vector.tensor_tensor(ang[2][CR, :], ang[2][CR, :], ang[2][CR, :], ALU.mult))
            step(nc.vector.tensor_scalar(cos_sin[CR, :], ang[2][CR, :], -2.0, 1.0, ALU.mult, ALU.add))
            step(nc.vector.tensor_scalar(cos_sin[SR, :], ang[2][SR, :], sign, None, ALU.mult))

        def rope_act(act):
            act.wait_ge(rope_s, 8)
            nc.scalar.activation(ang[2][CR, :], ang[0][CR, :], ACT.Sin, scale=0.5).then_inc(rope_a, 1)
            nc.scalar.activation(ang[2][SR, :], ang[0][SR, :], ACT.Sin).then_inc(rope_a, 1)

        def first_norm_dve(dve):
            for k in range(DT):
                norm_scaled(NF, x[:, k, :], x[:, k, :], vec[:, V_LNF + k:V_LNF + k + 1]).then_inc(NF["h"], 1)

        def squares_dve(dve, s):
            for k in range(DT):
                s.wait(dve, "sq", k + 1)
                if k == 0:
                    nc.vector.tensor_copy(ssq[:, :], sq[:, :]).then_inc(s["ssq"], 1)
                else:
                    s.wait(dve, "ssq", k)
                    nc.vector.tensor_tensor(ssq[:, :], ssq[:, :], sq[:, :], ALU.add).then_inc(s["ssq"], 1)

        def squares_act(act, s, arrived):
            for k in range(DT):
                arrived(k)
                if k:
                    s.wait(act, "ssq", k)
                nc.scalar.activation(sq[:, :], x[:, k, :], ACT.Square).then_inc(s["sq"], 1)

        block = ctx.enter_context(nc.Block())

        @block.sync
        def _(sp):
            sp.dma_start(stage[:, :], consts).then_inc(consts_in, 16)
            sp.dma_start(vec[:, :], vecs).then_inc(vecs_in, 16)
            sp.dma_start(pos_i[:, :], pos).then_inc(pos_in, 16)

            def load(u, s):
                sp.wait_ge(w_split, u + 1)
                sp.dma_start(raw[s][:, :, :].rearrange("p k n -> p (k n)"), wpack[u, :, :] if isinstance(u, int) else
                             wpack[bass.ds(u, 1), :, :].rearrange("o p n -> (o p) n")).then_inc(w_loaded[s], 16)
            with sp.Fori(0, N_UNITS // 2) as it:
                for s in range(2):
                    load(it * 2 + s, s)
            if N_UNITS % 2:
                load(N_UNITS - 1, 0)
            for k in range(DT):
                N5.wait(sp, "h", k + 1)
                sp.dma_start(outT[k * P:(k + 1) * P, :], tmp[k % 2][:, :]).then_inc(out_stored[k % 2], 16)
            for s in range(2):
                sp.wait_ge(out_stored[s], 16 * DT // 2)

        @block.gpsimd
        def _(pool):
            pool.sem_inc(w_split, 2)
            nc.gpsimd.memset(zero[:, :], 0.0).then_inc(zero_set, 1)
            pool.wait_ge(zero_set, 1)
            no_change = zero[:, :].rearrange("p (a n) -> p a n", a=1).to_broadcast([P, DT, P])

            def split(u, s, loads):
                pool.wait_ge(w_loaded[s], loads)
                pool.wait_ge(unit_done, u + 1)
                nc.gpsimd.tensor_tensor(w_hi[s][:, :, :], raw[s][:, :, :], no_change, ALU.add).then_inc(w_hi_done, 1)
                pool.wait_ge(w_hi_done, u + 1)
                nc.gpsimd.tensor_tensor(w_lo[s][:, :, :], raw[s][:, :, :], w_hi[s][:, :, :].bitcast(F32), ALU.subtract)\
                    .then_inc(w_split, 1)
            with pool.Fori(0, N_UNITS // 2) as it:
                for s in range(2):
                    split(it * 2 + s, s, it * 16 + 16)
            if N_UNITS % 2:
                split(N_UNITS - 1, 0, 16 * (N_UNITS // 2) + 16)

        @block.scalar
        def _(act):
            act.sem_inc(fv_read, 2)
            act.sem_inc(restA, 1)
            act.sem_inc(fox.pv_done, 4)
            act.sem_inc(mla.pv_done, 4)
            act.sem_inc(gate_read, 1)
            act.sem_inc(z_read, 2)
            act.sem_inc(pg_read, 1)
            for k in range(DT):
                act.dma_start(x[:, k, :], xT[k * P:(k + 1) * P, :]).then_inc(x_in[k], 16)
            squares_act(act, N1, lambda k: act.wait_ge(x_in[k], 16))
            act.wait_ge(setup_done, N_SETUP)
            norm_root(act, N1, D)
            norm_split_act(act, N1, DT, hi_tile)
            rope_act(act)
            small_act(act)
            fox_values_act(act)
            steps(act, fox, lambda n, b, turn: step_act(act, fox, n, b, turn, fox_prepare_act))
            last_act(act, fox)
            rest_act(act)
            gla_act(act)
            act.wait_ge(g_o, 8)
            mix_split_act(act, m_hi)
            act.wait_ge(m_lo, DT)
            for k in range(DT):
                act.dma_start(x[:, k, :], xT[k * P:(k + 1) * P, :]).then_inc(x_back, 16)
            residual_squares(act, wo_added, 0, N2)
            norm_root(act, N2, D)
            norm_split_act(act, N2, DT, hi_tile)
            mlp_act(act)
            norm_root(act, NF, D)
            squares_act(act, N3, lambda k: NF.wait(act, "h", k + 1))
            norm_root(act, N3, D)
            norm_split_act(act, N3, DT, hi_tile)
            mla_in_act(act)
            lora_norms_act(act)
            mla_setup_act(act)
            steps(act, mla, lambda n, b, turn: step_act(act, mla, n, b, turn, mla_prepare_act))
            last_act(act, mla)
            act.wait_ge(mla.norm_done, 2 * MLA_H)
            mix_split_act(act, m2_hi)
            act.wait_ge(m2_lo, DT)
            act.dma_start(p_raw[:, :, :], pT.rearrange("(k p) t -> p k t", p=P)).then_inc(p_in, 16)
            residual_squares(act, mo_added, 0, N4)
            act.wait_ge(p_in, 16)
            nc.scalar.activation(tau(p_hi), tau(p_raw), ACT.Copy).then_inc(p_hi_done, 1)
            norm_root(act, N4, D)
            norm_split_act(act, N4, DT, hi_tile)
            ple_act(act)
            norm_root(act, N5, D)

        @block.vector
        def _(dve):
            for s, credit in ((wo_added, 2), (up_read, 1), (dn_added, 2), (pp_read, 1), (a_split_lo, 1), (ple_added, 1), (mo_added, 2), (restB, 1)):
                dve.sem_inc(s, credit)
            setup_dve(dve)
            squares_dve(dve, N1)
            dve.wait_ge(vecs_in, 16)
            dve.wait_ge(setup_done, N_SETUP)
            norm_spread(dve, N1)
            norm_split_dve(dve, N1, DT, lambda k: x[:, k, :], gain_of(V_LN1), hi_tile, lo_tile)
            rope_dve(dve)
            small_dve(dve)
            fox_setup_dve(dve)
            steps(dve, fox, lambda n, b, turn: step_dve(dve, fox, n, b, turn, fox_prepare_dve, 4, False))
            for half in range(2):
                norm_half_dve(dve, fox, FOX_H - 1, 1, half, 4 + FOX_H // 2 - 1, False)
            rest_dve(dve)
            pool_dve(dve)
            gla_dve(dve)
            mix_split_dve(dve, m_hi, m_lo)
            dve.wait_ge(x_back, 16 * DT)
            residual_dve(dve, U_WO, wo_added, 0, N2)
            norm_spread(dve, N2)
            norm_split_dve(dve, N2, DT, lambda k: x[:, k, :], gain_of(V_LN2), hi_tile, lo_tile)
            mlp_dve(dve)
            norm_spread(dve, NF)
            first_norm_dve(dve)
            squares_dve(dve, N3)
            norm_spread(dve, N3)
            norm_split_dve(dve, N3, DT, lambda k: x[:, k, :], gain_of(V_NG), hi_tile, lo_tile)
            mla_in_dve(dve)
            lora_norms_dve(dve)
            mla_setup_dve(dve)
            steps(dve, mla, lambda n, b, turn: step_dve(dve, mla, n, b, turn, mla_prepare_dve, 0, True))
            for half in range(2):
                norm_half_dve(dve, mla, MLA_H - 1, 1, half, MLA_H // 2 - 1, True)
            mix_split_dve(dve, m2_hi, m2_lo)
            residual_dve(dve, U_MO, mo_added, 0, N4)
            dve.wait_ge(p_hi_done, 1)
            nc.vector.tensor_tensor(tau(p_lo), tau(p_raw), tau(p_hi).bitcast(F32), ALU.subtract).then_inc(p_lo_done, 1)
            norm_spread(dve, N4)
            norm_split_dve(dve, N4, DT, lambda k: x[:, k, :], lambda k: None, hi_tile, lo_tile)
            ple_dve(dve)
            norm_spread(dve, N5)
            for k in range(DT):
                if k >= 2:
                    dve.wait_ge(out_stored[k % 2], 16 * (k // 2))
                norm_scaled(N5, tmp[k % 2][:, :], x[:, k, :], vec[:, V_FN + k:V_FN + k + 1]).then_inc(N5["h"], 1)

        @block.tensor
        def _(pe):
            pe.sem_inc(unit_done, 2)
            pe.wait_ge(setup_done, N_SETUP)
            norm_pe(pe, N1, DT)
            N1.wait(pe, "lo", DT)
            pe.wait_ge(w_split, U_SMALL + 3)
            project(pe, U_SMALL % 2, range(DT), h_hi, h_lo, pjA)
            fox_values_pe(pe)
            pe.wait_ge(fv_read, 4 + 2)
            pe.wait_ge(fox.setup, 1)
            steps(pe, fox, lambda n, b, turn: step_pe(pe, fox, n, b, turn, fox_project, fox_vT))
            last_pe(pe, fox)
            rest_pe(pe)
            gla_pe(pe)
            pe.wait_ge(m_lo, DT)
            units_pe(pe, U_WO, DT, range(DT), h_hi, h_lo, lambda it, j: pe.wait_ge(wo_added, it * 2 + (j + 1)))
            norm_pe(pe, N2, DT + 1)
            N2.wait(pe, "lo", DT)
            mlp_pe(pe)
            norm_pe(pe, NF, DT + 1)
            norm_pe(pe, N3, DT)
            N3.wait(pe, "lo", DT)
            mla_in_pe(pe)
            lora_norms_pe(pe)
            NKV.wait(pe, "lo", 2)
            pe.wait_ge(z_read, DT + 2)
            pe.wait_ge(mla.setup, 5)
            steps(pe, mla, lambda n, b, turn: step_pe(pe, mla, n, b, turn, mla_project, mla_vT))
            last_pe(pe, mla)
            pe.wait_ge(m2_lo, DT)
            units_pe(pe, U_MO, DT, range(DT), h_hi, h_lo, lambda it, j: pe.wait_ge(mo_added, it * 2 + (j + 1)))
            norm_pe(pe, N4, DT + 1)
            N4.wait(pe, "lo", DT)
            ple_pe(pe)
            norm_pe(pe, N5, DT + 1)


def shape_constants():
    c = np.zeros((P, N_CONST), np.float32)
    i = np.arange(P)
    c[:, K_ID:K_ID + P] = np.eye(P)
    c[:, K_ONE:K_ONE + P] = 1.0
    c[:, K_BLK:K_BLK + P] = (i[:, None] // HD == i[None, :] // HD) / HD
    later = i[None, :] > i[:, None]
    chunk_later = i[None, :] // CHUNK > i[:, None] // CHUNK
    for k, m in ((0, later), (2, chunk_later)):
        by_query = c[:, K_MASK + 256 * k:K_MASK + 256 * (k + 1)]
        by_query[:, 0:P], by_query[:, P:] = m * NEG, NEG
        by_key = c[:, K_MASK + 256 * (k + 1):K_MASK + 256 * (k + 2)]
        by_key[:, 0:P], by_key[:, P:] = NEG, m.T * NEG
    c[:, K_ATT:K_ATT + P] = (i[:, None] // CHUNK == i[None, :] // CHUNK) & (i[:, None] <= i[None, :])
    t = np.arange(16)
    for tile, row, w in ((0, 0, 2), (0, HD, 4), (1, 0, 8), (1, HD, 16)):
        c[row:row + HD, K_CNT + 16 * tile:K_CNT + 16 * tile + 16] = 1.0 / np.minimum(t + 1, w)
    half = ROPE // 2
    c[:, K_FREQ] = (np.float32(ROPE_THETA) ** (-np.arange(0, ROPE, 2, dtype=np.float32) / np.float32(ROPE)))[i % half]
    c[:, K_SIGN] = np.where(i % ROPE < half, -1.0, 1.0)
    c[:, K_EPS] = EPS
    c[:, K_EPS + 1] = 1.0
    return c


def pack_units(w_in, w_o, w_gu, w_down, mla_in, w_q_b, w_kv_b, mla_out, ple_gate, ple_proj):
    units = np.zeros((N_UNITS, P, DT, P), np.float32)

    def put(u, w, cols, kt0=0, to=0, rows=slice(None)):
        part = w[rows][:, cols]
        k = part.shape[0] // P
        units[u, :, kt0:kt0 + k, to:to + part.shape[1]] = part.reshape(k, P, -1).transpose(1, 0, 2)

    def tile(c0, n=P):
        return slice(c0, c0 + n)

    put(U_SMALL, w_in, tile(C_GA, 16))
    put(U_SMALL, w_in, tile(C_FF, FOX_H), to=32)
    for i in range(FOX_H // 2):
        put(U_FV + i, w_in, tile(C_FV + P * i))
    for h in range(FOX_H):
        put(U_FQK + h, w_in, tile(C_FQ + HD * h, HD))
        put(U_FQK + h, w_in, tile(C_FK + HD * h, HD), to=HD)
    for i in range(N_REST):
        put(U_REST + i, w_in, tile(P * i))
    for i in range(DT):
        put(U_WO + i, w_o, tile(P * i))
    f0 = 0
    for c, n in enumerate(MLP_CHUNKS):
        for f in range(n):
            put(U_GU[c] + 2 * f, w_gu, tile(P * (f0 + f)))
            put(U_GU[c] + 2 * f + 1, w_gu, tile(FF + P * (f0 + f)))
        for i in range(DT):
            put(U_DN[c] + i, w_down, tile(P * i), rows=slice(P * f0, P * (f0 + n)))
        f0 += n
    for i in range(5):
        put(U_MIN + i, mla_in, tile(P * i))
    half = ROPE // 2
    k0 = QL + KVL
    put(U_MIN + 5, mla_in, tile(k0, ROPE), to=64)
    put(U_MIN + 5, mla_in, tile(k0 + half, half), to=96)
    put(U_MIN + 5, mla_in, tile(k0, half), to=96 + half)
    for i in range(DT):
        put(U_Z + i, mla_in, tile(k0 + ROPE + P * i))
    for h in range(MLA_H):
        q0 = (NOPE + ROPE) * h
        put(U_HEAD + h, w_q_b, tile(q0, NOPE + ROPE))
        put(U_HEAD + h, w_q_b, tile(q0 + NOPE + half, half), to=96)
        put(U_HEAD + h, w_q_b, tile(q0 + NOPE, half), to=96 + half)
        put(U_HEAD + h, w_kv_b, tile(P * h), kt0=3)
    for i in range(DT):
        put(U_MO + i, mla_out, tile(P * i))
        put(U_PLE + 2 * i, ple_gate, tile(P * i))
        put(U_PLE + 2 * i + 1, ple_proj, tile(P * i))
    return units.reshape(N_UNITS, P, DT * P)


def pack_vectors(inputs):
    v = np.zeros((P, N_VEC), np.float32)
    for col, name in ((V_LN1, "ln1"), (V_LN2, "ln2"), (V_LNF, "ln_f"), (V_FN, "final_norm_2"), (V_NG, "norm_g_2"), (V_GN, "gla_gn"), (V_BA, "b_a"),
                      (V_PS, "pool_scale"), (V_QN, "mla_q_norm_2"), (V_KVN, "mla_kv_norm_2")):
        a = np.asarray(inputs[name]).reshape(-1, P)
        v[:, col:col + a.shape[0]] = a.T
    v[32:32 + FOX_H, V_BF] = np.asarray(inputs["b_f"])[0]
    w = np.asarray(inputs["w_pool"])[0]
    for g in range(4):
        r = HD * (g % 2)
        v[r:r + HD, V_WPOOL + P * (g // 2) + r:V_WPOOL + P * (g // 2) + r + HD] = w[g]
    v[0:16, V_WAUP:V_WAUP + GLA_W] = np.asarray(inputs["w_a_up"])[0]
    return v


def kernel(**inputs):
    import concourse.bacc as bacc
    from concourse.bass_utils import run_bass_kernel_spmd

    def first(name):
        return np.asarray(inputs[name])[0]

    arrays = {
        "wpack": pack_units(first("w_in"), first("w_o"), first("w_gu"), first("w_down"), first("mla_w_in_2"),
                            first("mla_w_q_b_2"), first("mla_w_kv_b_2"), first("mla_w_out_2"), first("ple_gate_2"),
                            first("ple_proj_2")),
        "xT": np.ascontiguousarray(first("x").T),
        "pT": np.ascontiguousarray(np.asarray(inputs["p_2"])[0, 0].T),
        "vecs": pack_vectors(inputs),
        "consts": shape_constants(),
        "pos": np.ascontiguousarray(np.broadcast_to(np.asarray(inputs["positions_2"]), (P, T))),
    }
    nc = bacc.Bacc("TRN2", target_bir_lowering=False, num_devices=1)
    args = [nc.dram_tensor(f"in_{n}", a.shape, mybir.dt.from_np(a.dtype), kind="ExternalInput").ap() for n, a in arrays.items()]
    out = nc.dram_tensor("out", (D, T), F32, kind="ExternalOutput").ap()
    f_rows = nc.dram_tensor("f_rows", (2, FOX_H, T), F32).ap()
    build(nc, *args, out, f_rows)
    r = run_bass_kernel_spmd(nc, [{f"in_{n}": a for n, a in arrays.items()}], core_ids=[0])
    return np.ascontiguousarray(r.results[0]["out"].T).reshape(1, T, D)
```

```python
from contextlib import ExitStack

import numpy as np

import concourse.bass as bass
from concourse import mybir

F32 = mybir.dt.float32
F32R = mybir.dt.float32r
BF16 = mybir.dt.bfloat16
U32 = mybir.dt.uint32
I32 = mybir.dt.int32
ALU = mybir.AluOpType
ACT = mybir.ActivationFunctionType
AX_X = mybir.AxisListType.X

P = 128
T = 1024
D = 1024
DT = D // P
HALF = 512
EPS = 1e-6
CHUNK = 64
NCH = T // CHUNK

POOL_W = GLA_W = 256
GLA_TAU = 16.0
FOX_W = 512
FOX_H = 8
HD = 64
FF = 2816
FT = FF // P
MLP_CHUNKS = (6, 6, 5, 5)
MLA_H = 16
QL, KVL, NOPE, ROPE = 384, 256, 64, 32
MLA_SCALE = (NOPE + ROPE) ** -0.5
ROPE_THETA = 10000.0
NEG = -1.0e30

C_POOL, C_GQ, C_GK, C_GV, C_GG, C_GA = 0, 256, 512, 768, 1024, 1280
C_FQ = 1296
C_FK, C_FV, C_FF = C_FQ + FOX_W, C_FQ + 2 * FOX_W, C_FQ + 3 * FOX_W

U_SMALL = 0
U_FV = U_SMALL + 1
U_FQK = U_FV + FOX_H // 2
U_REST = U_FQK + FOX_H
N_REST = 10
U_WO = U_REST + N_REST
U_GU, U_DN = [], []
_u = U_WO + DT
for _n in MLP_CHUNKS:
    U_GU.append(_u)
    U_DN.append(_u + 2 * _n)
    _u += 2 * _n + DT
U_MIN = _u
U_Z = U_MIN + 6
U_HEAD = U_Z + DT
U_MO = U_HEAD + MLA_H
U_PLE = U_MO + DT
U_GATE = U_PLE + 2
N_UNITS = U_GATE + DT

V_LN1, V_LN2, V_LNF, V_NG = 0, 8, 16, 24
V_GN, V_BA, V_PS, V_QN, V_KVN, V_BF, V_FN = 32, 34, 36, 38, 41, 43, 44
V_WPOOL, V_WAUP = 56, 56 + 256
N_VEC = 56 + 512

K_ID, K_ONE, K_BLK = 0, 128, 256
K_MASK = 384
K_ATT = K_MASK + 4 * 256
K_CNT = K_ATT + 128
K_FREQ, K_SIGN, K_EPS = K_CNT + 32, K_CNT + 33, K_CNT + 34
N_CONST = K_CNT + 40


def build(nc, wpack, xT, pT, vecs, consts, pos, outT, f_rows):
    with ExitStack() as ctx:
        def sem(name):
            return ctx.enter_context(nc.semaphore(name))

        base = (nc.sbuf_base + 63) // 64 * 64
        R_X = base
        R_S = R_X + 32768
        R_M = R_S + 28672
        R_H = R_M + 32768
        R_RING = R_H + 65536
        R_W = R_RING + 24576
        R_C = R_W + 20480
        top = [R_C]

        def at(name, offset, shape, dt=F32):
            return nc.alloc_sbuf_tensor_at(name, shape, dt, offset=offset)

        def const(name, shape, dt=F32):
            n = int(np.prod(shape[1:])) * mybir.dt.size(dt)
            off = top[0]
            top[0] += (n + 31) // 32 * 32
            return at(name, off, shape, dt)

        x = at("x", R_X, [P, DT, T])
        h_hi = at("h_hi", R_H, [P, DT, T], F32R)
        h_lo = at("h_lo", R_H + 32768, [P, DT, T], F32R)
        mix = at("mix", R_M, [P, DT, T])
        mix_lo = at("mix_lo", R_M, [P, DT, T], F32R)
        raw = [at(f"w_raw{s}", R_RING + 4096 * s, [P, DT, P]) for s in range(2)]
        w_hi = [at(f"w_hi{s}", R_RING + 8192 + 4096 * s, [P, DT, P], F32R) for s in range(2)]
        w_lo = [at(f"w_lo{s}", R_RING + 16384 + 4096 * s, [P, DT, P], F32R) for s in range(2)]
        ssq = at("ssq", R_W, [P, T])
        diag = at("diag", R_W + 4096, [P, T])
        tmp = [at(f"tmp{s}", R_W + 8192 + 4096 * s, [P, T]) for s in range(2)]
        sq = at("sq", R_W + 16384, [P, T])
        cos_sin = at("cos_sin", R_S, [P, T])

        vec = const("vec", [P, N_VEC])
        ident = const("ident", [P, P])
        ones = const("ones", [P, P])
        head_mean = const("head_mean", [P, P])
        small_const = const("small_const", [P, 40])
        ident_bf = const("ident_bf", [P, P], BF16)
        masks = const("masks", [P, 4, 256], BF16)
        att_mask = const("att_mask", [P, P], U32)
        rt = const("rt", [P, 16])
        rv = const("rv", [P, 32])
        mx = const("mx", [P, 8])
        zero = const("zero", [P, 1])
        c_neg = const("c_neg", [DT, P], F32R)
        assert top[0] <= nc.sbuf_usable_end, top[0]
        eps = small_const[:, K_EPS - K_CNT:K_EPS - K_CNT + 1]

        PS = ctx.enter_context(nc.psum_tensor("ps", [P, 8, HALF], F32))
        pjA, pjB = PS[:, 0:2, :], PS[:, 2:4, :]

        def flat(ap):
            return ap.rearrange("p a n -> p (a n)")

        w_loaded = [sem(f"w_loaded{s}") for s in range(2)]
        w_hi_done = sem("w_hi_done")
        w_split = sem("w_split")
        unit_done = sem("unit_done")
        consts_in, vecs_in, pos_in = sem("consts_in"), sem("vecs_in"), sem("pos_in")
        x_in = [sem(f"x_in{k}") for k in range(DT)]
        x_back = sem("x_back")
        zero_set = sem("zero_set")
        setup_done = sem("setup_done")
        rope_s = sem("rope_steps")
        rope_a = sem("rope_sines")
        out_stored = [sem(f"out_stored{s}") for s in range(2)]

        norm_sem = {k: sem(f"norm_{k}") for k in ("sq", "ssq", "ms", "rt", "rv", "diag", "bc", "h", "hi", "lo")}
        counted = dict.fromkeys(norm_sem, 0)

        class Norm:
            def __init__(self, tiles, split=True, **more):
                self.base = dict(counted)
                n = dict(sq=tiles, ssq=tiles, h=tiles, hi=tiles * split, lo=tiles * split, ms=1, rt=1, rv=1, diag=1, bc=1)
                n.update(more)
                for k in n:
                    counted[k] += n[k]

            def __getitem__(self, k):
                return norm_sem[k]

            def wait(self, eng, k, n):
                eng.wait_ge(norm_sem[k], n + self.base[k])

        N1, N2 = Norm(DT), Norm(DT, ssq=DT + 1)
        N3 = Norm(DT, sq=2 * DT, ssq=2 * DT + 2, rt=2, rv=5, h=2 * DT)
        NQ, NKV, N4, N5 = Norm(3), Norm(2), Norm(DT, ssq=DT + 1), Norm(DT, ssq=DT + 1, split=False)

        def project(pe, slot, kts, hi, lo, dst, done=True, halves=(0, 1)):
            last = None
            for half in halves:
                t = slice(half * HALF, (half + 1) * HALF)
                n, total = 0, 3 * len(kts)
                for w, a in ((w_lo, hi), (w_hi, lo), (w_hi, hi)):
                    for i, kt in enumerate(kts):
                        last = nc.tensor.matmul(dst[:, half, :], w[slot][:, kt, :], a[:, i, t],
                                                start=(n == 0), stop=(n == total - 1))
                        n += 1
            if done:
                last.then_inc(unit_done, 1)
            return last

        def project_tiles(pe, units, order, hi, lo, arrived, done=1):
            for u, _ in units:
                pe.wait_ge(w_split, u + 3)
            for i, kt in enumerate(order):
                arrived(i)
                for u, dst in units:
                    for half in range(2):
                        t = slice(half * HALF, (half + 1) * HALF)
                        for n, (w, a) in enumerate(((w_lo, hi), (w_hi, lo), (w_hi, hi))):
                            last = nc.tensor.matmul(dst[:, half, :], w[u % 2][:, kt, :], a[:, kt, t], start=(i == 0 and n == 0),
                                                    stop=(i == len(order) - 1 and n == 2))
                    if i == len(order) - 1:
                        last.then_inc(unit_done, done)

        def norm_sum_pe(pe, s, n_ssq, src, col=0):
            s.wait(pe, "ssq", n_ssq)
            for b in range(DT):
                last = nc.tensor.matmul(PS[:, 7, col + b:col + b + 1], src[:, b * P:(b + 1) * P], ones[:, 0:1],
                                        start=True, stop=True)
            return last

        def norm_spread_pe(pe, s, src, bank):
            s.wait(pe, "diag", 1)
            for half in range(2):
                last = nc.tensor.matmul(PS[:, bank + half, :], ones[:, :], src[:, half * HALF:(half + 1) * HALF],
                                        start=True, stop=True)
            return last

        def norm_pe(pe, s, n_ssq):
            norm_sum_pe(pe, s, n_ssq, ssq).then_inc(s["ms"], 1)
            norm_spread_pe(pe, s, diag, 4).then_inc(s["bc"], 1)

        def norm_root(act, s, width, col=0):
            s.wait(act, "ms", 1)
            nc.scalar.activation(rt[:, 0:DT], PS[:, 7, col:col + DT], ACT.Sqrt, bias=eps, scale=1.0 / width)\
                .then_inc(s["rt"], 1)

        def diagonal(dst, col):
            for b in range(DT):
                last = nc.vector.tensor_scalar(dst[:, b * P:(b + 1) * P], ident[:, :], rv[:, col + b:col + b + 1], None, ALU.mult)
            return last

        def norm_diag(dve, s):
            s.wait(dve, "rt", 1)
            nc.vector.reciprocal(rv[:, 0:DT], rt[:, 0:DT]).then_inc(s["rv"], 1)
            s.wait(dve, "rv", 1)
            diagonal(diag, 0).then_inc(s["diag"], 1)

        def norm_spread(dve, s):
            norm_diag(dve, s)
            s.wait(dve, "bc", 1)

        def norm_scaled(s, dst, src, gain):
            if gain is None:
                return nc.vector.tensor_tensor(dst, src, flat(PS[:, 4:6, :]), ALU.mult)
            return nc.vector.scalar_tensor_tensor(dst, src, gain, flat(PS[:, 4:6, :]), ALU.mult, ALU.mult)

        def norm_split_dve(dve, s, n, src, gain, hi, lo):
            for k in range(n + 1):
                if k < n:
                    if k >= 2:
                        s.wait(dve, "lo", k - 1)
                    norm_scaled(s, tmp[k % 2][:, :], src(k), gain(k)).then_inc(s["h"], 1)
                if k >= 1:
                    s.wait(dve, "hi", k)
                    nc.vector.tensor_tensor(lo(k - 1), tmp[(k - 1) % 2][:, :], hi(k - 1).bitcast(F32), ALU.subtract)\
                        .then_inc(s["lo"], 1)

        def norm_split_act(act, s, n, hi):
            for k in range(n):
                s.wait(act, "h", k + 1)
                nc.scalar.activation(hi(k), tmp[k % 2][:, :], ACT.Copy).then_inc(s["hi"], 1)

        def gain_of(col):
            return lambda k: vec[:, col + k:col + k + 1]

        def hi_tile(k):
            return h_hi[:, k, :]

        def lo_tile(k):
            return h_lo[:, k, :]

        def units_pe(pe, first, n, kts, hi, lo, free):
            with pe.Fori(0, n // 2) as it:
                for j, dst in enumerate((pjA, pjB)):
                    pe.wait_ge(w_split, it * 2 + (first + j + 3))
                    free(it, j)
                    project(pe, (first + j) % 2, kts, hi, lo, dst)

        def residual_dve(dve, first, added, added0, s=None, ssq_first=True):
            if s is not None:
                nc.vector.memset(ssq[:, :], 0.0).then_inc(s["ssq"], 1)
            with dve.Fori(0, DT // 2) as it:
                for j, src in enumerate((pjA, pjB)):
                    tile = flat(x[:, bass.ds(it * 2 + j, 1), :])
                    dve.wait_ge(unit_done, it * 2 + (first + j + 3))
                    nc.vector.tensor_tensor(tile, flat(src), tile, ALU.add).then_inc(added, 1)
                    if s is not None:
                        s.wait(dve, "sq", it * 2 + (j + 1))
                        s.wait(dve, "ssq", it * 2 + (j + 1))
                        nc.vector.tensor_tensor(ssq[:, :], ssq[:, :], sq[:, :], ALU.add).then_inc(s["ssq"], 1)

        def residual_squares(act, added, added0, s):
            with act.Fori(0, DT // 2) as it:
                for j in range(2):
                    act.wait_ge(added, it * 2 + (added0 + j + 3))
                    nc.scalar.activation(sq[:, :], flat(x[:, bass.ds(it * 2 + j, 1), :]), ACT.Square).then_inc(s["sq"], 1)

        class Attention:

            def __init__(self, k, heads, rows_max, rows, mask):
                self.k, self.heads, self.rows_max, self.rows, self.mask = k, heads, rows_max, rows, mask
                self.s_ready = sem(f"{k}_s_ready")
                self.exp_done = sem(f"{k}_exp_done")
                self.pv_done = sem(f"{k}_pv_done")
                self.vt_ready = sem(f"{k}_vt_ready")
                self.vT_done = sem(f"{k}_vT_done")
                self.vaug_done = sem(f"{k}_vaug_done")
                self.mp_ready = sem(f"{k}_mp_ready")
                self.max_done = sem(f"{k}_max_done")
                self.mT_ready = sem(f"{k}_mT_ready")
                self.cneg_done = sem(f"{k}_cneg_done")
                self.hi_done = sem(f"{k}_hi_done")
                self.lo_done = sem(f"{k}_lo_done")
                self.rope_done = sem(f"{k}_rope_done")
                self.ln_done = sem(f"{k}_ln_done")
                self.r0_done = sem(f"{k}_r0_done")
                self.newton = sem(f"{k}_newton")
                self.norm_done = sem(f"{k}_norm_done")
                self.mx_done = sem(f"{k}_mx_done")
                self.setup = sem(f"{k}_setup")
                self.row_in = [sem(f"{k}_row_in{b}") for b in range(2)]


        PIECES = []
        for half in range(2):
            for j in range(4 * (half + 1)):
                d = j * P - half * HALF
                PIECES.append((half, j, min(max(d, 0), 256), d))
        N_PIECES = len(PIECES)
        LAST_OF_HALF = (3, N_PIECES - 1)
        S_BANK, O_BANK = (4, 5), (6, 7)
        MAX_BANK = ((2, 0), (3, 0), (0, 0), (1, 0), (2, 2), (0, 4), (2, 5), (0, 6))
        MAX_AFTER = {3: (0,), 4: (1, 2), 5: (3,), 6: (4,), 7: (5,), 8: (6,), 9: (7,)}
        N_MAX = len(MAX_BANK)
        V_BANK, M_BANK = 2, 3
        Pt = [at(f"probs{s}", R_W + 8192 + 2048 * s, [P, HALF]) for s in range(4)]
        ln_sum = at("ln_sum", R_W, [P, HALF])
        r0 = at("r0", R_W + 2048, [P, HALF])
        newton = at("newton", R_W + 4096, [P, HALF])
        rec = at("rec", R_W + 6144, [P, HALF])

        def max_width(i):
            w = max(256, (i % 4 + 1) * P)
            return w, i // 4 * HALF + w

        def buffers(k, q_at, klo_at, vaug_at):
            q_hi = [at(f"{k}_q_hi{b}", q_at + 4096 * b, [P, T], F32R) for b in range(2)]
            q_lo = [at(f"{k}_q_lo{b}", q_at + 8192 + 4096 * b, [P, T], F32R) for b in range(2)]
            k_hi = [at(f"{k}_k_hi{b}", q_at + 16384 + 4096 * b, [P, T], F32R) for b in range(2)]
            k_lo = [at(f"{k}_k_lo{b}", klo_at + 4096 * b, [P, T], F32R) for b in range(2)]
            vaug = [at(f"{k}_vaug{b}", vaug_at + 4096 * b, [P, DT, P]) for b in range(2)]
            return q_hi, q_lo, k_hi, k_lo, vaug

        def score_pe(pe, A, n, b, g):
            q_hi, q_lo, k_hi, k_lo, vaug = A.bufs
            half, j, off, d = PIECES[g]
            bank = S_BANK[g % 2]
            out = PS[:, bank, 0:HALF - off]
            t = slice(half * HALF + off, (half + 1) * HALF)
            r = slice(0, A.rows)
            keys = slice(j * P, (j + 1) * P)
            masked = d >= 0
            nc.tensor.matmul(out, k_lo[b][r, keys], q_hi[b][r, t], start=True, stop=False)
            nc.tensor.matmul(out, k_hi[b][r, keys], q_lo[b][r, t], start=False, stop=False)
            last = nc.tensor.matmul(out, k_hi[b][r, keys], q_hi[b][r, t], start=False, stop=not masked)
            if masked:
                extra = d - off
                m = masks[:, A.mask + 1, P - extra:2 * P]
                last = nc.tensor.matmul(PS[:, bank, 0:P + extra], ident_bf[:, :], m, start=False, stop=True)
            last.then_inc(A.s_ready, 1)

        def value_pe(pe, A, n, b, g):
            half, j, off, d = PIECES[g]
            if j == 0 and not (isinstance(n, int) and n == 0):
                pe.wait_ge(A.norm_done, n * 2 + (half - 1))
            pe.wait_ge(A.exp_done, n * N_PIECES + (g + 1))
            nc.tensor.matmul(PS[:, O_BANK[half], off:HALF], A.bufs[4][b][:, j, :], Pt[g % 4][:, 0:HALF - off],
                             start=(j == 0), stop=(g in LAST_OF_HALF)).then_inc(A.pv_done, 1)

        def vtrans_pe(pe, A, n, src):
            pe.wait_ge(A.vT_done, n + 1)
            pe.wait_ge(A.max_done, n * N_MAX + 7)
            for j in range(DT):
                last = nc.tensor.matmul(PS[:, V_BANK, j * HD:(j + 1) * HD], src[0:HD, j * P:(j + 1) * P], ident[0:HD, 0:HD],
                                        start=True, stop=True)
            last.then_inc(A.vt_ready, 1)

        def max_pe(pe, A, n, b, i):
            q_hi, _, k_hi, _, _ = A.bufs
            r = slice(0, A.rows_max)
            bank, reduced = MAX_BANK[i]
            if reduced:
                pe.wait_ge(A.max_done, n * N_MAX + reduced)
            queries = q_hi[b][r, i * P:(i + 1) * P]
            if i >= 4:
                nc.tensor.matmul(PS[:, bank, :], queries, k_hi[b][r, 0:HALF], start=True, stop=True)
            w, c, d = max_width(i)[0], i // 4, i % 4 * P
            nc.tensor.matmul(PS[:, bank + c, 0:w], queries, k_hi[b][r, c * HALF:c * HALF + w], start=True, stop=False)
            nc.tensor.matmul(PS[:, bank + c, d:w], ident_bf[:, :], masks[:, A.mask, 0:w - d], start=False, stop=True)\
                .then_inc(A.mp_ready, 1)

        def max_row_pe(pe, A, n):
            pe.wait_ge(A.mx_done, n + 1)
            nc.tensor.transpose(PS[0:DT, M_BANK, 0:P], mx[:, 0:DT], ident[:, :]).then_inc(A.mT_ready, 1)

        def exp_act(act, A, n, g):
            half, j, off, d = PIECES[g]
            act.wait_ge(A.s_ready, n * N_PIECES + (g + 1))
            act.wait_ge(A.pv_done, n * N_PIECES + (g + 1))
            nc.scalar.activation(Pt[g % 4][:, 0:HALF - off], PS[:, S_BANK[g % 2], 0:HALF - off], ACT.Exp).then_inc(A.exp_done, 1)

        def rough_act(act, A, n, half):
            act.wait_ge(A.pv_done, n * N_PIECES + (LAST_OF_HALF[half] + 1 + 4))
            if half == 1 or not (isinstance(n, int) and n == 0):
                act.wait_ge(A.norm_done, n * 2 + half)
            nc.scalar.activation(ln_sum[0:HD, :], PS[HD:P, O_BANK[half], :], ACT.Ln).then_inc(A.ln_done, 1)
            act.wait_ge(A.ln_done, n * 2 + (half + 1))
            nc.scalar.activation(r0[0:HD, :], ln_sum[0:HD, :], ACT.Exp, scale=-1.0).then_inc(A.r0_done, 1)

        def norm_half_dve(dve, A, n, b, half, tile, gate):
            dve.wait_ge(A.r0_done, n * 2 + (half + 1))
            steps = 3 if gate else 2
            seq = n * (2 * steps) + half * steps
            rows = slice(HD * b, HD * b + HD)
            if half == 1 or not (isinstance(n, int) and n == 0):
                dve.wait_ge(A.newton, seq)
                dve.wait_ge(A.norm_done, n * 2 + half)
            nc.vector.tensor_tensor(newton[0:HD, :], PS[HD:P, O_BANK[half], :], r0[0:HD, :], ALU.mult).then_inc(A.newton, 1)
            dve.wait_ge(A.newton, seq + 1)
            nc.vector.scalar_tensor_tensor(rec[rows, :], newton[0:HD, :], -2.0, r0[0:HD, :], ALU.add, ALU.mult).then_inc(A.newton, 1)
            dve.wait_ge(A.newton, seq + 2)
            dst = flat(mix[rows, bass.ds(tile, 1), half * HALF:(half + 1) * HALF])
            if gate:
                nc.vector.tensor_tensor(rec[rows, :], rec[rows, :], dst, ALU.mult).then_inc(A.newton, 1)
                dve.wait_ge(A.newton, seq + 3)
            nc.vector.scalar_tensor_tensor(dst, PS[0:HD, O_BANK[half], :], -1.0, rec[rows, :], ALU.mult, ALU.mult).then_inc(A.norm_done, 1)

        def max_dve(dve, A, n, i):
            dve.wait_ge(A.mp_ready, n * N_MAX + (i + 1))
            bank = MAX_BANK[i][0]
            nc.vector.reduce_max(mx[:, i:i + 1], flat(PS[:, bank:bank + 2, :])[:, 0:max_width(i)[1]] if i >= 4 else
                                 PS[:, bank, 0:max_width(i)[1]], AX_X).then_inc(A.max_done, 1)

        def negate_dve(dve, A, n):
            dve.wait_ge(A.max_done, (n + 1) * N_MAX)
            nc.vector.tensor_scalar(mx[:, 0:8], mx[:, 0:8], -1.0, None, ALU.mult).then_inc(A.mx_done, 1)

        def vaug_dve(dve, A, n, b):
            dve.wait_ge(A.vt_ready, n + 1)
            nc.vector.tensor_copy(A.bufs[4][b][:, :, 0:HD], PS[:, V_BANK, :].rearrange("p (j e) -> p j e", e=HD)).then_inc(A.vaug_done, 1)

        def max_row_dve(dve, A, n):
            dve.wait_ge(A.mT_ready, n + 1)
            nc.vector.tensor_copy(c_neg[:, :], PS[0:DT, M_BANK, 0:P]).then_inc(A.cneg_done, 1)

        def max_row_act(act, A, n, b, turn):
            act.wait_ge(A.cneg_done, n + 1)
            act.dma_start(A.bufs[0][b][A.rows - 1:A.rows, :].bitcast(F32), c_neg[:, :].bitcast(F32)).then_inc(A.row_in[b], 16)

        fox = Attention("fox", FOX_H, HD + 1, HD + 2, 0)
        fox.bufs = buffers("fox", R_X, R_X + 24576, R_S + 8192)
        fox.f_in = [sem(f"fox_f_in{b}") for b in range(2)]
        fox_vT = at("fox_vT", R_S + 16384, [HD, T])
        mla = Attention("mla", MLA_H, NOPE + ROPE, NOPE + ROPE + 1, 2)
        mla.bufs = buffers("mla", R_H + 40960, R_S + 8192, R_S + 16384)
        mla_vT = at("mla_vT", R_W + 16384, [HD, T])

        def attend_pe(pe, A, n, b, after=()):
            for g in range(N_PIECES):
                value_pe(pe, A, n, b, g)
                if g + 2 < N_PIECES:
                    score_pe(pe, A, n, b, g + 2)
                if after:
                    after(g)

        def step_pe(pe, A, n, b, turn, project_head, vT):
            prev = None if isinstance(n, int) and n == 0 else n - 1

            def first_scores():
                if isinstance(n, int) and n == 1 and A is mla:
                    pe.wait_ge(A.setup, 5)
                if prev is not None:
                    pe.wait_ge(A.row_in[1 - b], 16 * turn if b == 0 else turn * 16 + 16)
                    score_pe(pe, A, prev, 1 - b, 0)
                    score_pe(pe, A, prev, 1 - b, 1)

            def maxima(g):
                if g == min(MAX_AFTER):
                    pe.wait_ge(A.lo_done, (n + 1) * A.n_lo)
                    pe.wait_ge(A.vT_done, n + 1)
                    if A is fox:
                        pe.wait_ge(A.f_in[b], turn * 32 + 32)
                    elif prev is None:
                        pe.wait_ge(A.setup, 4)
                for i in MAX_AFTER.get(g, ()):
                    max_pe(pe, A, n, b, i)
                if g == N_PIECES - 2:
                    vtrans_pe(pe, A, n, vT)
                if g == N_PIECES - 1:
                    max_row_pe(pe, A, n)

            project_head(pe, n, b, first_scores)
            if prev is not None:
                attend_pe(pe, A, prev, 1 - b, maxima)
            else:
                for g in range(N_PIECES):
                    maxima(g)

        def last_pe(pe, A):
            pe.wait_ge(A.row_in[1], 16 * (A.heads // 2))
            for g in range(2):
                score_pe(pe, A, A.heads - 1, 1, g)
            attend_pe(pe, A, A.heads - 1, 1)

        def step_act(act, A, n, b, turn, prepare):
            prev = None if isinstance(n, int) and n == 0 else n - 1
            todo = prepare(act, n, b, turn)
            for g in range(N_PIECES):
                if prev is not None:
                    exp_act(act, A, prev, g)
                if g in todo:
                    todo[g]()
                if g == 6 and prev is not None:
                    rough_act(act, A, prev, 0)
            if prev is not None:
                rough_act(act, A, prev, 1)
            max_row_act(act, A, n, b, turn)

        def last_act(act, A, split=None):
            for g in range(N_PIECES):
                exp_act(act, A, A.heads - 1, g)
                if g == 6:
                    rough_act(act, A, A.heads - 1, 0)
                if split is not None and 4 <= g < 4 + DT - 1:
                    if g == 4:
                        act.wait_ge(A.norm_done, 2 * (A.heads - 2))
                    split(g - 4)
            rough_act(act, A, A.heads - 1, 1)

        def step_dve(dve, A, n, b, turn, prepare, tile0, gate):
            prev = None if isinstance(n, int) and n == 0 else n - 1
            prepare(dve, n, b)
            tile = turn + (tile0 - (b == 0))
            for i in range(N_MAX):
                max_dve(dve, A, n, i)
                if i == 3 and prev is not None:
                    norm_half_dve(dve, A, prev, 1 - b, 0, tile, gate)
            negate_dve(dve, A, n)
            vaug_dve(dve, A, n, b)
            max_row_dve(dve, A, n)
            if prev is not None:
                norm_half_dve(dve, A, prev, 1 - b, 1, tile, gate)
            elif A is mla:
                mla_constants_dve(dve)

        def steps(eng, A, step):
            for b in range(2):
                step(b, b, 0)
            with eng.Fori(1, A.heads // 2) as turn:
                for b in range(2):
                    step(turn * 2 + b, b, turn)

        small_read, f_stored = sem("small_read"), sem("f_stored")
        f_y, f_log, f_sum = sem("f_y"), sem("f_log"), sem("f_sum")
        fv_read = sem("fv_read")
        restA, restB = sem("rest_read_act"), sem("rest_read_dve")
        a_low = at("a_low", R_S + 4096, [16, T])
        FR = slice(32, 32 + FOX_H)
        f_t = [at(f"f_t{i}", R_X + 4096 * i, [P, T]) for i in range(4)]
        f_hi = at("f_hi", R_X + 16384, [P, T], F32R)
        f_lo = at("f_lo", R_X + 20480, [P, T], F32R)
        f_one = at("f_one", R_X + 24576, [P, T])
        z8 = at("z8", R_X, [P, 8, T])
        zg = at("zg", R_S + 8192, [P, 2, T])
        bcum = at("bcum", R_H, [P, 2, T])
        q_in = at("q_in", R_H + 8192, [P, 2, T])
        k_in = at("k_in", R_H + 16384, [P, 2, T])
        gt = [at(f"gla_t{i}", R_H + 24576 + 8192 * i, [P, 2, T]) for i in range(5)]
        kd_tok = at("kd_tok", R_H + 24576, [P, DT, 2, P])
        attm = at("attm", R_H + 32768, [P, 4, DT, P])
        S_all = at("S_all", R_H + 49152, [P, 2, NCH, P])
        v_tok = at("v_tok", R_S + 16384, [P, DT, 2, P])
        gla_o = at("gla_o", R_H, [P, 2, T])
        gla_sq = at("gla_sq", R_H + 8192, [P, 2, T])
        gla_ln = at("gla_ln", R_H + 16384, [P, 2, T])
        gla_y = at("gla_y", R_H + 24576, [P, 2, T])
        gla_n = at("gla_n", R_H + 32768, [P, 2, T])
        dec = at("dec", R_S + 24576, [P, 2 * NCH])
        s2 = at("pool_s2", R_W, [P, 2, T])
        s4 = at("pool_s4", R_W + 8192, [P, 2, T])
        s8 = at("pool_s8", R_W + 16384, [P, T])
        pool_step, pool_d, pool_mm = sem("pool_step"), sem("pool_d"), sem("pool_mm")
        pool_out = sem("pool_out")
        g_vt, g_vtok, g_gate, g_act, g_dve = sem("g_vt"), sem("g_vtok"), sem("g_gate"), sem("g_act"), sem("g_dve")
        g_kt, g_ktok, g_att, g_attm, g_kv, g_S = sem("g_kt"), sem("g_ktok"), sem("g_att"), sem("g_attm"), sem("g_kv"), sem("g_S")
        g_mm, g_o1, g_o, g_ms = sem("g_mm"), sem("g_o1"), sem("g_o"), sem("g_ms")
        g_zero = sem("g_zero")
        m_hi, m_lo = sem("mix_hi"), sem("mix_lo")
        wo_added = sem("wo_added")

        def psflat(a, n):
            return flat(PS[:, a:a + n, :])

        def small_dve(dve):
            dve.wait_ge(unit_done, U_SMALL + 3)
            nc.vector.tensor_copy(a_low[:, :], flat(pjA)[0:16, :]).then_inc(small_read, 1)
            bf = vec[FR, V_BF:V_BF + 1]
            nc.vector.tensor_scalar(f_t[0][FR, :], flat(pjA)[FR, :], bf, 0.0, ALU.add, ALU.min).then_inc(f_y, 1)
            nc.vector.memset(f_one[FR, :], 1.0).then_inc(f_y, 1)
            dve.wait_ge(f_log, 3)
            dve.wait_ge(f_y, 2)
            nc.vector.tensor_tensor(f_t[0][FR, :], f_t[2][FR, :], f_t[0][FR, :], ALU.subtract).then_inc(f_sum, 1)
            dve.wait_ge(f_sum, 1)
            nc.vector.tensor_tensor_scan(f_t[1][FR, :], f_one[FR, :], f_t[0][FR, :], 0.0, ALU.mult, ALU.add).then_inc(f_sum, 1)
            dve.wait_ge(f_sum, 2)
            nc.vector.tensor_copy(f_hi[FR, :], f_t[1][FR, :]).then_inc(f_sum, 1)
            dve.wait_ge(f_sum, 3)
            nc.vector.tensor_tensor(f_lo[FR, :], f_t[1][FR, :], f_hi[FR, :].bitcast(F32), ALU.subtract).then_inc(f_sum, 1)

        def small_act(act):
            act.wait_ge(unit_done, U_SMALL + 3)
            bf = vec[FR, V_BF:V_BF + 1]
            act.wait_ge(f_y, 1)
            nc.scalar.activation(f_t[1][FR, :], flat(pjA)[FR, :], ACT.Abs, bias=bf).then_inc(f_log, 1)
            act.wait_ge(f_log, 1)
            nc.scalar.activation(f_t[2][FR, :], f_t[1][FR, :], ACT.Exp, scale=-1.0).then_inc(f_log, 1)
            act.wait_ge(f_log, 2)
            nc.scalar.activation(f_t[2][FR, :], f_t[2][FR, :], ACT.Ln, bias=one[FR, :]).then_inc(f_log, 1)
            act.wait_ge(f_sum, 4)
            act.dma_start(f_rows[0, :, :], f_hi[FR, :].bitcast(F32)).then_inc(f_stored, 16)
            act.dma_start(f_rows[1, :, :], f_lo[FR, :].bitcast(F32)).then_inc(f_stored, 16)

        one = small_const[:, K_EPS - K_CNT + 1:K_EPS - K_CNT + 2]

        def fox_values_pe(pe):
            pe.wait_ge(f_y, 1)
            pe.wait_ge(f_log, 1)
            for i in range(1, FOX_H // 2):
                pe.wait_ge(w_split, U_FV + i + 3)
                if i >= 2:
                    pe.wait_ge(fv_read, i - 1)
                project(pe, (U_FV + i) % 2, range(DT), h_hi, h_lo, (pjB, pjA)[i % 2])

        def fox_values_act(act):
            with act.Fori(0, FOX_H // 4) as it:
                for j, src in enumerate((pjB, pjA)):
                    act.wait_ge(unit_done, it * 2 + (U_FV + j + 3))
                    nc.scalar.activation(flat(mix[:, bass.ds(it * 2 + j, 1), :]), flat(src), ACT.Copy).then_inc(fv_read, 1)

        def fox_project(pe, n, b, first_scores):
            pe.wait_ge(w_split, n + (U_FQK + 3))
            project(pe, (U_FQK + b) % 2, range(DT), h_hi, h_lo, pjA, done=False, halves=(0,))
            first_scores()
            project(pe, (U_FQK + b) % 2, range(DT), h_hi, h_lo, pjA, halves=(1,))

        def fox_prepare_act(act, n, b, turn):
            q_hi, q_lo, k_hi, k_lo, vaug = fox.bufs
            src = flat(pjA)
            if isinstance(n, int) and n == 0:
                act.wait_ge(fox.setup, 1)
                act.wait_ge(f_stored, 32)
            else:
                act.wait_ge(fox.vt_ready, n)
            for part, row in ((0, k_hi[b]), (1, k_lo[b])):
                act.dma_start(row[HD:HD + 1, :].bitcast(F32), f_rows[part, bass.ds(n, 1), :]).then_inc(fox.f_in[b], 16)

            def split():
                act.wait_ge(unit_done, n + (U_FQK + 3))
                nc.scalar.activation(q_hi[b][0:HD, :], src[0:HD, :], ACT.Copy, scale=HD ** -0.5).then_inc(fox.hi_done, 1)
                nc.scalar.activation(k_hi[b][0:HD, :], src[HD:P, :], ACT.Copy).then_inc(fox.hi_done, 1)

            def values():
                nc.scalar.activation(fox_vT[:, :], flat(mix[HD * b:HD * b + HD, bass.ds(turn, 1), :]), ACT.Copy).then_inc(fox.vT_done, 1)
            return {1: split, 2: values}

        def fox_prepare_dve(dve, n, b):
            q_hi, q_lo, k_hi, k_lo, vaug = fox.bufs
            src = flat(pjA)
            dve.wait_ge(fox.hi_done, n * 2 + 1)
            nc.vector.scalar_tensor_tensor(q_lo[b][0:HD, :], src[0:HD, :], HD ** -0.5, q_hi[b][0:HD, :].bitcast(F32),
                                           ALU.mult, ALU.subtract).then_inc(fox.lo_done, 1)
            dve.wait_ge(fox.hi_done, n * 2 + 2)
            nc.vector.tensor_tensor(k_lo[b][0:HD, :], src[HD:P, :], k_hi[b][0:HD, :].bitcast(F32), ALU.subtract)\
                .then_inc(fox.lo_done, 1)

        def fox_setup_dve(dve):
            dve.wait_ge(f_stored, 32)
            q_hi, q_lo, k_hi, k_lo, vaug = fox.bufs
            for b in range(2):
                nc.vector.memset(q_hi[b][HD:HD + 2, :].bitcast(F32), 1.0)
                nc.vector.memset(q_lo[b][HD:HD + 2, :].bitcast(F32), 0.0)
                nc.vector.memset(k_hi[b][HD:HD + 2, :].bitcast(F32), 1.0)
                nc.vector.memset(k_lo[b][HD:HD + 2, :].bitcast(F32), 0.0)
                last = nc.vector.memset(vaug[b][:, :, HD:P], 1.0)
            last.then_inc(fox.setup, 1)

        fox.n_lo = 2

        def rest_pe(pe):
            units_pe(pe, U_REST, N_REST, range(DT), h_hi, h_lo,
                     lambda it, j: pe.wait_ge((restA, restB)[j], it + 1))

        def rest_act(act):
            with act.Fori(0, 4) as it:
                act.wait_ge(unit_done, it * 2 + (U_REST + 3))
                nc.scalar.activation(flat(z8[:, bass.ds(it * 2, 1), :]), flat(pjA), ACT.Copy).then_inc(restA, 1)
            act.wait_ge(unit_done, U_REST + 8 + 3)
            nc.scalar.activation(zg[:, 0, :], flat(pjA), ACT.Copy).then_inc(restA, 1)

        def rest_dve(dve):
            with dve.Fori(0, 4) as it:
                dve.wait_ge(unit_done, it * 2 + (U_REST + 4))
                nc.vector.tensor_copy(flat(z8[:, bass.ds(it * 2 + 1, 1), :]), flat(pjB)).then_inc(restB, 1)
            dve.wait_ge(unit_done, U_REST + 9 + 3)
            nc.vector.tensor_copy(zg[:, 1, :], flat(pjB)).then_inc(restB, 1)

        def pool_dve(dve):
            dve.wait_ge(restA, N_REST // 2 + 1)
            dve.wait_ge(restB, N_REST // 2 + 1)
            count = [0]

            def shifted(dst, src, w):
                nc.vector.tensor_copy(dst[:, :, 0:w], src[:, :, 0:w])
                nc.vector.tensor_tensor(dst[:, :, w:T], src[:, :, w:T], src[:, :, 0:T - w], ALU.add).then_inc(pool_step, 1)
                count[0] += 1
                dve.wait_ge(pool_step, count[0])
            u = z8[:, 0:2, :]
            shifted(s2, u, 1)
            shifted(s4, s2, 2)
            s8_ = s8[:, :].rearrange("p (a n) -> p a n", a=1)
            shifted(s8_, s4[:, 1:2, :], 4)
            shifted(s2[:, 1:2, :], s8_, 8)
            cnt = small_const[:, 0:32].rearrange("p (c n) -> p c n", c=2)
            for c, r, src, w in ((0, 0, s2[:, 0, :], 2), (0, HD, s4[:, 0, :], 4), (1, 0, s8[:, :], 8), (1, HD, s2[:, 1, :], 16)):
                rows = slice(r, r + HD)
                nc.vector.tensor_tensor(src[rows, 0:16], src[rows, 0:16], cnt[rows, c, :], ALU.mult).then_inc(pool_step, 1)
                count[0] += 1
                nc.vector.scalar_tensor_tensor(z8[rows, c, 16:T], src[rows, 16:T], 1.0 / w, z8[rows, c, 16:T],
                                               ALU.mult, ALU.subtract)
                dve.wait_ge(pool_step, count[0])
                last = nc.vector.tensor_tensor(z8[rows, c, 0:16], src[rows, 0:16], z8[rows, c, 0:16], ALU.subtract)
            last.then_inc(pool_d, 1)

        def pool_pe(pe):
            pe.wait_ge(pool_d, 1)
            pe.wait_ge(g_act, 2)
            pe.wait_ge(g_dve, 2)
            for c, dst in enumerate((pjA, pjB)):
                for half in range(2):
                    last = nc.tensor.matmul(dst[:, half, :], vec[:, V_WPOOL + P * c:V_WPOOL + P * c + P],
                                            z8[:, c, half * HALF:(half + 1) * HALF], start=True, stop=True)
            last.then_inc(pool_mm, 1)

        def pool_act(act):
            act.wait_ge(pool_mm, 1)
            for c, src in enumerate((pjA, pjB)):
                nc.scalar.activation(mix[:, c, :], flat(src), ACT.Copy, scale=vec[:, V_PS + c:V_PS + c + 1]).then_inc(pool_out, 1)

        def by_chunk(ap):
            return ap.rearrange("p c (n t) -> p (c n) t", t=CHUNK)

        def chunk_col(col):
            return by_chunk(bcum[:, :, :])[:, :, col:col + 1].to_broadcast([P, 2 * NCH, CHUNK])

        def kv_place(c, n):
            return (4 if c == 0 else 0) + n % 2 * 2 + n // 8, n // 2 % 4 * P

        def tau(t):
            return flat(t[:, :, :])

        def gla_pe(pe):
            pe.wait_ge(restA, N_REST // 2 + 1)
            pe.wait_ge(restB, N_REST // 2 + 1)
            for blk in range(DT):
                for c in range(2):
                    last = nc.tensor.transpose(PS[:, 4 + blk // 2, (blk % 2 * 2 + c) * P:(blk % 2 * 2 + c + 1) * P],
                                               z8[:, 6 + c, blk * P:(blk + 1) * P], ident[:, :])
            last.then_inc(g_vt, 1)
            for c, dst in enumerate((pjA, pjB)):
                for half in range(2):
                    last = nc.tensor.matmul(dst[:, half, :], vec[0:16, V_WAUP + P * c:V_WAUP + P * c + P],
                                            a_low[:, half * HALF:(half + 1) * HALF], start=True, stop=True)
            last.then_inc(g_gate, 1)
            pool_pe(pe)
            pe.wait_ge(pool_out, 2)
            pe.wait_ge(g_dve, 8)
            for batch in range(2):
                if batch:
                    pe.wait_ge(g_attm, 1)
                for hh in range(2):
                    hd = batch * 2 + hh
                    rows = slice(HD * hh, HD * hh + HD)
                    for pr in range(DT):
                        s = slice(pr * P, (pr + 1) * P)
                        last = nc.tensor.matmul(PS[:, hh * 2 + pr // 4, pr % 4 * P:(pr % 4 + 1) * P], k_in[rows, batch, s],
                                                q_in[rows, batch, s], start=True, stop=True)
                last.then_inc(g_att, 1)
                if batch == 0:
                    pe.wait_ge(g_dve, 10)
                    pe.wait_ge(g_vtok, 1)
                    for blk in range(DT):
                        for c in range(2):
                            last = nc.tensor.transpose(PS[:, 4 + blk // 2, (blk % 2 * 2 + c) * P:(blk % 2 * 2 + c + 1) * P],
                                                       z8[:, 4 + c, blk * P:(blk + 1) * P], ident[:, :])
                    last.then_inc(g_kt, 1)
            pe.wait_ge(g_ktok, 1)
            for c in range(2):
                if c:
                    pe.wait_ge(g_attm, 2)
                for n in range(NCH - 1):
                    rows = slice(n % 2 * CHUNK, n % 2 * CHUNK + CHUNK)
                    bank, col = kv_place(c, n)
                    last = nc.tensor.matmul(PS[:, bank, col:col + P], kd_tok[rows, n // 2, c, :],
                                            v_tok[rows, n // 2, c, :], start=True, stop=True)
                last.then_inc(g_kv, 1)
            pe.wait_ge(g_S, 4 * (NCH - 1))
            for c, dst in enumerate((pjA, pjB)):
                for n in range(NCH):
                    last = nc.tensor.matmul(dst[:, n // 8, n % 8 * CHUNK:(n % 8 + 1) * CHUNK], S_all[:, c, n, :],
                                            z8[:, 2 + c, n * CHUNK:(n + 1) * CHUNK], start=True, stop=True)
            for hd in range(4):
                rows = slice(HD * (hd % 2), HD * (hd % 2) + HD)
                for pr in range(DT):
                    last = nc.tensor.matmul(PS[rows, 4 + hd // 2 * 2 + pr // 4, pr % 4 * P:(pr % 4 + 1) * P],
                                            v_tok[:, pr, hd // 2, HD * (hd % 2):HD * (hd % 2) + HD], attm[:, hd, pr, :],
                                            start=True, stop=True)
            last.then_inc(g_mm, 1)
            pe.wait_ge(g_act, 11)
            pe.wait_ge(g_o1, 1)
            for c in range(2):
                for half in range(2):
                    last = nc.tensor.matmul(PS[:, 2 * c + half, :], head_mean[:, :], gla_sq[:, c, half * HALF:(half + 1) * HALF],
                                            start=True, stop=True)
            last.then_inc(g_ms, 1)

        def gla_act(act):
            act.wait_ge(g_vt, 1)
            nc.scalar.activation(v_tok[:, :, :, :].rearrange("p a c n -> p (a c n)"), psflat(4, 4), ACT.Copy).then_inc(g_vtok, 1)
            act.wait_ge(g_gate, 1)
            for c, src in enumerate((pjA, pjB)):
                act.wait_ge(g_dve, c + 1)
                nc.scalar.activation(gt[1][:, c, :], flat(src), ACT.Abs, bias=vec[:, V_BA + c:V_BA + c + 1]).then_inc(g_act, 1)
            act.wait_ge(g_act, 2)
            nc.scalar.activation(tau(gt[2]), tau(gt[1]), ACT.Exp, scale=-1.0).then_inc(g_act, 1)
            act.wait_ge(g_act, 3)
            nc.scalar.activation(tau(gt[1]), tau(gt[2]), ACT.Ln, bias=one).then_inc(g_act, 1)
            pool_act(act)
            act.wait_ge(g_dve, 5)
            nc.scalar.activation(tau(gt[1]), tau(gt[0]), ACT.Exp, scale=1.0 / GLA_TAU).then_inc(g_act, 1)
            nc.scalar.activation(tau(gt[2]), tau(gt[0]), ACT.Exp, scale=-1.0 / GLA_TAU).then_inc(g_act, 1)
            nc.scalar.activation(tau(gt[3]), tau(bcum), ACT.Exp, scale=1.0 / GLA_TAU).then_inc(g_act, 1)
            act.wait_ge(g_dve, 6)
            nc.scalar.activation(tau(gt[4]), tau(gt[0]), ACT.Exp, scale=1.0 / GLA_TAU).then_inc(g_act, 1)
            nc.scalar.activation(dec[:, :], by_chunk(bcum[:, :, :])[:, :, CHUNK - 1], ACT.Exp, scale=1.0 / GLA_TAU).then_inc(g_act, 1)
            act.wait_ge(g_kt, 1)
            nc.scalar.activation(kd_tok[:, :, :, :].rearrange("p a c n -> p (a c n)"), psflat(4, 4), ACT.Copy).then_inc(g_ktok, 1)
            act.wait_ge(g_mm, 1)
            nc.scalar.activation(tau(gla_o), psflat(0, 4), ACT.Copy).then_inc(g_o1, 1)
            nc.scalar.activation(tau(zg), tau(zg), ACT.Silu).then_inc(g_act, 1)
            act.wait_ge(g_o, 1)
            nc.scalar.activation(tau(gla_sq), tau(gla_o), ACT.Square).then_inc(g_act, 1)
            act.wait_ge(g_ms, 1)
            nc.scalar.activation(tau(gla_ln), psflat(0, 4), ACT.Ln, bias=eps).then_inc(g_act, 1)
            act.wait_ge(g_act, 12)
            nc.scalar.activation(tau(gla_y), tau(gla_ln), ACT.Exp, scale=-0.5).then_inc(g_act, 1)

        def gla_dve(dve):
            dve.wait_ge(g_gate, 1)
            for c, src in enumerate((pjA, pjB)):
                nc.vector.tensor_scalar(gt[0][:, c, :], flat(src), vec[:, V_BA + c:V_BA + c + 1], 0.0, ALU.add, ALU.min).then_inc(g_dve, 1)
            nc.vector.memset(tau(gt[4]), 1.0).then_inc(g_zero, 1)
            dve.wait_ge(g_zero, 1)
            nc.vector.memset(by_chunk(gt[4][:, :, :])[:, :, 0:1], 0.0).then_inc(g_zero, 1)
            dve.wait_ge(g_act, 4)
            dve.wait_ge(g_dve, 2)
            nc.vector.tensor_tensor(tau(gt[3]), tau(gt[0]), tau(gt[1]), ALU.subtract).then_inc(g_dve, 1)
            dve.wait_ge(g_dve, 3)
            dve.wait_ge(g_zero, 2)
            nc.vector.tensor_tensor_scan(tau(bcum), tau(gt[4]), tau(gt[3]), 0.0, ALU.mult, ALU.add).then_inc(g_dve, 1)
            dve.wait_ge(g_dve, 4)
            nc.vector.tensor_tensor(by_chunk(gt[0][:, :, :]), by_chunk(bcum[:, :, :]), chunk_col(CHUNK // 2 - 1), ALU.subtract).then_inc(g_dve, 1)
            dve.wait_ge(g_act, 6)
            nc.vector.tensor_tensor(by_chunk(gt[0][:, :, :]), chunk_col(CHUNK - 1), by_chunk(bcum[:, :, :]), ALU.subtract).then_inc(g_dve, 1)
            gq, gk = flat(z8[:, 2:4, :]), flat(z8[:, 4:6, :])
            nc.vector.scalar_tensor_tensor(tau(q_in), gq, HD ** -0.5, tau(gt[1]), ALU.mult, ALU.mult).then_inc(g_dve, 1)
            nc.vector.tensor_tensor(tau(k_in), gk, tau(gt[2]), ALU.mult).then_inc(g_dve, 1)
            dve.wait_ge(g_act, 7)
            dve.wait_ge(g_dve, 8)
            nc.vector.scalar_tensor_tensor(gq, gq, HD ** -0.5, tau(gt[3]), ALU.mult, ALU.mult).then_inc(g_dve, 1)
            dve.wait_ge(g_act, 8)
            nc.vector.tensor_tensor(gk, gk, tau(gt[4]), ALU.mult).then_inc(g_dve, 1)
            dve.wait_ge(g_dve, 10)
            nc.vector.memset(attm[:, :, :, :].rearrange("p h a n -> p (h a n)"), 0.0).then_inc(g_zero, 1)
            nc.vector.memset(S_all[:, :, :, :].rearrange("p c a n -> p (c a n)"), 0.0).then_inc(g_zero, 1)
            dve.wait_ge(g_zero, 4)
            m = att_mask[:, :].rearrange("p (o n) -> p o n", o=1).to_broadcast([P, 4, P])
            for batch in range(2):
                dve.wait_ge(g_att, batch + 1)
                for bank in range(4):
                    hd, a = batch * 2 + bank // 2, bank % 2 * 4
                    last = nc.vector.copy_predicated(attm[:, hd, a:a + 4, :], m, PS[:, bank, :].rearrange("p (a n) -> p a n", n=P))
                last.then_inc(g_attm, 1)
            dve.wait_ge(g_act, 9)
            dve.wait_ge(g_kv, 2)
            done = 0
            for n in range(NCH - 1):
                for c in range(2):
                    for a in range(2):
                        r = slice(HD * a, HD * a + HD)
                        bank, col = kv_place(c, n)
                        kv = PS[r, bank, col + HD * a:col + HD * a + HD]
                        if n:
                            dve.wait_ge(g_S, done - 3)
                        nc.vector.scalar_tensor_tensor(S_all[r, c, n + 1, r], S_all[r, c, n, r], dec[r, c * NCH + n:c * NCH + n + 1],
                                                       kv, ALU.mult, ALU.add).then_inc(g_S, 1)
                        done += 1
            dve.wait_ge(g_o1, 1)
            nc.vector.tensor_tensor(tau(gla_o), psflat(4, 4), tau(gla_o), ALU.add).then_inc(g_o, 1)
            dve.wait_ge(g_act, 13)
            nc.vector.tensor_tensor(tau(gla_n), tau(gla_y), tau(gla_y), ALU.mult).then_inc(g_o, 1)
            dve.wait_ge(g_o, 2)
            nc.vector.scalar_tensor_tensor(tau(gla_n), psflat(0, 4), EPS, tau(gla_n), ALU.add, ALU.mult).then_inc(g_o, 1)
            dve.wait_ge(g_o, 3)
            nc.vector.tensor_scalar(tau(gla_n), tau(gla_n), -0.5, 1.5, ALU.mult, ALU.add).then_inc(g_o, 1)
            dve.wait_ge(g_o, 4)
            nc.vector.tensor_tensor(tau(gla_y), tau(gla_y), tau(gla_n), ALU.mult).then_inc(g_o, 1)
            dve.wait_ge(g_o, 5)
            for c in range(2):
                nc.vector.scalar_tensor_tensor(gla_o[:, c, :], gla_o[:, c, :], vec[:, V_GN + c:V_GN + c + 1], gla_y[:, c, :],
                                               ALU.mult, ALU.mult).then_inc(g_o, 1)
            dve.wait_ge(g_o, 7)
            nc.vector.tensor_tensor(flat(mix[:, 2:4, :]), tau(gla_o), tau(zg), ALU.mult).then_inc(g_o, 1)

        MIX_ORDER = (4, 5, 6, 7, 0, 1, 2, 3)

        def mix_hi_act(k, hi_done):
            nc.scalar.activation(hi_tile(k), mix[:, k, :], ACT.Copy).then_inc(hi_done, 1)

        def mix_lo_dve(dve, k, i, hi_done, lo_done):
            dve.wait_ge(hi_done, i + 1)
            nc.vector.tensor_tensor(mix_lo[:, k, :], mix[:, k, :], hi_tile(k).bitcast(F32), ALU.subtract).then_inc(lo_done, 1)

        gate_read, up_read, a_split_hi = sem("gate_read"), sem("up_read"), sem("a_split_hi")
        a_split_lo, dn_added = sem("a_split_lo"), sem("dn_added")
        a_hi = at("a_hi", R_M + 8192, [P, 6, T], F32R)
        a_lo = at("a_lo", R_M - 16384, [P, 6, T], F32R)
        F0 = [sum(MLP_CHUNKS[:c]) for c in range(len(MLP_CHUNKS))]

        def mlp_pe(pe):
            for c, fc in enumerate(MLP_CHUNKS):
                if c:
                    pe.wait_ge(dn_added, DT * c + 2)
                if c == 0:
                    project_tiles(pe, ((U_GU[c], pjA), (U_GU[c] + 1, pjB)), range(DT), h_hi, h_lo,
                                  lambda i: N2.wait(pe, "lo", i + 1))
                with pe.Fori(c == 0, fc) as f:
                    for j, (dst, free) in enumerate(((pjA, gate_read), (pjB, up_read))):
                        pe.wait_ge(w_split, f * 2 + (U_GU[c] + j + 3))
                        pe.wait_ge(free, f + (F0[c] + 1))
                        project(pe, (U_GU[c] + j) % 2, range(DT), h_hi, h_lo, dst)

                def arrived(i, c=c, fc=fc):
                    if i == 0:
                        pe.wait_ge(gate_read, F0[c] + fc + 1)
                    pe.wait_ge(a_split_lo, F0[c] + i + 2)
                project_tiles(pe, ((U_DN[c], pjA),), range(fc), a_hi, a_lo, arrived)
                pe.wait_ge(w_split, U_DN[c] + 1 + 3)
                project(pe, (U_DN[c] + 1) % 2, range(fc), a_hi, a_lo, pjB)
                units_pe(pe, U_DN[c] + 2, DT - 2, range(fc), a_hi, a_lo,
                         lambda it, j, c=c: pe.wait_ge(dn_added, it * 2 + (DT * c + j + 3)))

        def mlp_act(act):
            for c, fc in enumerate(MLP_CHUNKS):
                with act.Fori(0, fc) as f:
                    act.wait_ge(unit_done, f * 2 + (U_GU[c] + 3))
                    act.wait_ge(up_read, f + (F0[c] + 1))
                    nc.scalar.activation(tmp[0][:, :], flat(pjA), ACT.Silu).then_inc(gate_read, 1)
                    act.wait_ge(up_read, f + (F0[c] + 2))
                    nc.scalar.activation(flat(a_hi[:, bass.ds(f, 1), :]), tmp[1][:, :], ACT.Copy).then_inc(a_split_hi, 1)
                if c == len(MLP_CHUNKS) - 1:
                    two_squares_act(act, DT * c)

        def mlp_dve(dve):
            for c, fc in enumerate(MLP_CHUNKS):
                with dve.Fori(0, fc) as f:
                    dve.wait_ge(unit_done, f * 2 + (U_GU[c] + 4))
                    dve.wait_ge(gate_read, f + (F0[c] + 2))
                    dve.wait_ge(a_split_lo, f + (F0[c] + 1))
                    nc.vector.tensor_tensor(tmp[1][:, :], flat(pjB), tmp[0][:, :], ALU.mult).then_inc(up_read, 1)
                    dve.wait_ge(a_split_hi, f + (F0[c] + 1))
                    nc.vector.tensor_tensor(flat(a_lo[:, bass.ds(f, 1), :]), tmp[1][:, :],
                                            flat(a_hi[:, bass.ds(f, 1), :]).bitcast(F32), ALU.subtract).then_inc(a_split_lo, 1)
                if c < len(MLP_CHUNKS) - 1:
                    residual_dve(dve, U_DN[c], dn_added, DT * c)
                else:
                    two_squares_dve(dve, U_DN[c], DT * c)

        sq2, ssq2, diag2 = tmp[0], tmp[1], sq
        gain3 = const("gain3", [P, DT])

        def two_squares_act(act, added0):
            for k in range(DT):
                act.wait_ge(dn_added, added0 + k + 3)
                nc.scalar.activation(sq[:, :], x[:, k, :], ACT.Square).then_inc(N3["sq"], 1)
                nc.scalar.activation(sq2[:, :], x[:, k, :], ACT.Square, scale=vec[:, V_LNF + k:V_LNF + k + 1]).then_inc(N3["sq"], 1)

        def two_squares_dve(dve, first, added0):
            dve.wait_ge(a_split_lo, FT + 1)
            nc.vector.memset(ssq[:, :], 0.0).then_inc(N3["ssq"], 1)
            nc.vector.memset(ssq2[:, :], 0.0).then_inc(N3["ssq"], 1)
            for k in range(DT):
                dve.wait_ge(unit_done, first + k + 3)
                nc.vector.tensor_tensor(x[:, k, :], flat((pjA, pjB)[k % 2]), x[:, k, :], ALU.add).then_inc(dn_added, 1)
                for i, (total, part) in enumerate(((ssq, sq), (ssq2, sq2))):
                    N3.wait(dve, "sq", 2 * k + i + 1)
                    N3.wait(dve, "ssq", 2 * k + i + 1)
                    nc.vector.tensor_tensor(total[:, :], total[:, :], part[:, :], ALU.add).then_inc(N3["ssq"], 1)

        def two_norms_pe(pe):
            norm_sum_pe(pe, N3, 2 * DT + 2, ssq)
            norm_sum_pe(pe, N3, 2 * DT + 2, ssq2, DT).then_inc(N3["ms"], 1)
            norm_spread_pe(pe, N3, diag, 4)
            norm_spread_pe(pe, N3, diag2, 6).then_inc(N3["bc"], 1)

        def two_norms_act(act):
            N3.wait(act, "ms", 1)
            nc.scalar.activation(rt[:, 0:DT], PS[:, 7, 0:DT], ACT.Sqrt, bias=eps, scale=1.0 / D).then_inc(N3["rt"], 1)
            N3.wait(act, "rv", 3)
            nc.scalar.activation(rt[:, DT:2 * DT], rv[:, DT:2 * DT], ACT.Sqrt, bias=eps, scale=1.0 / D).then_inc(N3["rt"], 1)

        def two_norms_dve(dve):
            r1, s2_, r2, r12 = (rv[:, i * DT:(i + 1) * DT] for i in range(4))
            nc.vector.tensor_tensor(gain3[:, :], vec[:, V_LNF:V_LNF + DT], vec[:, V_NG:V_NG + DT], ALU.mult)
            N3.wait(dve, "rt", 1)
            nc.vector.reciprocal(r1, rt[:, 0:DT]).then_inc(N3["rv"], 1)
            N3.wait(dve, "rv", 1)
            nc.vector.tensor_tensor(s2_, PS[:, 7, DT:2 * DT], r1, ALU.mult).then_inc(N3["rv"], 1)
            N3.wait(dve, "rv", 2)
            nc.vector.tensor_tensor(s2_, s2_, r1, ALU.mult).then_inc(N3["rv"], 1)
            diagonal(diag2, 0)
            N3.wait(dve, "rt", 2)
            nc.vector.reciprocal(r2, rt[:, DT:2 * DT]).then_inc(N3["rv"], 1)
            N3.wait(dve, "rv", 4)
            nc.vector.tensor_tensor(r12, r1, r2, ALU.mult).then_inc(N3["rv"], 1)
            N3.wait(dve, "rv", 5)
            diagonal(diag, 3 * DT).then_inc(N3["diag"], 1)
            N3.wait(dve, "bc", 1)
            norm_split_dve(dve, N3, DT, lambda k: x[:, k, :], lambda k: gain3[:, k:k + 1], hi_tile, lo_tile)
            for k in range(DT):
                nc.vector.scalar_tensor_tensor(x[:, k, :], x[:, k, :], vec[:, V_LNF + k:V_LNF + k + 1], flat(PS[:, 6:8, :]),
                                               ALU.mult, ALU.mult).then_inc(N3["h"], 1)

        u5 = at("u5", R_S + 8192, [P, 5, T])
        k_rope = at("k_rope", R_S + 4096, [P, T])
        cq_hi, cq_lo = at("cq_hi", R_H, [P, 3, T], F32R), at("cq_lo", R_H + 12288, [P, 3, T], F32R)
        ckv_hi, ckv_lo = at("ckv_hi", R_H + 24576, [P, 2, T], F32R), at("ckv_lo", R_H + 32768, [P, 2, T], F32R)
        min_read, kr_step, z_read = sem("min_read"), sem("kr_step"), sem("z_read")
        CR, SR = slice(64, 96), slice(96, 128)

        def mla_in_pe(pe):
            project_tiles(pe, ((U_MIN, pjA), (U_MIN + 1, pjB)), range(DT), h_hi, h_lo, lambda i: N3.wait(pe, "lo", i + 1))
            for i in range(2, 6):
                pe.wait_ge(w_split, U_MIN + i + 3)
                pe.wait_ge(min_read, i - 1)
                if i == 5:
                    N3.wait(pe, "h", 2 * DT)
                    norm_sum_pe(pe, NQ, 3, ssq).then_inc(NQ["ms"], 1)
                project(pe, (U_MIN + i) % 2, range(DT), h_hi, h_lo, (pjA, pjB)[i % 2])

            def spread_q():
                norm_spread_pe(pe, NQ, diag, 4).then_inc(NQ["bc"], 1)

            def sum_kv():
                norm_sum_pe(pe, NKV, 2, ssq, DT).then_inc(NKV["ms"], 1)

            def spread_kv():
                NQ.wait(pe, "h", 3)
                norm_spread_pe(pe, NKV, diag, 4).then_inc(NKV["bc"], 1)
            between = {1: spread_q, 3: sum_kv, 5: spread_kv}
            for i in range(DT):
                pe.wait_ge(w_split, U_Z + i + 3)
                if i == 0:
                    pe.wait_ge(min_read, 5)
                elif i == 1:
                    pe.wait_ge(kr_step, 2)
                else:
                    pe.wait_ge(z_read, i - 1)
                project(pe, (U_Z + i) % 2, range(DT), h_hi, h_lo, (pjA, pjB)[i % 2])
                if i in between:
                    between[i]()

        def mla_in_dve(dve):
            def add_squares(s, i):
                s.wait(dve, "sq", i + 1)
                if i == 0:
                    nc.vector.tensor_copy(ssq[:, :], sq[:, :]).then_inc(s["ssq"], 1)
                else:
                    s.wait(dve, "ssq", i)
                    nc.vector.tensor_tensor(ssq[:, :], ssq[:, :], sq[:, :], ALU.add).then_inc(s["ssq"], 1)
            for i in range(5):
                dve.wait_ge(unit_done, U_MIN + i + 3)
                nc.vector.tensor_copy(u5[:, i, :], flat((pjA, pjB)[i % 2])).then_inc(min_read, 1)
                if i < 3:
                    add_squares(NQ, i)
            dve.wait_ge(unit_done, U_MIN + 5 + 3)
            ps = flat(pjB)
            nc.vector.scalar_tensor_tensor(tmp[0][CR, :], ps[CR, :], MLA_SCALE, cos_sin[CR, :], ALU.mult, ALU.mult).then_inc(kr_step, 1)
            nc.vector.scalar_tensor_tensor(tmp[1][CR, :], ps[SR, :], MLA_SCALE, cos_sin[SR, :], ALU.mult, ALU.mult).then_inc(kr_step, 1)
            dve.wait_ge(kr_step, 2)
            nc.vector.tensor_tensor(k_rope[CR, :], tmp[0][CR, :], tmp[1][CR, :], ALU.add).then_inc(kr_step, 1)
            norm_diag(dve, NQ)
            NQ.wait(dve, "ms", 1)
            for i in range(2):
                add_squares(NKV, i)
            NQ.wait(dve, "bc", 1)
            for k in range(3):
                norm_scaled(NQ, u5[:, k, :], u5[:, k, :], vec[:, V_QN + k:V_QN + k + 1]).then_inc(NQ["h"], 1)
            norm_spread(dve, NKV)
            for k in range(2):
                norm_scaled(NKV, u5[:, 3 + k, :], u5[:, 3 + k, :], vec[:, V_KVN + k:V_KVN + k + 1]).then_inc(NKV["h"], 1)
            for s, n, k0, hi, lo in ((NQ, 3, 0, cq_hi, cq_lo), (NKV, 2, 3, ckv_hi, ckv_lo)):
                s.wait(dve, "h", n)
                for k in range(n):
                    s.wait(dve, "hi", k + 1)
                    nc.vector.tensor_tensor(lo[:, k, :], u5[:, k0 + k, :], hi[:, k, :].bitcast(F32), ALU.subtract).then_inc(s["lo"], 1)

        def mla_in_act(act):
            def square(s, i, k):
                if i:
                    s.wait(act, "ssq", i)
                nc.scalar.activation(sq[:, :], u5[:, k, :], ACT.Square).then_inc(s["sq"], 1)
            for i in range(3):
                act.wait_ge(min_read, i + 1)
                square(NQ, i, i)
            act.wait_ge(min_read, 5)
            NQ.wait(act, "ssq", 3)
            square(NKV, 0, 3)
            norm_root(act, NQ, QL)
            square(NKV, 1, 4)
            for i in range(DT):
                if i == 4:
                    norm_root(act, NKV, KVL, DT)
                act.wait_ge(unit_done, U_Z + i + 3)
                nc.scalar.activation(mix[:, i, :], flat((pjA, pjB)[i % 2]), ACT.Silu).then_inc(z_read, 1)
            for s, n, k0, hi in ((NQ, 3, 0, cq_hi), (NKV, 2, 3, ckv_hi)):
                s.wait(act, "h", n)
                for k in range(n):
                    nc.scalar.activation(hi[:, k, :], u5[:, k0 + k, :], ACT.Copy).then_inc(s["hi"], 1)

        mla.n_lo = 3
        rope_x = at("rope_x", R_W + 16384, [P, T])
        rope_y = at("rope_y", R_W, [P, T])

        def mla_project(pe, n, b, first_scores):
            pe.wait_ge(w_split, n + (U_HEAD + 3))
            slot = (U_HEAD + b) % 2
            if isinstance(n, int) and n == 0:
                NQ.wait(pe, "lo", 3)
            project(pe, slot, (0, 1, 2), cq_hi, cq_lo, pjA, done=False).then_inc(q_ready, 1)
            if isinstance(n, int) and n == 0:
                NKV.wait(pe, "lo", 2)
            else:
                pe.wait_ge(mla.vaug_done, n)
                pe.wait_ge(mla.cneg_done, n)
            project(pe, slot, (3, 4), ckv_hi, ckv_lo, pjB, done=False, halves=(0,))
            first_scores()
            project(pe, slot, (3, 4), ckv_hi, ckv_lo, pjB, halves=(1,))

        q_ready = sem("mla_q_ready")

        def mla_setup_act(act):
            act.wait_ge(kr_step, 3)
            for b in range(2):
                nc.scalar.activation(mla.bufs[2][b][CR, :], k_rope[CR, :], ACT.Copy).then_inc(mla.setup, 1)

        def mla_setup_dve(dve):
            NKV.wait(dve, "lo", 2)
            dve.wait_ge(mla.setup, 2)
            for b in range(2):
                nc.vector.tensor_tensor(mla.bufs[3][b][CR, :], k_rope[CR, :], mla.bufs[2][b][CR, :].bitcast(F32), ALU.subtract)\
                    .then_inc(mla.setup, 1)

        def mla_constants_dve(dve):
            q_hi, q_lo, k_hi, k_lo, vaug = mla.bufs
            for b in range(2):
                nc.vector.memset(q_lo[b][96:97, :].bitcast(F32), 0.0)
                nc.vector.memset(k_hi[b][96:97, :].bitcast(F32), 1.0)
                nc.vector.memset(k_lo[b][96:97, :].bitcast(F32), 0.0)
                last = nc.vector.memset(vaug[b][:, :, HD:P], 1.0)
            last.then_inc(mla.setup, 1)

        def mla_prepare_act(act, n, b, turn):
            q_hi, q_lo, k_hi, k_lo, vaug = mla.bufs
            q, kv = flat(pjA), flat(pjB)
            act.wait_ge(q_ready, n + 1)
            nc.scalar.activation(q_hi[b][0:HD, :], q[0:HD, :], ACT.Copy, scale=MLA_SCALE).then_inc(mla.hi_done, 1)

            def keys():
                act.wait_ge(unit_done, n + (U_HEAD + 3))
                nc.scalar.activation(k_hi[b][0:HD, :], kv[0:HD, :], ACT.Copy).then_inc(mla.hi_done, 1)

            def values():
                if not (isinstance(n, int) and n == 0):
                    act.wait_ge(mla.vt_ready, n)
                nc.scalar.activation(mla_vT[:, :], kv[HD:P, :], ACT.Copy).then_inc(mla.vT_done, 1)

            def rope():
                act.wait_ge(mla.rope_done, n * 3 + 3)
                nc.scalar.activation(q_hi[b][CR, :], rope_x[CR, :], ACT.Copy).then_inc(mla.hi_done, 1)
            return {1: keys, 2: values, 3: rope}

        def mla_prepare_dve(dve, n, b):
            q_hi, q_lo, k_hi, k_lo, vaug = mla.bufs
            q, kv = flat(pjA), flat(pjB)
            dve.wait_ge(q_ready, n + 1)
            if not (isinstance(n, int) and n == 0):
                dve.wait_ge(mla.lo_done, n * 3)
            nc.vector.tensor_tensor(rope_x[CR, :], q[CR, :], cos_sin[CR, :], ALU.mult).then_inc(mla.rope_done, 1)
            nc.vector.tensor_tensor(rope_y[CR, :], q[SR, :], cos_sin[SR, :], ALU.mult).then_inc(mla.rope_done, 1)
            dve.wait_ge(mla.rope_done, n * 3 + 2)
            nc.vector.tensor_tensor(rope_x[CR, :], rope_x[CR, :], rope_y[CR, :], ALU.add).then_inc(mla.rope_done, 1)
            dve.wait_ge(mla.hi_done, n * 3 + 1)
            nc.vector.scalar_tensor_tensor(q_lo[b][0:HD, :], q[0:HD, :], MLA_SCALE, q_hi[b][0:HD, :].bitcast(F32),
                                           ALU.mult, ALU.subtract).then_inc(mla.lo_done, 1)
            dve.wait_ge(mla.hi_done, n * 3 + 2)
            nc.vector.tensor_tensor(k_lo[b][0:HD, :], kv[0:HD, :], k_hi[b][0:HD, :].bitcast(F32), ALU.subtract).then_inc(mla.lo_done, 1)
            dve.wait_ge(mla.hi_done, n * 3 + 3)
            dve.wait_ge(mla.rope_done, n * 3 + 3)
            nc.vector.tensor_tensor(q_lo[b][CR, :], rope_x[CR, :], q_hi[b][CR, :].bitcast(F32), ALU.subtract).then_inc(mla.lo_done, 1)

        m2_hi, m2_lo, mo_added = sem("mix2_hi"), sem("mix2_lo"), sem("mo_added")
        p_in, p_hi_done, p_lo_done = sem("p_in"), sem("p_hi_done"), sem("p_lo_done")
        pg_read, pp_read, ple_added = sem("ple_gate_read"), sem("emb_read"), sem("ple_added")
        ple_mul, pp_ready = sem("ple_mul"), sem("emb_ready")
        p_raw = at("p_raw", R_S, [P, 2, T])
        p_hi, p_lo = at("p_hi", R_S + 8192, [P, 2, T], F32R), at("p_lo", R_S + 16384, [P, 2, T], F32R)
        emb = at("emb", R_M, [P, DT, T])
        result = at("result", R_H, [P, DT, T])

        def emb_unit(pe, e):
            kts = (e % 4 * 2, e % 4 * 2 + 1)
            last = project(pe, (U_PLE + e // 4) % 2, kts, p_hi, p_lo, (pjA, pjB)[e % 2], done=e % 4 == 3)
            if e % 4 < 3:
                last.then_inc(pp_ready, 1)

        def ple_pe(pe):
            pe.wait_ge(p_lo_done, 1)
            for e in range(DT):
                if e % 4 == 0:
                    pe.wait_ge(w_split, U_PLE + e // 4 + 3)
                if e < 2:
                    pe.wait_ge(mo_added, DT - 1 + e + 2)
                else:
                    pe.wait_ge(pp_read, e - 1)
                emb_unit(pe, e)
                if e == 1:
                    norm_sum_pe(pe, N4, DT + 1, ssq).then_inc(N4["ms"], 1)
                if e == 3:
                    norm_spread_pe(pe, N4, diag, 4).then_inc(N4["bc"], 1)

            def arrived(i):
                if i == 0:
                    pe.wait_ge(pp_read, DT)
                N4.wait(pe, "lo", i + 1)
            project_tiles(pe, ((U_GATE, pjA), (U_GATE + 1, pjB)), range(DT), h_hi, h_lo, arrived)
            units_pe(pe, U_GATE + 2, DT - 2, range(DT), h_hi, h_lo, lambda it, j: pe.wait_ge(pg_read, it * 2 + (j + 1)))

        def emb_act(act):
            for e in range(DT):
                act.wait_ge(unit_done if e % 4 == 3 else pp_ready, U_PLE + e // 4 + 3 if e % 4 == 3 else e - e // 4 + 1)
                nc.scalar.activation(emb[:, e, :], flat((pjA, pjB)[e % 2]), ACT.Copy).then_inc(pp_read, 1)
                if e == 1:
                    norm_root(act, N4, D)

        def ple_act(act):
            with act.Fori(0, DT // 2) as it:
                for j, src in enumerate((pjA, pjB)):
                    act.wait_ge(unit_done, it * 2 + (U_GATE + j + 3))
                    act.wait_ge(ple_added, it * 2 + (j + 1))
                    nc.scalar.activation(tmp[j][:, :], flat(src), ACT.Sigmoid).then_inc(pg_read, 1)
                    act.wait_ge(ple_added, it * 2 + (j + 3))
                    nc.scalar.activation(sq[:, :], flat(x[:, bass.ds(it * 2 + j, 1), :]), ACT.Square).then_inc(N5["sq"], 1)

        def ple_dve(dve):
            dve.wait_ge(N4["lo"], N4.base["lo"] + DT)
            nc.vector.memset(ssq[:, :], 0.0).then_inc(N5["ssq"], 1)
            with dve.Fori(0, DT // 2) as it:
                for j in range(2):
                    tile = flat(x[:, bass.ds(it * 2 + j, 1), :])
                    dve.wait_ge(pg_read, it * 2 + (j + 1))
                    nc.vector.tensor_tensor(tmp[j][:, :], flat(emb[:, bass.ds(it * 2 + j, 1), :]), tmp[j][:, :], ALU.mult).then_inc(ple_mul, 1)
                    dve.wait_ge(ple_mul, it * 2 + (j + 1))
                    nc.vector.tensor_tensor(tile, tmp[j][:, :], tile, ALU.add).then_inc(ple_added, 1)
                    N5.wait(dve, "sq", it * 2 + (j + 1))
                    N5.wait(dve, "ssq", it * 2 + (j + 1))
                    nc.vector.tensor_tensor(ssq[:, :], ssq[:, :], sq[:, :], ALU.add).then_inc(N5["ssq"], 1)

        stage = at("const_stage", R_M, [P, N_CONST])
        pos_i = at("pos_i", R_S + 8192, [P, T], I32)
        ang = [at(f"ang{i}", R_S + 12288 + 4096 * i, [P, T]) for i in range(4)]

        def setup_dve(dve):
            dve.wait_ge(consts_in, 16)
            for dst, k, n in ((ident[:, :], K_ID, P), (ones[:, :], K_ONE, P), (head_mean[:, :], K_BLK, P),
                              (ident_bf[:, :], K_ID, P), (masks[:, :, :].rearrange("p a n -> p (a n)"), K_MASK, 1024),
                              (att_mask[:, :], K_ATT, P), (small_const[:, :], K_CNT, 40)):
                nc.vector.tensor_copy(dst, stage[:, k:k + n]).then_inc(setup_done, 1)

        N_SETUP = 7

        def rope_dve(dve):
            r = slice(64, 128)
            two_pi = 2 * np.pi
            c1 = 6.28125
            c2 = float(np.floor((two_pi - c1) * 2 ** 20) / 2 ** 20)
            c3 = float(two_pi - c1 - c2)
            magic = 1.5 * 2 ** 23
            freq, sign = small_const[r, 32:33], small_const[SR, 33:34]
            a, turns, s = ang[0][r, :], ang[1][r, :], ang[2]
            lim = 3.14159
            steps = [lambda: nc.vector.tensor_copy(a, pos_i[r, :]),
                     lambda: nc.vector.tensor_scalar(a, a, freq, None, ALU.mult),
                     lambda: nc.vector.tensor_scalar(turns, a, float(1 / two_pi), magic, ALU.mult, ALU.add),
                     lambda: nc.vector.tensor_scalar(turns, turns, magic, None, ALU.subtract),
                     lambda: nc.vector.scalar_tensor_tensor(a, turns, -c1, a, ALU.mult, ALU.add),
                     lambda: nc.vector.scalar_tensor_tensor(a, turns, -c2, a, ALU.mult, ALU.add),
                     lambda: nc.vector.scalar_tensor_tensor(a, turns, -c3, a, ALU.mult, ALU.add),
                     lambda: nc.vector.tensor_scalar(a, a, lim, -lim, ALU.min, ALU.max),
                     lambda: nc.vector.tensor_tensor(s[CR, :], s[CR, :], s[CR, :], ALU.mult),
                     lambda: nc.vector.tensor_scalar(cos_sin[CR, :], s[CR, :], -2.0, 1.0, ALU.mult, ALU.add),
                     lambda: nc.vector.tensor_scalar(cos_sin[SR, :], s[SR, :], sign, None, ALU.mult)]

            def run(k):
                if k == 0:
                    dve.wait_ge(pos_in, 16)
                    dve.wait_ge(setup_done, N_SETUP)
                else:
                    dve.wait_ge(rope_s, k)
                if k == 8:
                    dve.wait_ge(rope_a, 2)
                steps[k]().then_inc(rope_s, 1)
            return run

        def rope_act(act):
            act.wait_ge(rope_s, 8)
            nc.scalar.activation(ang[2][CR, :], ang[0][CR, :], ACT.Sin, scale=0.5).then_inc(rope_a, 1)
            nc.scalar.activation(ang[2][SR, :], ang[0][SR, :], ACT.Sin).then_inc(rope_a, 1)

        first_sq = (sq, tmp[0])

        def squares_dve(dve, s, between):
            for k in range(DT):
                s.wait(dve, "sq", k + 1)
                part = first_sq[k % 2]
                if k == 0:
                    nc.vector.tensor_copy(ssq[:, :], part[:, :]).then_inc(s["ssq"], 1)
                else:
                    s.wait(dve, "ssq", k)
                    nc.vector.tensor_tensor(ssq[:, :], ssq[:, :], part[:, :], ALU.add).then_inc(s["ssq"], 1)
                if 2 <= k < 6:
                    between(2 * k - 4)
                    between(2 * k - 3)

        def squares_act(act, s):
            for k in range(DT):
                act.wait_ge(x_in[k], 16)
                if k >= 2:
                    s.wait(act, "ssq", k - 1)
                nc.scalar.activation(first_sq[k % 2][:, :], x[:, k, :], ACT.Square).then_inc(s["sq"], 1)

        block = ctx.enter_context(nc.Block())

        @block.sync
        def _(sp):
            sp.dma_start(stage[:, :], consts).then_inc(consts_in, 16)
            sp.dma_start(vec[:, :], vecs).then_inc(vecs_in, 16)
            sp.dma_start(pos_i[:, :], pos).then_inc(pos_in, 16)

            def load(u, s):
                sp.wait_ge(w_split, u + 1)
                sp.dma_start(raw[s][:, :, :].rearrange("p k n -> p (k n)"), wpack[u, :, :] if isinstance(u, int) else
                             wpack[bass.ds(u, 1), :, :].rearrange("o p n -> (o p) n")).then_inc(w_loaded[s], 16)
            with sp.Fori(0, N_UNITS // 2) as it:
                for s in range(2):
                    load(it * 2 + s, s)
            if N_UNITS % 2:
                load(N_UNITS - 1, 0)
            for k in range(DT):
                N5.wait(sp, "h", k + 1)
                sp.dma_start(outT[k * P:(k + 1) * P, :], result[:, k, :]).then_inc(out_stored[k % 2], 16)
            for s in range(2):
                sp.wait_ge(out_stored[s], 16 * DT // 2)

        @block.gpsimd
        def _(pool):
            pool.sem_inc(w_split, 2)
            nc.gpsimd.memset(zero[:, :], 0.0).then_inc(zero_set, 1)
            pool.wait_ge(zero_set, 1)
            no_change = zero[:, :].rearrange("p (a n) -> p a n", a=1).to_broadcast([P, DT, P])

            def split(u, s, loads):
                pool.wait_ge(w_loaded[s], loads)
                pool.wait_ge(unit_done, u + 1)
                nc.gpsimd.tensor_tensor(w_hi[s][:, :, :], raw[s][:, :, :], no_change, ALU.add).then_inc(w_hi_done, 1)
                pool.wait_ge(w_hi_done, u + 1)
                nc.gpsimd.tensor_tensor(w_lo[s][:, :, :], raw[s][:, :, :], w_hi[s][:, :, :].bitcast(F32), ALU.subtract)\
                    .then_inc(w_split, 1)
            with pool.Fori(0, N_UNITS // 2) as it:
                for s in range(2):
                    split(it * 2 + s, s, it * 16 + 16)
            if N_UNITS % 2:
                split(N_UNITS - 1, 0, 16 * (N_UNITS // 2) + 16)

        @block.scalar
        def _(act):
            act.sem_inc(restA, 1)
            act.sem_inc(fox.pv_done, 4)
            act.sem_inc(mla.pv_done, 4)
            act.sem_inc(gate_read, 1)
            for k in range(DT):
                act.dma_start(x[:, k, :], xT[k * P:(k + 1) * P, :]).then_inc(x_in[k], 16)
            squares_act(act, N1)
            act.wait_ge(setup_done, N_SETUP)
            norm_root(act, N1, D)
            norm_split_act(act, N1, DT, hi_tile)
            rope_act(act)
            small_act(act)
            fox_values_act(act)
            steps(act, fox, lambda n, b, turn: step_act(act, fox, n, b, turn, fox_prepare_act))
            last_act(act, fox)
            rest_act(act)
            gla_act(act)
            act.wait_ge(g_o, 8)
            for k in MIX_ORDER:
                mix_hi_act(k, m_hi)
            act.wait_ge(m_lo, DT)
            for k in range(DT):
                act.dma_start(x[:, k, :], xT[k * P:(k + 1) * P, :]).then_inc(x_back, 16)
            residual_squares(act, wo_added, 0, N2)
            norm_root(act, N2, D)
            norm_split_act(act, N2, DT, hi_tile)
            mlp_act(act)
            two_norms_act(act)
            norm_split_act(act, N3, DT, hi_tile)
            mla_in_act(act)
            mla_setup_act(act)
            steps(act, mla, lambda n, b, turn: step_act(act, mla, n, b, turn, mla_prepare_act))
            last_act(act, mla, lambda k: mix_hi_act(k, m2_hi))
            act.wait_ge(mla.norm_done, 2 * MLA_H)
            mix_hi_act(DT - 1, m2_hi)
            act.dma_start(p_raw[:, :, :], pT.rearrange("(k p) t -> p k t", p=P)).then_inc(p_in, 16)
            act.wait_ge(p_in, 16)
            nc.scalar.activation(tau(p_hi), tau(p_raw), ACT.Copy).then_inc(p_hi_done, 1)
            residual_squares(act, mo_added, 0, N4)
            emb_act(act)
            norm_split_act(act, N4, DT, hi_tile)
            ple_act(act)
            norm_root(act, N5, D)

        @block.vector
        def _(dve):
            for s, credit in ((wo_added, 2), (up_read, 1), (dn_added, 2), (a_split_lo, 1), (ple_added, 2), (mo_added, 2), (restB, 1)):
                dve.sem_inc(s, credit)
            rope_step = rope_dve(dve)
            setup_dve(dve)
            squares_dve(dve, N1, rope_step)
            dve.wait_ge(vecs_in, 16)
            dve.wait_ge(setup_done, N_SETUP)
            norm_spread(dve, N1)
            norm_split_dve(dve, N1, DT, lambda k: x[:, k, :], gain_of(V_LN1), hi_tile, lo_tile)
            for k in range(8, 11):
                rope_step(k)
            small_dve(dve)
            fox_setup_dve(dve)
            steps(dve, fox, lambda n, b, turn: step_dve(dve, fox, n, b, turn, fox_prepare_dve, 4, False))
            for half in range(2):
                norm_half_dve(dve, fox, FOX_H - 1, 1, half, 4 + FOX_H // 2 - 1, False)
            rest_dve(dve)
            pool_dve(dve)
            gla_dve(dve)
            for i, k in enumerate(MIX_ORDER):
                mix_lo_dve(dve, k, i, m_hi, m_lo)
            dve.wait_ge(x_back, 16 * DT)
            residual_dve(dve, U_WO, wo_added, 0, N2)
            norm_spread(dve, N2)
            norm_split_dve(dve, N2, DT, lambda k: x[:, k, :], gain_of(V_LN2), hi_tile, lo_tile)
            mlp_dve(dve)
            two_norms_dve(dve)
            mla_in_dve(dve)
            mla_setup_dve(dve)
            steps(dve, mla, lambda n, b, turn: step_dve(dve, mla, n, b, turn, mla_prepare_dve, 0, True))
            for k in range(2):
                mix_lo_dve(dve, k, k, m2_hi, m2_lo)
            norm_half_dve(dve, mla, MLA_H - 1, 1, 0, MLA_H // 2 - 1, True)
            for k in range(2, DT - 1):
                mix_lo_dve(dve, k, k, m2_hi, m2_lo)
            norm_half_dve(dve, mla, MLA_H - 1, 1, 1, MLA_H // 2 - 1, True)
            mix_lo_dve(dve, DT - 1, DT - 1, m2_hi, m2_lo)
            dve.wait_ge(p_hi_done, 1)
            nc.vector.tensor_tensor(tau(p_lo), tau(p_raw), tau(p_hi).bitcast(F32), ALU.subtract).then_inc(p_lo_done, 1)
            residual_dve(dve, U_MO, mo_added, 0, N4)
            norm_spread(dve, N4)
            norm_split_dve(dve, N4, DT, lambda k: x[:, k, :], lambda k: None, hi_tile, lo_tile)
            ple_dve(dve)
            norm_spread(dve, N5)
            for k in range(DT):
                norm_scaled(N5, result[:, k, :], x[:, k, :], vec[:, V_FN + k:V_FN + k + 1]).then_inc(N5["h"], 1)

        @block.tensor
        def _(pe):
            pe.sem_inc(unit_done, 2)
            pe.wait_ge(setup_done, N_SETUP)
            norm_pe(pe, N1, DT)
            project_tiles(pe, ((U_SMALL, pjA), (U_FV, pjB)), range(DT), h_hi, h_lo, lambda i: N1.wait(pe, "lo", i + 1))
            fox_values_pe(pe)
            pe.wait_ge(fv_read, FOX_H // 2)
            pe.wait_ge(fox.setup, 1)
            steps(pe, fox, lambda n, b, turn: step_pe(pe, fox, n, b, turn, fox_project, fox_vT))
            last_pe(pe, fox)
            rest_pe(pe)
            gla_pe(pe)
            project_tiles(pe, ((U_WO, pjA),), MIX_ORDER, h_hi, mix_lo, lambda i: pe.wait_ge(m_lo, i + 1))
            pe.wait_ge(w_split, U_WO + 1 + 3)
            project(pe, (U_WO + 1) % 2, range(DT), h_hi, mix_lo, pjB)
            units_pe(pe, U_WO + 2, DT - 2, range(DT), h_hi, mix_lo, lambda it, j: pe.wait_ge(wo_added, it * 2 + (j + 3)))
            norm_pe(pe, N2, DT + 1)
            mlp_pe(pe)
            two_norms_pe(pe)
            mla_in_pe(pe)
            pe.wait_ge(z_read, DT)
            steps(pe, mla, lambda n, b, turn: step_pe(pe, mla, n, b, turn, mla_project, mla_vT))
            last_pe(pe, mla)
            project_tiles(pe, ((U_MO, pjA),), range(DT), h_hi, mix_lo, lambda i: pe.wait_ge(m2_lo, i + 1))
            pe.wait_ge(w_split, U_MO + 1 + 3)
            project(pe, (U_MO + 1) % 2, range(DT), h_hi, mix_lo, pjB)
            units_pe(pe, U_MO + 2, DT - 2, range(DT), h_hi, mix_lo, lambda it, j: pe.wait_ge(mo_added, it * 2 + (j + 3)))
            ple_pe(pe)
            norm_pe(pe, N5, DT + 1)


def shape_constants():
    c = np.zeros((P, N_CONST), np.float32)
    i = np.arange(P)
    c[:, K_ID:K_ID + P] = np.eye(P)
    c[:, K_ONE:K_ONE + P] = 1.0
    c[:, K_BLK:K_BLK + P] = (i[:, None] // HD == i[None, :] // HD) / HD
    later = i[None, :] > i[:, None]
    chunk_later = i[None, :] // CHUNK > i[:, None] // CHUNK
    for k, m in ((0, later), (2, chunk_later)):
        by_query = c[:, K_MASK + 256 * k:K_MASK + 256 * (k + 1)]
        by_query[:, 0:P], by_query[:, P:] = m * NEG, NEG
        by_key = c[:, K_MASK + 256 * (k + 1):K_MASK + 256 * (k + 2)]
        by_key[:, 0:P], by_key[:, P:] = NEG, m.T * NEG
    c[:, K_ATT:K_ATT + P] = (i[:, None] // CHUNK == i[None, :] // CHUNK) & (i[:, None] <= i[None, :])
    t = np.arange(16)
    for tile, row, w in ((0, 0, 2), (0, HD, 4), (1, 0, 8), (1, HD, 16)):
        c[row:row + HD, K_CNT + 16 * tile:K_CNT + 16 * tile + 16] = 1.0 / np.minimum(t + 1, w)
    half = ROPE // 2
    c[:, K_FREQ] = (np.float32(ROPE_THETA) ** (-np.arange(0, ROPE, 2, dtype=np.float32) / np.float32(ROPE)))[i % half]
    c[:, K_SIGN] = np.where(i % ROPE < half, -1.0, 1.0)
    c[:, K_EPS] = EPS
    c[:, K_EPS + 1] = 1.0
    return c


def pack_units(w_in, w_o, w_gu, w_down, mla_in, w_q_b, w_kv_b, mla_out, ple_gate, ple_proj):
    units = np.zeros((N_UNITS, P, DT, P), np.float32)

    def put(u, w, cols, kt0=0, to=0, rows=slice(None)):
        part = w[rows][:, cols]
        k = part.shape[0] // P
        units[u, :, kt0:kt0 + k, to:to + part.shape[1]] = part.reshape(k, P, -1).transpose(1, 0, 2)

    def tile(c0, n=P):
        return slice(c0, c0 + n)

    put(U_SMALL, w_in, tile(C_GA, 16))
    put(U_SMALL, w_in, tile(C_FF, FOX_H), to=32)
    for i in range(FOX_H // 2):
        put(U_FV + i, w_in, tile(C_FV + P * i))
    for h in range(FOX_H):
        put(U_FQK + h, w_in, tile(C_FQ + HD * h, HD))
        put(U_FQK + h, w_in, tile(C_FK + HD * h, HD), to=HD)
    for i in range(N_REST):
        put(U_REST + i, w_in, tile(P * i))
    for i in range(DT):
        put(U_WO + i, w_o, tile(P * i))
    f0 = 0
    for c, n in enumerate(MLP_CHUNKS):
        for f in range(n):
            put(U_GU[c] + 2 * f, w_gu, tile(P * (f0 + f)))
            put(U_GU[c] + 2 * f + 1, w_gu, tile(FF + P * (f0 + f)))
        for i in range(DT):
            put(U_DN[c] + i, w_down, tile(P * i), rows=slice(P * f0, P * (f0 + n)))
        f0 += n
    for i in range(5):
        put(U_MIN + i, mla_in, tile(P * i))
    half = ROPE // 2
    k0 = QL + KVL
    put(U_MIN + 5, mla_in, tile(k0, ROPE), to=64)
    put(U_MIN + 5, mla_in, tile(k0 + half, half), to=96)
    put(U_MIN + 5, mla_in, tile(k0, half), to=96 + half)
    for i in range(DT):
        put(U_Z + i, mla_in, tile(k0 + ROPE + P * i))
    for h in range(MLA_H):
        q0 = (NOPE + ROPE) * h
        put(U_HEAD + h, w_q_b, tile(q0, NOPE + ROPE))
        put(U_HEAD + h, w_q_b, tile(q0 + NOPE + half, half), to=96)
        put(U_HEAD + h, w_q_b, tile(q0 + NOPE, half), to=96 + half)
        put(U_HEAD + h, w_kv_b, tile(P * h), kt0=3)
    for i in range(DT):
        put(U_MO + i, mla_out, tile(P * i))
        put(U_PLE + i // 4, ple_proj, tile(P * i), kt0=i % 4 * 2)
        put(U_GATE + i, ple_gate, tile(P * i))
    return units.reshape(N_UNITS, P, DT * P)


def pack_vectors(inputs):
    v = np.zeros((P, N_VEC), np.float32)
    for col, name in ((V_LN1, "ln1"), (V_LN2, "ln2"), (V_LNF, "ln_f"), (V_FN, "final_norm_2"), (V_NG, "norm_g_2"), (V_GN, "gla_gn"), (V_BA, "b_a"),
                      (V_PS, "pool_scale"), (V_QN, "mla_q_norm_2"), (V_KVN, "mla_kv_norm_2")):
        a = np.asarray(inputs[name]).reshape(-1, P)
        v[:, col:col + a.shape[0]] = a.T
    v[32:32 + FOX_H, V_BF] = np.asarray(inputs["b_f"])[0]
    w = np.asarray(inputs["w_pool"])[0]
    for g in range(4):
        r = HD * (g % 2)
        v[r:r + HD, V_WPOOL + P * (g // 2) + r:V_WPOOL + P * (g // 2) + r + HD] = w[g]
    v[0:16, V_WAUP:V_WAUP + GLA_W] = np.asarray(inputs["w_a_up"])[0]
    return v


def kernel(**inputs):
    import concourse.bacc as bacc
    from concourse.bass_utils import run_bass_kernel_spmd

    def first(name):
        return np.asarray(inputs[name])[0]

    arrays = {
        "wpack": pack_units(first("w_in"), first("w_o"), first("w_gu"), first("w_down"), first("mla_w_in_2"),
                            first("mla_w_q_b_2"), first("mla_w_kv_b_2"), first("mla_w_out_2"), first("ple_gate_2"),
                            first("ple_proj_2")),
        "xT": np.ascontiguousarray(first("x").T),
        "pT": np.ascontiguousarray(np.asarray(inputs["p_2"])[0, 0].T),
        "vecs": pack_vectors(inputs),
        "consts": shape_constants(),
        "pos": np.ascontiguousarray(np.broadcast_to(np.asarray(inputs["positions_2"]), (P, T))),
    }
    nc = bacc.Bacc("TRN2", target_bir_lowering=False, num_devices=1)
    args = [nc.dram_tensor(f"in_{n}", a.shape, mybir.dt.from_np(a.dtype), kind="ExternalInput").ap() for n, a in arrays.items()]
    out = nc.dram_tensor("out", (D, T), F32, kind="ExternalOutput").ap()
    f_rows = nc.dram_tensor("f_rows", (2, FOX_H, T), F32).ap()
    build(nc, *args, out, f_rows)
    r = run_bass_kernel_spmd(nc, [{f"in_{n}": a for n, a in arrays.items()}], core_ids=[0])
    return np.ascontiguousarray(r.results[0]["out"].T).reshape(1, T, D)
```

```python
from contextlib import ExitStack

import numpy as np

import concourse.bass as bass
from concourse import mybir

F32 = mybir.dt.float32
F32R = mybir.dt.float32r
BF16 = mybir.dt.bfloat16
U32 = mybir.dt.uint32
I32 = mybir.dt.int32
ALU = mybir.AluOpType
ACT = mybir.ActivationFunctionType
LN_EXP = "natural_log_exp_and_others"
AX_X = mybir.AxisListType.X

P = 128
T = 1024
D = 1024
DT = D // P
HALF = 512
EPS = 1e-6
CHUNK = 64
NCH = T // CHUNK

POOL_W = GLA_W = 256
GLA_TAU = 16.0
FOX_W = 512
FOX_H = 8
HD = 64
FF = 2816
FT = FF // P
MLP_CHUNKS = (5, 5, 6, 6)
MLA_H = 16
QL, KVL, NOPE, ROPE = 384, 256, 64, 32
MLA_SCALE = (NOPE + ROPE) ** -0.5
ROPE_THETA = 10000.0
NEG = -1.0e30

C_POOL, C_GQ, C_GK, C_GV, C_GG, C_GA = 0, 256, 512, 768, 1024, 1280
C_FQ = 1296
C_FK, C_FV, C_FF = C_FQ + FOX_W, C_FQ + 2 * FOX_W, C_FQ + 3 * FOX_W

U_SMALL = 0
U_FV = (U_SMALL + 1, U_SMALL + 2, U_SMALL + 4, U_SMALL + 5)
U_FQK0 = U_SMALL + 3
U_FQK = U_FV[-1]
U_REST = U_FQK + FOX_H
assert len(U_FV) == FOX_H // 2
N_REST = 10
U_WO = U_REST + N_REST
N_HALVED = 2 + 2 * (DT - 2)
U_GU, U_DN = [], []
_u = U_WO + N_HALVED
for _n in MLP_CHUNKS:
    U_GU.append(_u)
    U_DN.append(_u + 2 * _n)
    _u += 2 * _n + DT
U_MIN = U_DN[-1] + N_HALVED
U_Z = U_MIN + 6
U_HEAD = U_Z + DT
U_MO = U_HEAD + MLA_H
U_PLE = U_MO + DT
U_GATE = U_PLE + 2
N_UNITS = U_GATE + N_HALVED

V_LN1, V_LN2, V_LNF, V_NG = 0, 8, 16, 24
V_GN, V_BA, V_PS, V_QN, V_KVN, V_BF, V_FN = 32, 34, 36, 38, 41, 43, 44
V_WPOOL, V_WAUP = 56, 56 + 256
N_VEC = 56 + 512

K_ID, K_ONE, K_BLK = 0, 128, 256
K_MASK = 384
K_ATT = K_MASK + 4 * 256
K_CNT = K_ATT + 128
K_FREQ, K_SIGN, K_EPS = K_CNT + 32, K_CNT + 33, K_CNT + 34
N_CONST = K_CNT + 40


def build(nc, wpack, xT, pT, vecs, consts, pos, outT, f_rows):
    with ExitStack() as ctx:
        def sem(name):
            return ctx.enter_context(nc.semaphore(name))

        base = (nc.sbuf_base + 63) // 64 * 64
        R_X = base
        R_S = R_X + 32768
        R_M = R_S + 28672
        R_H = R_M + 32768
        R_RING = R_H + 65536
        R_W = R_RING + 24576
        R_C = R_W + 20480
        top = [R_C]

        def at(name, offset, shape, dt=F32):
            return nc.alloc_sbuf_tensor_at(name, shape, dt, offset=offset)

        def const(name, shape, dt=F32):
            n = int(np.prod(shape[1:])) * mybir.dt.size(dt)
            off = top[0]
            top[0] += (n + 31) // 32 * 32
            return at(name, off, shape, dt)

        x = at("x", R_X, [P, DT, T])
        h_hi = at("h_hi", R_H, [P, DT, T], F32R)
        h_lo = at("h_lo", R_H + 32768, [P, DT, T], F32R)
        mix = at("mix", R_M, [P, DT, T])
        mix_lo = at("mix_lo", R_M, [P, DT, T], F32R)
        raw = [at(f"w_raw{s}", R_RING + 4096 * s, [P, DT, P]) for s in range(2)]
        w_hi = [at(f"w_hi{s}", R_RING + 8192 + 4096 * s, [P, DT, P], F32R) for s in range(2)]
        w_lo = [at(f"w_lo{s}", R_RING + 16384 + 4096 * s, [P, DT, P], F32R) for s in range(2)]
        ssq = at("ssq", R_W, [P, T])
        diag = at("diag", R_W + 4096, [P, T])
        tmp = [at(f"tmp{s}", R_W + 8192 + 4096 * s, [P, T]) for s in range(2)]
        sq = at("sq", R_W + 16384, [P, T])
        cos_sin = at("cos_sin", R_S, [P, T])

        vec = const("vec", [P, N_VEC])
        ident = const("ident", [P, P])
        ones = const("ones", [P, P])
        head_mean = const("head_mean", [P, P])
        small_const = const("small_const", [P, 40])
        ident_bf = const("ident_bf", [P, P], BF16)
        masks = const("masks", [P, 4, 256], BF16)
        att_mask = const("att_mask", [P, P], U32)
        rt = const("rt", [P, 16])
        rv = const("rv", [P, 32])
        mx = const("mx", [P, 8])
        zero = const("zero", [P, 1])
        c_neg = const("c_neg", [DT, P], F32R)
        assert top[0] <= nc.sbuf_usable_end, top[0]
        eps = small_const[:, K_EPS - K_CNT:K_EPS - K_CNT + 1]

        PS = ctx.enter_context(nc.psum_tensor("ps", [P, 8, HALF], F32))
        pjA, pjB = PS[:, 0:2, :], PS[:, 2:4, :]

        def flat(ap):
            return ap.rearrange("p a n -> p (a n)")

        w_loaded = [sem(f"w_loaded{s}") for s in range(2)]
        w_hi_done = sem("w_hi_done")
        w_split = sem("w_split")
        unit_done = sem("unit_done")
        consts_in, vecs_in, pos_in = sem("consts_in"), sem("vecs_in"), sem("pos_in")
        x_in = [sem(f"x_in{k}") for k in range(DT)]
        x_back = sem("x_back")
        zero_set = sem("zero_set")
        setup_done = sem("setup_done")
        rope_s = sem("rope_steps")
        rope_a = sem("rope_sines")
        out_stored = sem("out_stored")

        norm_sem = {k: sem(f"norm_{k}") for k in ("sq", "ssq", "ms", "rt", "rv", "diag", "bc", "h", "hi", "lo")}
        counted = dict.fromkeys(norm_sem, 0)

        class Norm:
            def __init__(self, tiles, split=True, **more):
                self.base = dict(counted)
                n = dict(sq=tiles, ssq=tiles, h=tiles, hi=tiles * split, lo=tiles * split, ms=1, rt=1, rv=1, diag=1, bc=1)
                n.update(more)
                for k in n:
                    counted[k] += n[k]

            def __getitem__(self, k):
                return norm_sem[k]

            def wait(self, eng, k, n):
                eng.wait_ge(norm_sem[k], n + self.base[k])

        two = dict(ms=2, rt=2, rv=2, diag=2, bc=2)
        N1 = Norm(2 * DT, **two)
        N2 = Norm(2 * DT, sq=N_HALVED, ssq=N_HALVED + 1, **two)
        N3 = Norm(2 * DT, sq=2 * N_HALVED, ssq=2 * N_HALVED + 2, ms=2, rt=4, rv=10, diag=2, bc=2)
        NQ, NKV, N4, N5 = Norm(3), Norm(2), Norm(DT, ssq=DT + 1), Norm(2 * DT, split=False, sq=N_HALVED, ssq=N_HALVED + 1, **two)

        def project(pe, slot, kts, hi, lo, dst, done=True, halves=(0, 1)):
            last = None
            for half in halves:
                t = slice(half * HALF, (half + 1) * HALF)
                n, total = 0, 3 * len(kts)
                for w, a in ((w_lo, hi), (w_hi, lo), (w_hi, hi)):
                    for i, kt in enumerate(kts):
                        last = nc.tensor.matmul(dst[:, half, :], w[slot][:, kt, :], a[:, i, t],
                                                start=(n == 0), stop=(n == total - 1))
                        n += 1
            if done:
                last.then_inc(unit_done, 1)
            return last

        def project_tiles(pe, units, order, hi, lo, arrived, done=1):
            for u, _ in units:
                pe.wait_ge(w_split, u + 3)
            for i, kt in enumerate(order):
                arrived(i)
                for u, dst in units:
                    for half in range(2):
                        t = slice(half * HALF, (half + 1) * HALF)
                        for n, (w, a) in enumerate(((w_lo, hi), (w_hi, lo), (w_hi, hi))):
                            last = nc.tensor.matmul(dst[:, half, :], w[u % 2][:, kt, :], a[:, kt, t], start=(i == 0 and n == 0),
                                                    stop=(i == len(order) - 1 and n == 2))
                    if i == len(order) - 1:
                        last.then_inc(unit_done, done)

        def project_by_half(pe, units, hi, lo, arrived, together):
            def part(u, dst, half, kt):
                if half == 0 and kt == 0:
                    pe.wait_ge(w_split, u + 3)
                for n, (w, a) in enumerate(((w_lo, hi), (w_hi, lo), (w_hi, hi))):
                    last = nc.tensor.matmul(dst[:, half, :], w[u % 2][:, kt, :], a[:, kt, cols(half)], start=(kt == 0 and n == 0),
                                            stop=(kt == DT - 1 and n == 2))
                if half == 1 and kt == DT - 1:
                    last.then_inc(unit_done, 1)
            for half in range(2):
                if together[half]:
                    for kt in range(DT):
                        arrived(half, kt)
                        for u, dst in units:
                            part(u, dst, half, kt)
                else:
                    for i, (u, dst) in enumerate(units):
                        for kt in range(DT):
                            if i == 0:
                                arrived(half, kt)
                            part(u, dst, half, kt)

        def norm_sum_pe(pe, s, n_ssq, src, col=0):
            s.wait(pe, "ssq", n_ssq)
            for b in range(DT):
                last = nc.tensor.matmul(PS[:, 7, col + b:col + b + 1], src[:, b * P:(b + 1) * P], ones[:, 0:1],
                                        start=True, stop=True)
            return last

        def norm_spread_pe(pe, s, src, bank):
            s.wait(pe, "diag", 1)
            for half in range(2):
                last = nc.tensor.matmul(PS[:, bank + half, :], ones[:, :], src[:, half * HALF:(half + 1) * HALF],
                                        start=True, stop=True)
            return last

        def norm_pe(pe, s, n_ssq):
            norm_sum_pe(pe, s, n_ssq, ssq).then_inc(s["ms"], 1)
            norm_spread_pe(pe, s, diag, 4).then_inc(s["bc"], 1)

        def norm_root(act, s, width, col=0):
            s.wait(act, "ms", 1)
            nc.scalar.activation(rt[:, 0:DT], PS[:, 7, col:col + DT], ACT.Sqrt, bias=eps, scale=1.0 / width)\
                .then_inc(s["rt"], 1)

        def diagonal(dst, col):
            for b in range(DT):
                last = nc.vector.tensor_scalar(dst[:, b * P:(b + 1) * P], ident[:, :], rv[:, col + b:col + b + 1], None, ALU.mult)
            return last

        def norm_diag(dve, s):
            s.wait(dve, "rt", 1)
            nc.vector.reciprocal(rv[:, 0:DT], rt[:, 0:DT]).then_inc(s["rv"], 1)
            s.wait(dve, "rv", 1)
            diagonal(diag, 0).then_inc(s["diag"], 1)

        def norm_spread(dve, s):
            norm_diag(dve, s)
            s.wait(dve, "bc", 1)

        def norm_scaled(s, dst, src, gain):
            if gain is None:
                return nc.vector.tensor_tensor(dst, src, flat(PS[:, 4:6, :]), ALU.mult)
            return nc.vector.scalar_tensor_tensor(dst, src, gain, flat(PS[:, 4:6, :]), ALU.mult, ALU.mult)

        def norm_split_dve(dve, s, n, src, gain, hi, lo):
            for k in range(n + 1):
                if k < n:
                    if k >= 2:
                        s.wait(dve, "lo", k - 1)
                    norm_scaled(s, tmp[k % 2][:, :], src(k), gain(k)).then_inc(s["h"], 1)
                if k >= 1:
                    s.wait(dve, "hi", k)
                    nc.vector.tensor_tensor(lo(k - 1), tmp[(k - 1) % 2][:, :], hi(k - 1).bitcast(F32), ALU.subtract)\
                        .then_inc(s["lo"], 1)

        def norm_split_act(act, s, tiles, hi):
            for k in tiles:
                s.wait(act, "h", k + 1)
                nc.scalar.activation(hi(k), tmp[k % 2][:, :], ACT.Copy).then_inc(s["hi"], 1)

        def cols(half):
            return slice(half * HALF, (half + 1) * HALF)

        def half_sum_pe(pe, s, n_ssq, half):
            s.wait(pe, "ssq", n_ssq)
            if half:
                s.wait(pe, "rt", 1)
            for b in range(half * 4, half * 4 + 4):
                last = nc.tensor.matmul(PS[:, 7, b:b + 1], ssq[:, b * P:(b + 1) * P], ones[:, 0:1], start=True, stop=True)
            last.then_inc(s["ms"], 1)

        def half_spread_pe(pe, s, half):
            s.wait(pe, "diag", half + 1)
            nc.tensor.matmul(PS[:, 4 + half, :], ones[:, :], diag[:, cols(half)], start=True, stop=True).then_inc(s["bc"], 1)

        def half_root(act, s, half):
            s.wait(act, "ms", half + 1)
            nc.scalar.activation(rt[:, half * 4:half * 4 + 4], PS[:, 7, half * 4:half * 4 + 4], ACT.Sqrt, bias=eps, scale=1.0 / D)\
                .then_inc(s["rt"], 1)

        def half_diag(dve, s, half):
            s.wait(dve, "rt", half + 1)
            nc.vector.reciprocal(rv[:, half * 4:half * 4 + 4], rt[:, half * 4:half * 4 + 4]).then_inc(s["rv"], 1)
            s.wait(dve, "rv", half + 1)
            for b in range(half * 4, half * 4 + 4):
                last = nc.vector.tensor_scalar(diag[:, b * P:(b + 1) * P], ident[:, :], rv[:, b:b + 1], None, ALU.mult)
            last.then_inc(s["diag"], 1)

        def half_split_dve(dve, s, half, k, gain):
            c = cols(half)
            if k < DT:
                if k >= 2:
                    s.wait(dve, "lo", half * DT + k - 1)
                nc.vector.scalar_tensor_tensor(tmp[k % 2][:, c], x[:, k, c], gain(k), PS[:, 4 + half, :], ALU.mult, ALU.mult)\
                    .then_inc(s["h"], 1)
            if k >= 1:
                s.wait(dve, "hi", half * DT + k)
                nc.vector.tensor_tensor(h_lo[:, k - 1, c], tmp[(k - 1) % 2][:, c], h_hi[:, k - 1, c].bitcast(F32), ALU.subtract)\
                    .then_inc(s["lo"], 1)

        def half_split_act(act, s, half, k):
            s.wait(act, "h", half * DT + k + 1)
            nc.scalar.activation(h_hi[:, k, cols(half)], tmp[k % 2][:, cols(half)], ACT.Copy).then_inc(s["hi"], 1)

        HALVED_BANK = (0, 2)

        def halved_pe(pe, first, order, hi, lo, free, free0, after):
            def unit(u, slot, half, bank, n):
                pe.wait_ge(w_split, u + 3)
                pe.wait_ge(free, n)
                t = cols(half)
                k = 0
                for w, a in ((w_lo, hi), (w_hi, lo), (w_hi, hi)):
                    for kt in order:
                        last = nc.tensor.matmul(PS[:, bank, :], w[slot][:, kt, :], a[:, kt, t], start=(k == 0), stop=(k == 3 * len(order) - 1))
                        k += 1
                last.then_inc(unit_done, 1)
            n = (DT - 2) // 2
            with pe.Fori(0, n) as it:
                for j in range(2):
                    unit(it * 2 + (first + 2 + j), (first + j) % 2, 0, HALVED_BANK[j], it * 2 + (free0 + j + 1))
            for i in range(2):
                unit(first + DT + i, (first + i) % 2, 1, HALVED_BANK[i], free0 + DT - 2 + i + 1)
                after[i]()
            with pe.Fori(1, n) as it:
                for j in range(2):
                    unit(it * 2 + (first + DT + j), (first + j) % 2, 1, HALVED_BANK[j], it * 2 + (free0 + DT - 2 + j + 1))

        def halved_dve(dve, first, added, s, after, residual=None, sums=((ssq, sq),)):
            def add(i, c, src, u, n, j):
                if residual is not None:
                    return residual(i, c, n, j)
                dve.wait_ge(unit_done, u + 3)
                tile = flat(x[:, bass.ds(i, 1), c])
                nc.vector.tensor_tensor(tile, src, tile, ALU.add).then_inc(added, 1)

            def total(c, n):
                for i, (whole, part) in enumerate(sums):
                    event = n * len(sums) + (i + 1)
                    s.wait(dve, "sq", event)
                    s.wait(dve, "ssq", event)
                    nc.vector.tensor_tensor(whole[:, c], whole[:, c], part[:, c], ALU.add).then_inc(s["ssq"], 1)
            for whole, _ in sums:
                nc.vector.memset(whole[:, :], 0.0).then_inc(s["ssq"], 1)
            for i, src in enumerate((pjA, pjB)):
                add(i, slice(0, T), flat(src), first + i, i, i)
                total(slice(0, T), i)
            with dve.Fori(0, (DT - 2) // 2) as it:
                for j in range(2):
                    add(it * 2 + (2 + j), cols(0), PS[:, HALVED_BANK[j], :], it * 2 + (first + 2 + j), it * 2 + (2 + j), j)
                    total(cols(0), it * 2 + (2 + j))
            for i in range(DT - 2):
                add(2 + i, cols(1), PS[:, HALVED_BANK[i % 2], :], first + DT + i, DT + i, i % 2)
                total(cols(1), DT + i)
                after.get(i, lambda: None)()

        def halved_act(act, added, added0, s, after, gate=None):
            def square(i, c, src, j, n):
                if gate is not None:
                    gate(src, c, j, n)
                act.wait_ge(added, n + (added0 + 1))
                nc.scalar.activation(sq[:, c], flat(x[:, bass.ds(i, 1), c]), ACT.Square).then_inc(s["sq"], 1)
            for i, src in enumerate((pjA, pjB)):
                square(i, slice(0, T), flat(src), i, i)
            with act.Fori(0, (DT - 2) // 2) as it:
                for j in range(2):
                    square(it * 2 + (2 + j), cols(0), PS[:, HALVED_BANK[j], :], j, it * 2 + (2 + j))
            for i in range(DT - 2):
                square(2 + i, cols(1), PS[:, HALVED_BANK[i % 2], :], i % 2, DT + i)
                after.get(i, lambda: None)()

        SPLIT_AFTER = {1: (0, 1, 2, 3), 2: (4, 5, 6), 3: (7, 8)}

        def halved_norm_dve(dve, first, added, s, gain):
            def split(half, steps):
                for k in steps:
                    half_split_dve(dve, s, half, k, gain)

            def after1():
                s.wait(dve, "bc", 1)
                split(0, SPLIT_AFTER[1])
            halved_dve(dve, first, added, s, {0: lambda: half_diag(dve, s, 0), 1: after1, 2: lambda: split(0, SPLIT_AFTER[2]),
                                              3: lambda: split(0, SPLIT_AFTER[3])})
            half_diag(dve, s, 1)
            s.wait(dve, "bc", 2)
            split(1, range(DT + 1))

        def halved_norm_act(act, added, added0, s):
            def split(steps):
                for k in steps:
                    if k < DT:
                        half_split_act(act, s, 0, k)
            halved_act(act, added, added0, s, {0: lambda: half_root(act, s, 0), 1: lambda: split((0, 1, 2)), 2: lambda: split((3, 4, 5)),
                                               3: lambda: split((6, 7))})
            half_root(act, s, 1)
            for k in range(DT):
                half_split_act(act, s, 1, k)

        def halved_norm_pe(pe, first, order, hi, lo, added, added0, s, nxt):
            halved_pe(pe, first, order, hi, lo, added, added0, (lambda: half_sum_pe(pe, s, DT + 1, 0), lambda: half_spread_pe(pe, s, 0)))

            def arrived(half, k):
                if (half, k) == (0, 0):
                    pe.wait_ge(added, added0 + N_HALVED)
                if (half, k) == (0, 2):
                    half_sum_pe(pe, s, N_HALVED + 1, 1)
                if (half, k) == (0, 6):
                    half_spread_pe(pe, s, 1)
                s.wait(pe, "lo", half * DT + k + 1)
            project_by_half(pe, ((nxt, pjA), (nxt + 1, pjB)), h_hi, h_lo, arrived, (False, False))

        def gain_of(col):
            return lambda k: vec[:, col + k:col + k + 1]

        def hi_tile(k):
            return h_hi[:, k, :]

        def lo_tile(k):
            return h_lo[:, k, :]

        def units_pe(pe, first, n, kts, hi, lo, free):
            with pe.Fori(0, n // 2) as it:
                for j, dst in enumerate((pjA, pjB)):
                    pe.wait_ge(w_split, it * 2 + (first + j + 3))
                    free(it, j)
                    project(pe, (first + j) % 2, kts, hi, lo, dst)

        def residual_dve(dve, first, added, added0, s=None, ssq_first=True):
            if s is not None:
                nc.vector.memset(ssq[:, :], 0.0).then_inc(s["ssq"], 1)
            with dve.Fori(0, DT // 2) as it:
                for j, src in enumerate((pjA, pjB)):
                    tile = flat(x[:, bass.ds(it * 2 + j, 1), :])
                    dve.wait_ge(unit_done, it * 2 + (first + j + 3))
                    nc.vector.tensor_tensor(tile, flat(src), tile, ALU.add).then_inc(added, 1)
                    if s is not None:
                        s.wait(dve, "sq", it * 2 + (j + 1))
                        s.wait(dve, "ssq", it * 2 + (j + 1))
                        nc.vector.tensor_tensor(ssq[:, :], ssq[:, :], sq[:, :], ALU.add).then_inc(s["ssq"], 1)

        def residual_squares(act, added, added0, s):
            with act.Fori(0, DT // 2) as it:
                for j in range(2):
                    act.wait_ge(added, it * 2 + (added0 + j + 3))
                    nc.scalar.activation(sq[:, :], flat(x[:, bass.ds(it * 2 + j, 1), :]), ACT.Square).then_inc(s["sq"], 1)

        class Attention:

            def __init__(self, k, heads, rows_max, rows, mask):
                self.k, self.heads, self.rows_max, self.rows, self.mask = k, heads, rows_max, rows, mask
                self.s_ready = sem(f"{k}_s_ready")
                self.exp_done = sem(f"{k}_exp_done")
                self.p_hi_done = sem(f"{k}_p_hi_done")
                self.p_lo_done = sem(f"{k}_p_lo_done")
                self.pv_hi = sem(f"{k}_pv_hi")
                self.pv_done = sem(f"{k}_pv_done")
                self.vt_ready = sem(f"{k}_vt_ready")
                self.vT_done = sem(f"{k}_vT_done")
                self.vaug_done = sem(f"{k}_vaug_done")
                self.mp_ready = sem(f"{k}_mp_ready")
                self.max_done = sem(f"{k}_max_done")
                self.mT_ready = sem(f"{k}_mT_ready")
                self.cneg_done = sem(f"{k}_cneg_done")
                self.hi_done = sem(f"{k}_hi_done")
                self.lo_done = sem(f"{k}_lo_done")
                self.rope_done = sem(f"{k}_rope_done")
                self.ln_done = sem(f"{k}_ln_done")
                self.r0_done = sem(f"{k}_r0_done")
                self.newton = sem(f"{k}_newton")
                self.norm_done = sem(f"{k}_norm_done")
                self.mx_done = sem(f"{k}_mx_done")
                self.setup = sem(f"{k}_setup")
                self.row_in = [sem(f"{k}_row_in{b}") for b in range(2)]


        PIECES = []
        for half in range(2):
            for j in range(4 * (half + 1)):
                d = j * P - half * HALF
                PIECES.append((half, j, min(max(d, 0), 256), d))
        N_PIECES = len(PIECES)
        LAST_OF_HALF = (3, N_PIECES - 1)
        S_BANK, O_BANK = (4, 5), (6, 7)
        MAX_BANK = ((0, 0), (1, 0), (2, 0), (3, 0), (2, 4), (0, 2), (2, 5), (0, 6))
        MAX_AFTER = {4: (0, 1), 5: (2, 3), 6: (4,), 7: (5,), 8: (6,), 9: (7,)}
        N_MAX = len(MAX_BANK)
        V_BANK, M_BANK = 2, 3
        Pt = [at(f"probs{s}", R_W + 8192 + 2048 * s, [P, HALF]) for s in range(4)]
        P_lo = [at(f"probs_lo{s}", R_W + 8192 + 2048 * s, [P, HALF], F32R) for s in range(4)]
        ln_sum = at("ln_sum", R_W, [P, HALF])
        r0 = at("r0", R_W + 2048, [P, HALF])
        newton = at("newton", R_W + 4096, [P, HALF])
        rec = at("rec", R_W + 6144, [P, HALF])

        def max_width(i):
            w = max(256, (i % 4 + 1) * P)
            return w, i // 4 * HALF + w

        def buffers(k, q_at, klo_at, vaug_at, vlo_at, phi_at):
            q_hi = [at(f"{k}_q_hi{b}", q_at + 4096 * b, [P, T], F32R) for b in range(2)]
            q_lo = [at(f"{k}_q_lo{b}", q_at + 8192 + 4096 * b, [P, T], F32R) for b in range(2)]
            k_hi = [at(f"{k}_k_hi{b}", q_at + 16384 + 4096 * b, [P, T], F32R) for b in range(2)]
            k_lo = [at(f"{k}_k_lo{b}", klo_at + 4096 * b, [P, T], F32R) for b in range(2)]
            vaug = [at(f"{k}_vaug{b}", vaug_at + 4096 * b, [P, DT, P], F32R) for b in range(2)]
            v_lo = [at(f"{k}_v_lo{b}", vlo_at + 2048 * b, [P, DT, HD], F32R) for b in range(2)]
            p_hi = [at(f"{k}_p_hi{s}", phi_at + 2048 * s, [P, HALF], F32R) for s in range(2)]
            return (q_hi, q_lo, k_hi, k_lo, vaug), v_lo, p_hi

        def score_pe(pe, A, n, b, g):
            q_hi, q_lo, k_hi, k_lo, vaug = A.bufs
            half, j, off, d = PIECES[g]
            bank = S_BANK[g % 2]
            out = PS[:, bank, 0:HALF - off]
            t = slice(half * HALF + off, (half + 1) * HALF)
            r = slice(0, A.rows)
            keys = slice(j * P, (j + 1) * P)
            masked = d >= 0
            nc.tensor.matmul(out, k_lo[b][r, keys], q_hi[b][r, t], start=True, stop=False)
            nc.tensor.matmul(out, k_hi[b][r, keys], q_lo[b][r, t], start=False, stop=False)
            last = nc.tensor.matmul(out, k_hi[b][r, keys], q_hi[b][r, t], start=False, stop=not masked)
            if masked:
                extra = d - off
                m = masks[:, A.mask + 1, P - extra:2 * P]
                last = nc.tensor.matmul(PS[:, bank, 0:P + extra], ident_bf[:, :], m, start=False, stop=True)
            last.then_inc(A.s_ready, 1)

        def value_pe(pe, A, n, b, g):
            half, j, off, d = PIECES[g]
            if j == 0 and not (isinstance(n, int) and n == 0):
                pe.wait_ge(A.norm_done, n * 2 + (half - 1))
            pe.wait_ge(A.p_hi_done, n * N_PIECES + (g + 1))
            p = A.p_hi[g % 2][:, 0:HALF - off]
            nc.tensor.matmul(PS[:, O_BANK[half], off:HALF], A.bufs[4][b][:, j, :], p, start=(j == 0), stop=False)
            nc.tensor.matmul(PS[0:HD, O_BANK[half], off:HALF], A.v_lo[b][:, j, :], p, start=False, stop=False).then_inc(A.pv_hi, 1)

        def value_low_pe(pe, A, n, b, g):
            half, j, off, d = PIECES[g]
            pe.wait_ge(A.p_lo_done, n * N_PIECES + (g + 3))
            nc.tensor.matmul(PS[:, O_BANK[half], off:HALF], A.bufs[4][b][:, j, :], P_lo[g % 4][:, 0:HALF - off],
                             start=False, stop=(g in LAST_OF_HALF)).then_inc(A.pv_done, 1)

        def vtrans_pe(pe, A, n, src):
            pe.wait_ge(A.vT_done, n + 1)
            pe.wait_ge(A.max_done, n * N_MAX + 7)
            for j in range(DT):
                dst, part = PS[:, V_BANK, j * HD:(j + 1) * HD], src[0:HD, j * P:(j + 1) * P]
                if j == 0:
                    nc.tensor.matmul(dst, part, ident[0:HD, 0:HD], start=True, stop=True)
                else:
                    last = nc.tensor.transpose(dst, part, ident[0:HD, 0:HD])
            last.then_inc(A.vt_ready, 1)

        def max_pe(pe, A, n, b, i):
            q_hi, _, k_hi, _, _ = A.bufs
            r = slice(0, A.rows_max)
            bank, reduced = MAX_BANK[i]
            if reduced:
                pe.wait_ge(A.max_done, n * N_MAX + reduced)
            queries = q_hi[b][r, i * P:(i + 1) * P]
            if i >= 4:
                nc.tensor.matmul(PS[:, bank, :], queries, k_hi[b][r, 0:HALF], start=True, stop=True)
            w, c, d = max_width(i)[0], i // 4, i % 4 * P
            nc.tensor.matmul(PS[:, bank + c, 0:w], queries, k_hi[b][r, c * HALF:c * HALF + w], start=True, stop=False)
            nc.tensor.matmul(PS[:, bank + c, d:w], ident_bf[:, :], masks[:, A.mask, 0:w - d], start=False, stop=True)\
                .then_inc(A.mp_ready, 1)

        def max_row_pe(pe, A, n):
            pe.wait_ge(A.mx_done, n + 1)
            nc.tensor.transpose(PS[0:DT, M_BANK, 0:P], mx[:, 0:DT], ident[:, :]).then_inc(A.mT_ready, 1)

        def exp_act(act, A, n, g):
            half, j, off, d = PIECES[g]
            scores = PS[:, S_BANK[g % 2], 0:HALF - off]
            act.wait_ge(A.s_ready, n * N_PIECES + (g + 1))
            act.wait_ge(A.pv_hi, n * N_PIECES + (g + 1))
            act.wait_ge(A.p_lo_done, n * N_PIECES + (g + 1))
            nc.scalar.activation(A.p_hi[g % 2][:, 0:HALF - off], scores, ACT.Exp).then_inc(A.p_hi_done, 1)
            act.wait_ge(A.pv_done, n * N_PIECES + (g + 1))
            nc.scalar.activation(Pt[g % 4][:, 0:HALF - off], scores, ACT.Exp).then_inc(A.exp_done, 1)

        def low_pool(pool, A, n, g):
            off = PIECES[g][2]
            w = slice(0, HALF - off)
            pool.wait_ge(A.exp_done, n * N_PIECES + (g + 1))
            nc.gpsimd.tensor_tensor(P_lo[g % 4][:, w], Pt[g % 4][:, w], A.p_hi[g % 2][:, w].bitcast(F32), ALU.subtract)\
                .then_inc(A.p_lo_done, 1)

        def rough_act(act, A, n, half):
            act.wait_ge(A.pv_done, n * N_PIECES + (LAST_OF_HALF[half] + 1 + 4))
            if half == 1 or not (isinstance(n, int) and n == 0):
                act.wait_ge(A.norm_done, n * 2 + half)
            nc.scalar.activation(ln_sum[0:HD, :], PS[HD:P, O_BANK[half], :], ACT.Ln).then_inc(A.ln_done, 1)
            act.wait_ge(A.ln_done, n * 2 + (half + 1))
            nc.scalar.activation(r0[0:HD, :], ln_sum[0:HD, :], ACT.Exp, scale=-1.0).then_inc(A.r0_done, 1)

        def norm_half_dve(dve, A, n, b, half, tile, gate):
            dve.wait_ge(A.r0_done, n * 2 + (half + 1))
            steps = 3 if gate else 2
            seq = n * (2 * steps) + half * steps
            rows = slice(HD * b, HD * b + HD)
            if half == 1 or not (isinstance(n, int) and n == 0):
                dve.wait_ge(A.newton, seq)
                dve.wait_ge(A.norm_done, n * 2 + half)
            nc.vector.tensor_tensor(newton[0:HD, :], PS[HD:P, O_BANK[half], :], r0[0:HD, :], ALU.mult).then_inc(A.newton, 1)
            dve.wait_ge(A.newton, seq + 1)
            nc.vector.scalar_tensor_tensor(rec[rows, :], newton[0:HD, :], -2.0, r0[0:HD, :], ALU.add, ALU.mult).then_inc(A.newton, 1)
            dve.wait_ge(A.newton, seq + 2)
            dst = flat(mix[rows, bass.ds(tile, 1), half * HALF:(half + 1) * HALF])
            if gate:
                nc.vector.tensor_tensor(rec[rows, :], rec[rows, :], dst, ALU.mult).then_inc(A.newton, 1)
                dve.wait_ge(A.newton, seq + 3)
            nc.vector.scalar_tensor_tensor(dst, PS[0:HD, O_BANK[half], :], -1.0, rec[rows, :], ALU.mult, ALU.mult).then_inc(A.norm_done, 1)

        def max_dve(dve, A, n, i):
            dve.wait_ge(A.mp_ready, n * N_MAX + (i + 1))
            bank = MAX_BANK[i][0]
            nc.vector.reduce_max(mx[:, i:i + 1], flat(PS[:, bank:bank + 2, :])[:, 0:max_width(i)[1]] if i >= 4 else
                                 PS[:, bank, 0:max_width(i)[1]], AX_X).then_inc(A.max_done, 1)

        def negate_dve(dve, A, n):
            dve.wait_ge(A.max_done, (n + 1) * N_MAX)
            nc.vector.tensor_scalar(mx[:, 0:8], mx[:, 0:8], -1.0, None, ALU.mult).then_inc(A.mx_done, 1)

        def vaug_dve(dve, A, n, b):
            dve.wait_ge(A.vt_ready, n + 1)
            v = PS[:, V_BANK, :].rearrange("p (j e) -> p j e", e=HD)
            nc.vector.tensor_copy(A.bufs[4][b][:, :, 0:HD], v).then_inc(A.vaug_done, 1)
            dve.wait_ge(A.vaug_done, n * 2 + 1)
            nc.vector.tensor_tensor(A.v_lo[b][:, :, :], v, A.bufs[4][b][:, :, 0:HD].bitcast(F32), ALU.subtract).then_inc(A.vaug_done, 1)

        def max_row_dve(dve, A, n):
            dve.wait_ge(A.mT_ready, n + 1)
            nc.vector.tensor_copy(c_neg[:, :], PS[0:DT, M_BANK, 0:P]).then_inc(A.cneg_done, 1)

        def max_row_act(act, A, n, b, turn):
            act.wait_ge(A.cneg_done, n + 1)
            act.dma_start(A.bufs[0][b][A.rows - 1:A.rows, :].bitcast(F32), c_neg[:, :].bitcast(F32)).then_inc(A.row_in[b], 16)

        fox = Attention("fox", FOX_H, HD + 1, HD + 2, 0)
        fox.bufs, fox.v_lo, fox.p_hi = buffers("fox", R_X, R_X + 24576, R_S + 8192, R_S + 20480, R_S + 24576)
        fox.f_in = [sem(f"fox_f_in{b}") for b in range(2)]
        fox_vT = at("fox_vT", R_S + 16384, [HD, T])
        mla = Attention("mla", MLA_H, NOPE + ROPE, NOPE + ROPE + 1, 2)
        mla.bufs, mla.v_lo, mla.p_hi = buffers("mla", R_H + 40960, R_S + 8192, R_S + 16384, R_S + 24576, R_S + 4096)
        mla_vT = at("mla_vT", R_W + 16384, [HD, T])

        def attend_pe(pe, A, n, b, after=()):
            for g in range(N_PIECES):
                value_pe(pe, A, n, b, g)
                if g:
                    value_low_pe(pe, A, n, b, g - 1)
                if g + 2 < N_PIECES:
                    pe.wait_ge(A.exp_done, n * N_PIECES + (g + 1))
                    score_pe(pe, A, n, b, g + 2)
                if after and g < N_PIECES - 1:
                    after(g)
            value_low_pe(pe, A, n, b, N_PIECES - 1)
            if after:
                after(N_PIECES - 1)

        def step_pe(pe, A, n, b, turn, project_head, vT):
            prev = None if isinstance(n, int) and n == 0 else n - 1

            def first_scores():
                if isinstance(n, int) and n == 1 and A is mla:
                    pe.wait_ge(mla_constants, 8)
                if prev is not None:
                    pe.wait_ge(A.row_in[1 - b], 16 * turn if b == 0 else turn * 16 + 16)
                    score_pe(pe, A, prev, 1 - b, 0)
                    score_pe(pe, A, prev, 1 - b, 1)

            def maxima(g):
                if g == min(MAX_AFTER):
                    pe.wait_ge(A.lo_done, (n + 1) * A.n_lo)
                    if A is fox:
                        pe.wait_ge(A.f_in[b], turn * 32 + 32)
                    elif prev is None:
                        pe.wait_ge(A.setup, 4)
                for i in MAX_AFTER.get(g, ()):
                    if i == 2:
                        pe.wait_ge(A.vT_done, n + 1)
                    max_pe(pe, A, n, b, i)
                if g == N_PIECES - 1:
                    vtrans_pe(pe, A, n, vT)
                    max_row_pe(pe, A, n)

            project_head(pe, n, b, first_scores)
            if prev is not None:
                attend_pe(pe, A, prev, 1 - b, maxima)
            else:
                for g in range(N_PIECES):
                    maxima(g)

        def last_pe(pe, A):
            pe.wait_ge(A.row_in[1], 16 * (A.heads // 2))
            for g in range(2):
                score_pe(pe, A, A.heads - 1, 1, g)
            attend_pe(pe, A, A.heads - 1, 1)

        def step_act(act, A, n, b, turn, prepare):
            prev = None if isinstance(n, int) and n == 0 else n - 1
            todo = prepare(act, n, b, turn)
            for g in range(N_PIECES):
                if prev is not None:
                    exp_act(act, A, prev, g)
                if g in todo:
                    todo[g]()
                if g == 6 and prev is not None:
                    rough_act(act, A, prev, 0)
            if prev is not None:
                rough_act(act, A, prev, 1)
            max_row_act(act, A, n, b, turn)

        def last_act(act, A, split=None):
            for g in range(N_PIECES):
                exp_act(act, A, A.heads - 1, g)
                if g == 6:
                    rough_act(act, A, A.heads - 1, 0)
                if split is not None and g >= N_PIECES - 2:
                    act.wait_ge(A.norm_done, 2 * (A.heads - 2))
                    split(g - (N_PIECES - 2))
            rough_act(act, A, A.heads - 1, 1)
            if split is not None:
                for k in range(2, DT - 1):
                    split(k)

        def step_dve(dve, A, n, b, turn, prepare, tile0, gate):
            prev = None if isinstance(n, int) and n == 0 else n - 1
            prepare(dve, n, b)
            tile = turn + (tile0 - (b == 0))
            for i in range(N_MAX):
                max_dve(dve, A, n, i)
                if i == 3 and prev is not None:
                    norm_half_dve(dve, A, prev, 1 - b, 0, tile, gate)
            negate_dve(dve, A, n)
            vaug_dve(dve, A, n, b)
            max_row_dve(dve, A, n)
            if prev is not None:
                norm_half_dve(dve, A, prev, 1 - b, 1, tile, gate)

        def steps(eng, A, step):
            for b in range(2):
                step(b, b, 0)
            with eng.Fori(1, A.heads // 2) as turn:
                for b in range(2):
                    step(turn * 2 + b, b, turn)

        small_read, f_stored = sem("small_read"), sem("f_stored")
        f_y, f_log, f_sum = sem("f_y"), sem("f_log"), sem("f_sum")
        fv_read = sem("fv_read")
        rest_read = sem("rest_read")
        a_low = at("a_low", R_S + 4096, [16, T])
        FR = slice(32, 32 + FOX_H)
        f_t = [at(f"f_t{i}", R_X + 4096 * i, [P, T]) for i in range(4)]
        f_hi = at("f_hi", R_X + 16384, [P, T], F32R)
        f_lo = at("f_lo", R_X + 20480, [P, T], F32R)
        f_one = at("f_one", R_X + 24576, [P, T])
        z8 = at("z8", R_X, [P, 8, T])
        zg = mix[:, 2:4, :]
        g0, g1 = at("gla_g0", R_S + 8192, [P, 2, T]), at("gla_g1", R_S + 16384, [P, 2, T])
        restart = at("gla_restart", R_X + 24576, [P, 2, T])
        bcum = at("bcum", R_M + 8192, [P, 2, T])
        e_q = at("gla_e_q", R_X + 24576, [P, 2, T])
        q_in, k_in = at("q_in", R_W, [P, 2, T]), at("k_in", R_W + 8192, [P, 2, T])
        kd_tok = at("kd_tok", R_S + 8192, [P, DT, 2, P])
        v_tok = at("v_tok", R_S + 16384, [P, DT, 2, P])
        attm = [at("attm0", R_X, [P, 2, DT, P]), at("attm1", R_X + 24576, [P, 2, DT, P])]
        S_all = at("S_all", R_H + 32768, [P, 2, NCH, P])
        gla_o = at("gla_o", R_H + 49152, [P, 2, T])
        gla_y = at("gla_y", R_H + 57344, [P, 2, T])
        gla_sq = at("gla_sq", R_W, [P, 2, T])
        gla_ln = at("gla_ln", R_W + 8192, [P, 2, T])
        gla_n = at("gla_n", R_W + 16384, [P, T])
        dec = at("dec", R_S + 24576, [P, 2 * NCH])
        s2 = at("pool_s2", R_W, [P, 2, T])
        s4 = at("pool_s4", R_W + 8192, [P, 2, T])
        s8 = at("pool_s8", R_W + 16384, [P, T])
        pool_step, pool_d, pool_mm = sem("pool_step"), sem("pool_d"), sem("pool_mm")
        pool_out = sem("pool_out")
        g_vt, g_vtok, g_gate, g_act, g_dve = sem("g_vt"), sem("g_vtok"), sem("g_gate"), sem("g_act"), sem("g_dve")
        g_kt, g_ktok, g_att, g_attm, g_kv, g_S = sem("g_kt"), sem("g_ktok"), sem("g_att"), sem("g_attm"), sem("g_kv"), sem("g_S")
        g_intra, g_inter, g_o1, g_o, g_ms = sem("g_intra"), sem("g_inter"), sem("g_o1"), sem("g_o"), sem("g_ms")
        g_sq, g_newton = sem("g_sq"), sem("g_newton")
        g_zero = sem("g_zero")
        m_hi, m_lo = sem("mix_hi"), sem("mix_lo")
        wo_added = sem("wo_added")

        def psflat(a, n):
            return flat(PS[:, a:a + n, :])

        def small_dve(dve):
            dve.wait_ge(unit_done, U_SMALL + 3)
            nc.vector.tensor_copy(a_low[:, :], flat(pjA)[0:16, :]).then_inc(small_read, 1)
            bf = vec[FR, V_BF:V_BF + 1]
            nc.vector.tensor_scalar(f_t[0][FR, :], flat(pjA)[FR, :], bf, 0.0, ALU.add, ALU.min).then_inc(f_y, 1)
            nc.vector.memset(f_one[FR, :], 1.0).then_inc(f_y, 1)
            dve.wait_ge(f_log, 3)
            dve.wait_ge(f_y, 2)
            nc.vector.tensor_tensor(f_t[0][FR, :], f_t[2][FR, :], f_t[0][FR, :], ALU.subtract).then_inc(f_sum, 1)
            dve.wait_ge(f_sum, 1)
            nc.vector.tensor_tensor_scan(f_t[1][FR, :], f_one[FR, :], f_t[0][FR, :], 0.0, ALU.mult, ALU.add).then_inc(f_sum, 1)
            dve.wait_ge(f_sum, 2)
            nc.vector.tensor_copy(f_hi[FR, :], f_t[1][FR, :]).then_inc(f_sum, 1)
            dve.wait_ge(f_sum, 3)
            nc.vector.tensor_tensor(f_lo[FR, :], f_t[1][FR, :], f_hi[FR, :].bitcast(F32), ALU.subtract).then_inc(f_sum, 1)

        def small_act(act):
            act.wait_ge(unit_done, U_SMALL + 3)
            bf = vec[FR, V_BF:V_BF + 1]
            act.wait_ge(f_y, 1)
            nc.scalar.activation(f_t[1][FR, :], flat(pjA)[FR, :], ACT.Abs, bias=bf).then_inc(f_log, 1)
            act.wait_ge(f_log, 1)
            nc.scalar.activation(f_t[2][FR, :], f_t[1][FR, :], ACT.Exp, scale=-1.0).then_inc(f_log, 1)
            act.wait_ge(f_log, 2)
            nc.scalar.activation(f_t[2][FR, :], f_t[2][FR, :], ACT.Ln, bias=one[FR, :]).then_inc(f_log, 1)
            act.wait_ge(f_sum, 4)
            act.dma_start(f_rows[0, :, :], f_hi[FR, :].bitcast(F32)).then_inc(f_stored, 16)
            act.dma_start(f_rows[1, :, :], f_lo[FR, :].bitcast(F32)).then_inc(f_stored, 16)

        one = small_const[:, K_EPS - K_CNT + 1:K_EPS - K_CNT + 2]

        def fox_values_pe(pe):
            pe.wait_ge(w_split, U_FV[1] + 3)
            project(pe, U_FV[1] % 2, range(DT), h_hi, h_lo, FV_BANKS[1])

        FV_BANKS = (pjB, PS[:, 4:6, :], pjB, PS[:, 6:8, :])

        def fox_values_act(act, i):
            act.wait_ge(unit_done, U_FV[i] + 3)
            nc.scalar.activation(mix[:, i, :], flat(FV_BANKS[i]), ACT.Copy).then_inc(fv_read, 1)

        def fox_project(pe, n, b, first_scores):
            if isinstance(n, int) and n == 0:
                pe.wait_ge(f_y, 1)
                pe.wait_ge(f_log, 1)
                pe.wait_ge(w_split, U_FQK0 + 3)
                project(pe, U_FQK0 % 2, range(DT), h_hi, h_lo, pjA)
                for i in range(2, FOX_H // 2):
                    pe.wait_ge(w_split, U_FV[i] + 3)
                    if i == 2:
                        pe.wait_ge(fv_read, 1)
                    project(pe, U_FV[i] % 2, range(DT), h_hi, h_lo, FV_BANKS[i])
                return
            pe.wait_ge(w_split, n + (U_FQK + 3))
            project(pe, (U_FQK + b) % 2, range(DT), h_hi, h_lo, pjA, done=False, halves=(0,))
            first_scores()
            project(pe, (U_FQK + b) % 2, range(DT), h_hi, h_lo, pjA, halves=(1,))

        def fox_prepare_act(act, n, b, turn):
            q_hi, q_lo, k_hi, k_lo, vaug = fox.bufs
            src = flat(pjA)
            if isinstance(n, int) and n == 0:
                act.wait_ge(fox.setup, 10)
                act.wait_ge(f_stored, 32)
            else:
                act.wait_ge(fox.vt_ready, n)
            for part, row in ((0, k_hi[b]), (1, k_lo[b])):
                act.dma_start(row[HD:HD + 1, :].bitcast(F32), f_rows[part, bass.ds(n, 1), :]).then_inc(fox.f_in[b], 16)

            def queries():
                act.wait_ge(unit_done, U_FQK0 + 3 if isinstance(n, int) and n == 0 else n + (U_FQK + 3))
                nc.scalar.activation(q_hi[b][0:HD, :], src[0:HD, :], ACT.Copy, scale=HD ** -0.5).then_inc(fox.hi_done, 1)

            def values():
                if isinstance(n, int) and n == 0:
                    for i in range(2, FOX_H // 2):
                        fox_values_act(act, i)
                nc.scalar.activation(fox_vT[:, :], flat(mix[HD * b:HD * b + HD, bass.ds(turn, 1), :]), ACT.Copy).then_inc(fox.vT_done, 1)
            return {1: queries, 3: values}

        def fox_prepare_dve(dve, n, b):
            q_hi, q_lo, k_hi, k_lo, vaug = fox.bufs
            src = flat(pjA)
            dve.wait_ge(unit_done, U_FQK0 + 3 if isinstance(n, int) and n == 0 else n + (U_FQK + 3))
            if isinstance(n, int) and n == 0:
                dve.wait_ge(fox.setup, 10)
            dve.wait_ge(fox.hi_done, n * 2 + 1)
            nc.vector.tensor_copy(k_hi[b][0:HD, :], src[HD:P, :]).then_inc(fox.hi_done, 1)
            nc.vector.scalar_tensor_tensor(q_lo[b][0:HD, :], src[0:HD, :], HD ** -0.5, q_hi[b][0:HD, :].bitcast(F32),
                                           ALU.mult, ALU.subtract).then_inc(fox.lo_done, 1)
            dve.wait_ge(fox.hi_done, n * 2 + 2)
            nc.vector.tensor_tensor(k_lo[b][0:HD, :], src[HD:P, :], k_hi[b][0:HD, :].bitcast(F32), ALU.subtract)\
                .then_inc(fox.lo_done, 1)

        def fox_constants_pool(pool):
            pool.wait_ge(f_stored, 32)
            pool.wait_ge(rope_s, ROPE_STEPS)
            q_hi, q_lo, k_hi, k_lo, vaug = fox.bufs
            pool.wait_ge(w_split, U_FQK + 1 + 2)
            n = 0
            for b in range(2):
                for dst, value in ((q_hi[b][HD:HD + 2, :], 1.0), (q_lo[b][HD:HD + 2, :], 0.0), (k_hi[b][HD:HD + 2, :], 1.0),
                                   (k_lo[b][HD:HD + 2, :], 0.0), (vaug[b][:, :, HD:P], 1.0)):
                    nc.gpsimd.memset(dst.bitcast(F32), value).then_inc(fox.setup, 1)
                    n += 1
                    pool.wait_ge(fox.setup, n)

        fox.n_lo = 2

        MIX_ORDER = (4, 5, 6, 7, 0, 1, 2, 3)

        def mix_hi_act(k, hi_done):
            nc.scalar.activation(hi_tile(k), mix[:, k, :], ACT.Copy).then_inc(hi_done, 1)

        def mix_lo_dve(dve, k, i, hi_done, lo_done):
            dve.wait_ge(hi_done, i + 1)
            nc.vector.tensor_tensor(mix_lo[:, k, :], mix[:, k, :], hi_tile(k).bitcast(F32), ALU.subtract).then_inc(lo_done, 1)

        def pool_dve(dve):
            dve.wait_ge(rest_read, 2)
            count = [0]

            def shifted(dst, src, w):
                nc.vector.tensor_copy(dst[:, :, 0:w], src[:, :, 0:w])
                nc.vector.tensor_tensor(dst[:, :, w:T], src[:, :, w:T], src[:, :, 0:T - w], ALU.add).then_inc(pool_step, 1)
                count[0] += 1
                dve.wait_ge(pool_step, count[0])
            u = z8[:, 0:2, :]
            shifted(s2, u, 1)
            shifted(s4, s2, 2)
            s8_ = s8[:, :].rearrange("p (a n) -> p a n", a=1)
            shifted(s8_, s4[:, 1:2, :], 4)
            shifted(s2[:, 1:2, :], s8_, 8)
            cnt = small_const[:, 0:32].rearrange("p (c n) -> p c n", c=2)
            for c, r, src, w in ((0, 0, s2[:, 0, :], 2), (0, HD, s4[:, 0, :], 4), (1, 0, s8[:, :], 8), (1, HD, s2[:, 1, :], 16)):
                rows = slice(r, r + HD)
                nc.vector.tensor_tensor(src[rows, 0:16], src[rows, 0:16], cnt[rows, c, :], ALU.mult).then_inc(pool_step, 1)
                count[0] += 1
                nc.vector.scalar_tensor_tensor(z8[rows, c, 16:T], src[rows, 16:T], 1.0 / w, z8[rows, c, 16:T],
                                               ALU.mult, ALU.subtract)
                dve.wait_ge(pool_step, count[0])
                last = nc.vector.tensor_tensor(z8[rows, c, 0:16], src[rows, 0:16], z8[rows, c, 0:16], ALU.subtract)
            last.then_inc(pool_d, 1)

        def pool_pe(pe):
            pe.wait_ge(pool_d, 1)
            pe.wait_ge(g_act, 2)
            for c in range(2):
                for half in range(2):
                    last = nc.tensor.matmul(PS[:, 4 + 2 * c + half, :], vec[:, V_WPOOL + P * c:V_WPOOL + P * c + P],
                                            z8[:, c, half * HALF:(half + 1) * HALF], start=True, stop=True)
            last.then_inc(pool_mm, 1)

        def pool_act(act):
            act.wait_ge(pool_mm, 1)
            for c in range(2):
                nc.scalar.activation(mix[:, c, :], psflat(4 + 2 * c, 2), ACT.Copy, scale=vec[:, V_PS + c:V_PS + c + 1]).then_inc(pool_out, 1)

        def by_chunk(ap):
            return ap.rearrange("p c (n t) -> p (c n) t", t=CHUNK)

        def chunk_col(col):
            return by_chunk(bcum[:, :, :])[:, :, col:col + 1].to_broadcast([P, 2 * NCH, CHUNK])

        def kv_place(c, n):
            return 2 * c + n % 2, n // 2 * CHUNK

        def tau(t):
            return flat(t[:, :, :])

        def turn_pe(first):
            for blk in range(DT):
                for c in range(2):
                    last = nc.tensor.transpose(PS[:, 4 + blk // 2, (blk % 2 * 2 + c) * P:(blk % 2 * 2 + c + 1) * P],
                                               z8[:, first + c, blk * P:(blk + 1) * P], ident[:, :])
            return last

        def att_pe(batch):
            for hh in range(2):
                rows = slice(HD * hh, HD * hh + HD)
                for pr in range(DT):
                    t = slice(pr * P, (pr + 1) * P)
                    last = nc.tensor.matmul(PS[:, 4 + hh * 2 + pr // 4, pr % 4 * P:(pr % 4 + 1) * P], k_in[rows, batch, t],
                                            q_in[rows, batch, t], start=True, stop=True)
            last.then_inc(g_att, 1)

        def rest_pe(pe):
            for i in range(N_REST):
                pe.wait_ge(w_split, U_REST + i + 3)
                if i >= 2:
                    pe.wait_ge(rest_read, i - 1)
                project(pe, (U_REST + i) % 2, range(DT), h_hi, h_lo, (pjA, pjB)[i % 2])
                if i == 0:
                    pe.wait_ge(small_read, 1)
                    pe.wait_ge(fox.norm_done, 2 * FOX_H)
                    for c in range(2):
                        for half in range(2):
                            last = nc.tensor.matmul(PS[:, 4 + 2 * c + half, :], vec[0:16, V_WAUP + P * c:V_WAUP + P * c + P],
                                                    a_low[:, half * HALF:(half + 1) * HALF], start=True, stop=True)
                    last.then_inc(g_gate, 1)
                elif i == 5:
                    pool_pe(pe)
                elif i == 6:
                    pe.wait_ge(pool_out, 2)
                    pe.wait_ge(g_dve, 9)
                    att_pe(0)
                elif i == 7:
                    pe.wait_ge(g_attm, 1)
                    pe.wait_ge(g_dve, 10)
                    turn_pe(4).then_inc(g_kt, 1)
                elif i == 8:
                    pe.wait_ge(g_ktok, 1)
                    pe.wait_ge(rest_read, 8)
                    turn_pe(6).then_inc(g_vt, 1)

        def gla_pe(pe):
            pe.wait_ge(g_vtok, 1)
            att_pe(1)
            pe.wait_ge(rest_read, N_REST)
            for c in range(2):
                for n in range(NCH - 1):
                    rows = slice(n % 2 * CHUNK, n % 2 * CHUNK + CHUNK)
                    bank, col = kv_place(c, n)
                    for a in range(2):
                        r = slice(HD * a, HD * a + HD)
                        last = nc.tensor.matmul(PS[r, bank, col:col + HD], kd_tok[rows, n // 2, c, r], v_tok[rows, n // 2, c, r],
                                                start=True, stop=True)
                last.then_inc(g_kv, 1)
            pe.wait_ge(g_attm, 2)
            for hd in range(4):
                rows = slice(HD * (hd % 2), HD * (hd % 2) + HD)
                for pr in range(DT):
                    last = nc.tensor.matmul(PS[rows, 4 + hd // 2 * 2 + pr // 4, pr % 4 * P:(pr % 4 + 1) * P],
                                            v_tok[:, pr, hd // 2, rows], attm[hd // 2][:, hd % 2, pr, :], start=True, stop=True)
            last.then_inc(g_intra, 1)
            for c, dst in enumerate((pjA, pjB)):
                pe.wait_ge(g_S, 2 * (c + 1) * (NCH - 1))
                for n in range(NCH):
                    last = nc.tensor.matmul(dst[:, n // 8, n % 8 * CHUNK:(n % 8 + 1) * CHUNK], S_all[:, c, n, :],
                                            z8[:, 2 + c, n * CHUNK:(n + 1) * CHUNK], start=True, stop=True)
                last.then_inc(g_inter, 1)

        def gla_mean_pe(pe, c):
            pe.wait_ge(g_sq, c + 1)
            for half in range(2):
                last = nc.tensor.matmul(PS[:, 4 + 2 * c + half, :], head_mean[:, :], gla_sq[:, c, half * HALF:(half + 1) * HALF],
                                        start=True, stop=True)
            last.then_inc(g_ms, 1)

        def rest_act(act):
            act.wait_ge(g_gate, 1)
            for c in range(2):
                act.wait_ge(g_dve, c + 1)
                nc.scalar.activation(g1[:, c, :], psflat(4 + 2 * c, 2), ACT.Abs, bias=vec[:, V_BA + c:V_BA + c + 1]).then_inc(g_act, 1)
            act.wait_ge(g_act, 2)
            nc.scalar.activation(tau(g1), tau(g1), ACT.Exp, scale=-1.0).then_inc(g_act, 1)
            act.preload_act_table_set("natural_log")
            act.wait_ge(g_act, 3)
            nc.scalar.activation(tau(g1), tau(g1), ACT.Ln, bias=one).then_inc(g_act, 1)

            def store(i, fn=ACT.Copy):
                act.wait_ge(unit_done, U_REST + i + 3)
                dst = z8[:, i, :] if i < 8 else zg[:, i - 8, :]
                nc.scalar.activation(dst, flat((pjA, pjB)[i % 2]), fn).then_inc(rest_read, 1)
            store(0)
            store(1)
            inv = 1.0 / GLA_TAU
            act.wait_ge(g_dve, 5)
            nc.scalar.activation(tau(e_q), tau(g1), ACT.Exp, scale=inv).then_inc(g_act, 1)
            act.wait_ge(g_act, 5)
            nc.scalar.activation(tau(g1), tau(g1), ACT.Exp, scale=-inv).then_inc(g_act, 1)
            nc.scalar.activation(tau(g0), tau(bcum), ACT.Exp, scale=inv).then_inc(g_act, 1)
            nc.scalar.activation(dec[:, :], by_chunk(bcum[:, :, :])[:, :, CHUNK - 1], ACT.Exp, scale=inv).then_inc(g_act, 1)
            for i in range(2, 5):
                store(i)
            store(5)
            pool_act(act)
            act.wait_ge(g_dve, 8)
            nc.scalar.activation(tau(g0), tau(g0), ACT.Exp, scale=inv).then_inc(g_act, 1)
            act.wait_ge(g_dve, 9)
            store(6)
            store(7)
            act.wait_ge(g_kt, 1)
            nc.scalar.activation(kd_tok[:, :, :, :].rearrange("p a c n -> p (a c n)"), psflat(4, 4), ACT.Copy).then_inc(g_ktok, 1)
            store(8, ACT.Silu)
            act.wait_ge(g_vt, 1)
            nc.scalar.activation(v_tok[:, :, :, :].rearrange("p a c n -> p (a c n)"), psflat(4, 4), ACT.Copy).then_inc(g_vtok, 1)
            store(9, ACT.Silu)

        def gla_act(act):
            act.preload_act_table_set(LN_EXP)
            for k in MIX_ORDER[:6]:
                mix_hi_act(k, m_hi)
            act.wait_ge(g_intra, 1)
            nc.scalar.activation(tau(gla_o), psflat(4, 4), ACT.Copy).then_inc(g_o1, 1)
            for c in range(2):
                act.wait_ge(g_o, c + 1)
                nc.scalar.activation(gla_sq[:, c, :], gla_o[:, c, :], ACT.Square).then_inc(g_sq, 1)
            for k in range(DT):
                act.dma_start(x[:, k, :], xT[k * P:(k + 1) * P, :]).then_inc(x_back, 16)
            for c in range(2):
                act.wait_ge(g_ms, c + 1)
                nc.scalar.activation(gla_ln[:, c, :], psflat(4 + 2 * c, 2), ACT.Ln, bias=eps).then_inc(g_act, 1)
                act.wait_ge(g_act, 10 + 2 * c)
                nc.scalar.activation(gla_y[:, c, :], gla_ln[:, c, :], ACT.Exp, scale=-0.5).then_inc(g_act, 1)
            for c in range(2):
                act.wait_ge(g_newton, 5 * (c + 1))
                mix_hi_act(2 + c, m_hi)

        def gla_dve(dve):
            dve.wait_ge(g_gate, 1)
            for c in range(2):
                nc.vector.tensor_scalar(g0[:, c, :], psflat(4 + 2 * c, 2), vec[:, V_BA + c:V_BA + c + 1], 0.0, ALU.add, ALU.min).then_inc(g_dve, 1)
            nc.vector.memset(tau(restart), 1.0).then_inc(g_zero, 1)
            dve.wait_ge(g_zero, 1)
            nc.vector.memset(by_chunk(restart[:, :, :])[:, :, 0:1], 0.0).then_inc(g_zero, 1)
            dve.wait_ge(g_act, 4)
            dve.wait_ge(g_dve, 2)
            nc.vector.tensor_tensor(tau(g0), tau(g0), tau(g1), ALU.subtract).then_inc(g_dve, 1)
            dve.wait_ge(g_dve, 3)
            dve.wait_ge(g_zero, 2)
            nc.vector.tensor_tensor_scan(tau(bcum), tau(restart), tau(g0), 0.0, ALU.mult, ALU.add).then_inc(g_dve, 1)
            dve.wait_ge(g_dve, 4)
            nc.vector.tensor_tensor(by_chunk(g1[:, :, :]), by_chunk(bcum[:, :, :]), chunk_col(CHUNK // 2 - 1), ALU.subtract).then_inc(g_dve, 1)
            pool_dve(dve)
            gq, gk = flat(z8[:, 2:4, :]), flat(z8[:, 4:6, :])
            dve.wait_ge(pool_d, 1)
            dve.wait_ge(rest_read, 4)
            dve.wait_ge(g_act, 7)
            nc.vector.scalar_tensor_tensor(tau(q_in), gq, HD ** -0.5, tau(e_q), ALU.mult, ALU.mult).then_inc(g_dve, 1)
            dve.wait_ge(g_dve, 6)
            nc.vector.scalar_tensor_tensor(gq, gq, HD ** -0.5, tau(g0), ALU.mult, ALU.mult).then_inc(g_dve, 1)
            dve.wait_ge(g_dve, 7)
            nc.vector.tensor_tensor(by_chunk(g0[:, :, :]), chunk_col(CHUNK - 1), by_chunk(bcum[:, :, :]), ALU.subtract).then_inc(g_dve, 1)
            dve.wait_ge(rest_read, 6)
            nc.vector.tensor_tensor(tau(k_in), gk, tau(g1), ALU.mult).then_inc(g_dve, 1)
            dve.wait_ge(g_act, 9)
            dve.wait_ge(g_dve, 9)
            nc.vector.tensor_tensor(gk, gk, tau(g0), ALU.mult).then_inc(g_dve, 1)

            m = att_mask[:, :].rearrange("p (o n) -> p o n", o=1).to_broadcast([P, 4, P])

            def zero_att(batch):
                nc.vector.memset(attm[batch][:, :, :, :].rearrange("p h a n -> p (h a n)"), 0.0).then_inc(g_zero, 1)

            def copy_att(batch):
                dve.wait_ge(g_att, batch + 1)
                for bank in range(4):
                    a = bank % 2 * 4
                    last = nc.vector.copy_predicated(attm[batch][:, bank // 2, a:a + 4, :], m,
                                                     PS[:, 4 + bank, :].rearrange("p (a n) -> p a n", n=P))
                last.then_inc(g_attm, 1)
            dve.wait_ge(pool_mm, 1)
            zero_att(0)
            dve.wait_ge(g_zero, 3)
            copy_att(0)
            dve.wait_ge(g_vt, 1)
            zero_att(1)
            dve.wait_ge(unit_done, U_REST + N_REST + 2)
            nc.vector.memset(S_all[:, :, :, :].rearrange("p c a n -> p (c a n)"), 0.0).then_inc(g_zero, 1)
            dve.wait_ge(g_zero, 4)
            copy_att(1)

            def mix_lo_parts(parts):
                for i in parts:
                    mix_lo_dve(dve, MIX_ORDER[i], i, m_hi, m_lo)
            mix_lo_parts((0,))
            dve.wait_ge(g_act, 8)
            dve.wait_ge(g_zero, 5)
            done = 0
            for c in range(2):
                dve.wait_ge(g_kv, c + 1)
                for n in range(NCH - 1):
                    for a in range(2):
                        r = slice(HD * a, HD * a + HD)
                        bank, col = kv_place(c, n)
                        if n:
                            dve.wait_ge(g_S, done - 1)
                        nc.vector.scalar_tensor_tensor(S_all[r, c, n + 1, r], S_all[r, c, n, r], dec[r, c * NCH + n:c * NCH + n + 1],
                                                       PS[r, bank, col:col + HD], ALU.mult, ALU.add).then_inc(g_S, 1)
                        done += 1
            mix_lo_parts((1,))
            dve.wait_ge(g_o1, 1)
            for c, src in enumerate((pjA, pjB)):
                dve.wait_ge(g_inter, c + 1)
                nc.vector.tensor_tensor(gla_o[:, c, :], flat(src), gla_o[:, c, :], ALU.add).then_inc(g_o, 1)
                if c == 0:
                    mix_lo_parts(range(2, 6))
            for c in range(2):
                dve.wait_ge(g_o, c + 1)
                nc.vector.scalar_tensor_tensor(zg[:, c, :], gla_o[:, c, :], vec[:, V_GN + c:V_GN + c + 1], zg[:, c, :],
                                               ALU.mult, ALU.mult).then_inc(g_o, 1)
            for c in range(2):
                y, n = gla_y[:, c, :], gla_n[:, :]
                dve.wait_ge(g_act, 11 + 2 * c)
                if c:
                    dve.wait_ge(g_newton, 5 * c)
                nc.vector.tensor_tensor(n, y, y, ALU.mult).then_inc(g_newton, 1)
                dve.wait_ge(g_newton, 5 * c + 1)
                nc.vector.scalar_tensor_tensor(n, psflat(4 + 2 * c, 2), EPS, n, ALU.add, ALU.mult).then_inc(g_newton, 1)
                dve.wait_ge(g_newton, 5 * c + 2)
                nc.vector.tensor_scalar(n, n, -0.5, 1.5, ALU.mult, ALU.add).then_inc(g_newton, 1)
                dve.wait_ge(g_newton, 5 * c + 3)
                nc.vector.tensor_tensor(y, y, n, ALU.mult).then_inc(g_newton, 1)
                dve.wait_ge(g_newton, 5 * c + 4)
                dve.wait_ge(g_o, 3 + c)
                nc.vector.tensor_tensor(zg[:, c, :], zg[:, c, :], y, ALU.mult).then_inc(g_newton, 1)
            for i in range(6, DT):
                mix_lo_dve(dve, MIX_ORDER[i], i, m_hi, m_lo)

        gate_read, up_read, a_split_hi = sem("gate_read"), sem("up_read"), sem("a_split_hi")
        a_split_lo, dn_added = sem("a_split_lo"), sem("dn_added")
        a_hi = at("a_hi", R_M + 8192, [P, 6, T], F32R)
        a_lo = at("a_lo", R_M - 16384, [P, 6, T], F32R)
        F0 = [sum(MLP_CHUNKS[:c]) for c in range(len(MLP_CHUNKS))]

        def mlp_pe(pe):
            for c, fc in enumerate(MLP_CHUNKS):
                if c:
                    pe.wait_ge(dn_added, DT * c + 2)
                with pe.Fori(c == 0, fc) as f:
                    for j, (dst, free) in enumerate(((pjA, gate_read), (pjB, up_read))):
                        pe.wait_ge(w_split, f * 2 + (U_GU[c] + j + 3))
                        pe.wait_ge(free, f + (F0[c] + 1))
                        project(pe, (U_GU[c] + j) % 2, range(DT), h_hi, h_lo, dst)

                def arrived(i, c=c, fc=fc):
                    if i == 0:
                        pe.wait_ge(gate_read, F0[c] + fc + 1)
                    pe.wait_ge(a_split_lo, F0[c] + i + 2)
                project_tiles(pe, ((U_DN[c], pjA),), range(fc), a_hi, a_lo, arrived)
                pe.wait_ge(w_split, U_DN[c] + 1 + 3)
                project(pe, (U_DN[c] + 1) % 2, range(fc), a_hi, a_lo, pjB)
                if c < len(MLP_CHUNKS) - 1:
                    units_pe(pe, U_DN[c] + 2, DT - 2, range(fc), a_hi, a_lo,
                             lambda it, j, c=c: pe.wait_ge(dn_added, it * 2 + (DT * c + j + 3)))
                else:
                    halved_pe(pe, U_DN[c], range(fc), a_hi, a_lo, dn_added, LAST0,
                              (lambda: two_sums_pe(pe, 0), lambda: two_spreads_pe(pe, 0)))

        def mlp_act(act):
            for c, fc in enumerate(MLP_CHUNKS):
                with act.Fori(0, fc) as f:
                    act.wait_ge(unit_done, f * 2 + (U_GU[c] + 3))
                    act.wait_ge(up_read, f + (F0[c] + 1))
                    nc.scalar.activation(tmp[0][:, :], flat(pjA), ACT.Silu).then_inc(gate_read, 1)
                    act.wait_ge(up_read, f + (F0[c] + 2))
                    nc.scalar.activation(flat(a_hi[:, bass.ds(f, 1), :]), tmp[1][:, :], ACT.Copy).then_inc(a_split_hi, 1)
                if c == len(MLP_CHUNKS) - 1:
                    two_norms_act(act)

        def mlp_dve(dve):
            for c, fc in enumerate(MLP_CHUNKS):
                with dve.Fori(0, fc) as f:
                    dve.wait_ge(unit_done, f * 2 + (U_GU[c] + 4))
                    dve.wait_ge(gate_read, f + (F0[c] + 2))
                    dve.wait_ge(a_split_lo, f + (F0[c] + 1))
                    nc.vector.tensor_tensor(tmp[1][:, :], flat(pjB), tmp[0][:, :], ALU.mult).then_inc(up_read, 1)
                    dve.wait_ge(a_split_hi, f + (F0[c] + 1))
                    nc.vector.tensor_tensor(flat(a_lo[:, bass.ds(f, 1), :]), tmp[1][:, :],
                                            flat(a_hi[:, bass.ds(f, 1), :]).bitcast(F32), ALU.subtract).then_inc(a_split_lo, 1)
                if c < len(MLP_CHUNKS) - 1:
                    residual_dve(dve, U_DN[c], dn_added, DT * c)
                else:
                    two_norms_dve(dve, U_DN[c])

        sq2, ssq2, diag2 = tmp[0], tmp[1], sq
        gain3 = const("gain3", [P, DT])

        LAST0 = DT * (len(MLP_CHUNKS) - 1) + 2
        x2_done = sem("x2_done")

        def two_sums_pe(pe, half):
            N3.wait(pe, "ssq", 2 + 2 * (DT, N_HALVED)[half])
            if half:
                N3.wait(pe, "rv", 3)
            for total, col in ((ssq, 0), (ssq2, DT)):
                for b in range(half * 4, half * 4 + 4):
                    last = nc.tensor.matmul(PS[:, 7, col + b:col + b + 1], total[:, b * P:(b + 1) * P], ones[:, 0:1],
                                            start=True, stop=True)
            last.then_inc(N3["ms"], 1)

        def two_spreads_pe(pe, half):
            N3.wait(pe, "diag", half + 1)
            nc.tensor.matmul(PS[:, 4 + half, :], ones[:, :], diag[:, cols(half)], start=True, stop=True)
            nc.tensor.matmul(PS[:, 6 + half, :], ones[:, :], diag2[:, cols(half)], start=True, stop=True).then_inc(N3["bc"], 1)

        def two_norms_act(act):
            def squares(i, c, n):
                act.wait_ge(dn_added, LAST0 + n + 1)
                nc.scalar.activation(sq[:, c], x[:, i, c], ACT.Square).then_inc(N3["sq"], 1)
                nc.scalar.activation(sq2[:, c], x[:, i, c], ACT.Square, scale=vec[:, V_LNF + i:V_LNF + i + 1]).then_inc(N3["sq"], 1)

            def roots(half):
                c = slice(half * 4, half * 4 + 4)
                N3.wait(act, "ms", half + 1)
                nc.scalar.activation(rt[:, c], PS[:, 7, c], ACT.Sqrt, bias=eps, scale=1.0 / D).then_inc(N3["rt"], 1)
                N3.wait(act, "rv", 5 * half + 3)
                nc.scalar.activation(rt[:, DT + half * 4:DT + half * 4 + 4], rv[:, DT + half * 4:DT + half * 4 + 4], ACT.Sqrt,
                                     bias=eps, scale=1.0 / D).then_inc(N3["rt"], 1)
            for i in range(2):
                squares(i, slice(0, T), i)
            for i in range(2, DT):
                squares(i, cols(0), i)
            for i in range(DT - 2):
                squares(2 + i, cols(1), DT + i)
                if i == 0:
                    roots(0)
                for k in {1: (0, 1, 2), 2: (3, 4, 5), 3: (6, 7)}.get(i, ()):
                    half_split_act(act, N3, 0, k)
            roots(1)
            for k in range(DT):
                half_split_act(act, N3, 1, k)

        def two_norms_dve(dve, first):
            def diagonals(half):
                r1, s2_, r2, r12 = (rv[:, i * DT + half * 4:i * DT + half * 4 + 4] for i in range(4))
                c = slice(half * 4, half * 4 + 4)

                def diagonal(dst, col):
                    for b in range(half * 4, half * 4 + 4):
                        last = nc.vector.tensor_scalar(dst[:, b * P:(b + 1) * P], ident[:, :], rv[:, col + b:col + b + 1], None, ALU.mult)
                    return last
                N3.wait(dve, "rt", 2 * half + 1)
                nc.vector.reciprocal(r1, rt[:, c]).then_inc(N3["rv"], 1)
                N3.wait(dve, "rv", 5 * half + 1)
                nc.vector.tensor_tensor(s2_, PS[:, 7, DT + half * 4:DT + half * 4 + 4], r1, ALU.mult).then_inc(N3["rv"], 1)
                N3.wait(dve, "rv", 5 * half + 2)
                nc.vector.tensor_tensor(s2_, s2_, r1, ALU.mult).then_inc(N3["rv"], 1)
                diagonal(diag2, 0)
                N3.wait(dve, "rt", 2 * half + 2)
                nc.vector.reciprocal(r2, rt[:, DT + half * 4:DT + half * 4 + 4]).then_inc(N3["rv"], 1)
                N3.wait(dve, "rv", 5 * half + 4)
                nc.vector.tensor_tensor(r12, r1, r2, ALU.mult).then_inc(N3["rv"], 1)
                N3.wait(dve, "rv", 5 * half + 5)
                diagonal(diag, 3 * DT).then_inc(N3["diag"], 1)

            def split(half, steps):
                for k in steps:
                    half_split_dve(dve, N3, half, k, lambda k: gain3[:, k:k + 1])

            def scale_x(half, tiles):
                for k in tiles:
                    nc.vector.scalar_tensor_tensor(x[:, k, cols(half)], x[:, k, cols(half)], vec[:, V_LNF + k:V_LNF + k + 1],
                                                   PS[:, 6 + half, :], ALU.mult, ALU.mult).then_inc(x2_done, 1)

            def after1():
                N3.wait(dve, "bc", 1)
                split(0, SPLIT_AFTER[1])
            dve.wait_ge(a_split_lo, FT + 1)
            nc.vector.tensor_tensor(gain3[:, :], vec[:, V_LNF:V_LNF + DT], vec[:, V_NG:V_NG + DT], ALU.mult)
            halved_dve(dve, first, dn_added, N3, {0: lambda: diagonals(0), 1: after1, 2: lambda: split(0, SPLIT_AFTER[2]),
                                                  3: lambda: split(0, SPLIT_AFTER[3])}, sums=((ssq, sq), (ssq2, sq2)))
            scale_x(0, range(6))
            diagonals(1)
            scale_x(0, range(6, DT))
            N3.wait(dve, "bc", 2)
            split(1, range(DT + 1))
            scale_x(1, range(DT))

        u5 = at("u5", R_S + 8192, [P, 5, T])
        k_rope = at("k_rope", R_S + 4096, [P, T])
        cq_hi, cq_lo = at("cq_hi", R_H, [P, 3, T], F32R), at("cq_lo", R_H + 12288, [P, 3, T], F32R)
        ckv_hi, ckv_lo = at("ckv_hi", R_H + 24576, [P, 2, T], F32R), at("ckv_lo", R_H + 32768, [P, 2, T], F32R)
        min_read, kr_step, z_read = sem("min_read"), sem("kr_step"), sem("z_read")
        CR, SR = slice(64, 96), slice(96, 128)

        def mla_in_pe(pe):
            def arrived(half, k):
                if (half, k) == (0, 0):
                    pe.wait_ge(dn_added, LAST0 + N_HALVED)
                if (half, k) == (0, 2):
                    two_sums_pe(pe, 1)
                if (half, k) == (0, 6):
                    two_spreads_pe(pe, 1)
                N3.wait(pe, "lo", half * DT + k + 1)
            project_by_half(pe, ((U_MIN, pjA), (U_MIN + 1, pjB)), h_hi, h_lo, arrived, (False, False))
            for i in range(2, 6):
                pe.wait_ge(w_split, U_MIN + i + 3)
                pe.wait_ge(min_read, i - 1)
                if i == 5:
                    pe.wait_ge(x2_done, 2 * DT)
                    norm_sum_pe(pe, NQ, 3, ssq).then_inc(NQ["ms"], 1)
                project(pe, (U_MIN + i) % 2, range(DT), h_hi, h_lo, (pjA, pjB)[i % 2])

            def spread_q():
                norm_spread_pe(pe, NQ, diag, 4).then_inc(NQ["bc"], 1)

            def sum_kv():
                norm_sum_pe(pe, NKV, 2, ssq, DT).then_inc(NKV["ms"], 1)

            def spread_kv():
                NQ.wait(pe, "h", 3)
                norm_spread_pe(pe, NKV, diag, 4).then_inc(NKV["bc"], 1)
            between = {1: spread_q, 3: sum_kv, 5: spread_kv}
            for i in range(DT):
                pe.wait_ge(w_split, U_Z + i + 3)
                if i == 0:
                    pe.wait_ge(min_read, 5)
                elif i == 1:
                    pe.wait_ge(kr_step, 2)
                else:
                    pe.wait_ge(z_read, i - 1)
                project(pe, (U_Z + i) % 2, range(DT), h_hi, h_lo, (pjA, pjB)[i % 2])
                if i in between:
                    between[i]()

        def mla_in_dve(dve):
            def add_squares(s, i):
                s.wait(dve, "sq", i + 1)
                if i == 0:
                    nc.vector.tensor_copy(ssq[:, :], sq[:, :]).then_inc(s["ssq"], 1)
                else:
                    s.wait(dve, "ssq", i)
                    nc.vector.tensor_tensor(ssq[:, :], ssq[:, :], sq[:, :], ALU.add).then_inc(s["ssq"], 1)
            for i in range(5):
                dve.wait_ge(unit_done, U_MIN + i + 3)
                nc.vector.tensor_copy(u5[:, i, :], flat((pjA, pjB)[i % 2])).then_inc(min_read, 1)
                if i < 3:
                    add_squares(NQ, i)
            dve.wait_ge(unit_done, U_MIN + 5 + 3)
            ps = flat(pjB)
            nc.vector.scalar_tensor_tensor(tmp[0][CR, :], ps[CR, :], MLA_SCALE, cos_sin[CR, :], ALU.mult, ALU.mult).then_inc(kr_step, 1)
            nc.vector.scalar_tensor_tensor(tmp[1][CR, :], ps[SR, :], MLA_SCALE, cos_sin[SR, :], ALU.mult, ALU.mult).then_inc(kr_step, 1)
            dve.wait_ge(kr_step, 2)
            nc.vector.tensor_tensor(k_rope[CR, :], tmp[0][CR, :], tmp[1][CR, :], ALU.add).then_inc(kr_step, 1)
            norm_diag(dve, NQ)
            NQ.wait(dve, "ms", 1)
            for i in range(2):
                add_squares(NKV, i)
            NQ.wait(dve, "bc", 1)
            for k in range(3):
                norm_scaled(NQ, u5[:, k, :], u5[:, k, :], vec[:, V_QN + k:V_QN + k + 1]).then_inc(NQ["h"], 1)
            norm_spread(dve, NKV)
            for k in range(2):
                norm_scaled(NKV, u5[:, 3 + k, :], u5[:, 3 + k, :], vec[:, V_KVN + k:V_KVN + k + 1]).then_inc(NKV["h"], 1)
            for s, n, k0, hi, lo in ((NQ, 3, 0, cq_hi, cq_lo), (NKV, 2, 3, ckv_hi, ckv_lo)):
                s.wait(dve, "h", n)
                for k in range(n):
                    s.wait(dve, "hi", k + 1)
                    nc.vector.tensor_tensor(lo[:, k, :], u5[:, k0 + k, :], hi[:, k, :].bitcast(F32), ALU.subtract).then_inc(s["lo"], 1)

        def mla_in_act(act):
            def square(s, i, k):
                if i:
                    s.wait(act, "ssq", i)
                nc.scalar.activation(sq[:, :], u5[:, k, :], ACT.Square).then_inc(s["sq"], 1)
            for i in range(3):
                act.wait_ge(min_read, i + 1)
                square(NQ, i, i)
            act.wait_ge(min_read, 5)
            NQ.wait(act, "ssq", 3)
            square(NKV, 0, 3)
            norm_root(act, NQ, QL)
            square(NKV, 1, 4)
            for i in range(DT):
                if i == 4:
                    norm_root(act, NKV, KVL, DT)
                act.wait_ge(unit_done, U_Z + i + 3)
                nc.scalar.activation(mix[:, i, :], flat((pjA, pjB)[i % 2]), ACT.Silu).then_inc(z_read, 1)
            for s, n, k0, hi in ((NQ, 3, 0, cq_hi), (NKV, 2, 3, ckv_hi)):
                s.wait(act, "h", n)
                for k in range(n):
                    nc.scalar.activation(hi[:, k, :], u5[:, k0 + k, :], ACT.Copy).then_inc(s["hi"], 1)

        mla.n_lo = 3
        rope_x = at("rope_x", R_W + 16384, [P, T])
        rope_y = at("rope_y", R_W, [P, T])

        def mla_project(pe, n, b, first_scores):
            def first_head_pe(slot, kts, hi, lo, dst, s):
                for i, kt in enumerate(kts):
                    s.wait(pe, "lo", i + 1)
                    for half in range(2):
                        for k, (w, a) in enumerate(((w_lo, hi), (w_hi, lo), (w_hi, hi))):
                            last = nc.tensor.matmul(dst[:, half, :], w[slot][:, kt, :], a[:, i, cols(half)], start=(i == 0 and k == 0),
                                                    stop=(i == len(kts) - 1 and k == 2))
                return last
            pe.wait_ge(w_split, n + (U_HEAD + 3))
            slot = (U_HEAD + b) % 2
            if isinstance(n, int) and n == 0:
                first_head_pe(slot, (0, 1, 2), cq_hi, cq_lo, pjA, NQ).then_inc(q_ready, 1)
                first_head_pe(slot, (3, 4), ckv_hi, ckv_lo, pjB, NKV).then_inc(unit_done, 1)
                return
            project(pe, slot, (0, 1, 2), cq_hi, cq_lo, pjA, done=False).then_inc(q_ready, 1)
            pe.wait_ge(mla.vaug_done, n * 2)
            pe.wait_ge(mla.cneg_done, n)
            project(pe, slot, (3, 4), ckv_hi, ckv_lo, pjB, done=False, halves=(0,))
            first_scores()
            project(pe, slot, (3, 4), ckv_hi, ckv_lo, pjB, halves=(1,))

        q_ready = sem("mla_q_ready")

        def mla_setup_act(act):
            act.wait_ge(kr_step, 3)
            for b in range(2):
                nc.scalar.activation(mla.bufs[2][b][CR, :], k_rope[CR, :], ACT.Copy).then_inc(mla.setup, 1)

        def mla_setup_dve(dve):
            NKV.wait(dve, "lo", 2)
            dve.wait_ge(mla.setup, 2)
            for b in range(2):
                nc.vector.tensor_tensor(mla.bufs[3][b][CR, :], k_rope[CR, :], mla.bufs[2][b][CR, :].bitcast(F32), ALU.subtract)\
                    .then_inc(mla.setup, 1)

        def mla_constants_pool(pool):
            pool.wait_ge(unit_done, U_Z + DT + 2)
            NKV.wait(pool, "lo", 2)
            q_hi, q_lo, k_hi, k_lo, vaug = mla.bufs
            pool.wait_ge(w_split, U_HEAD + 1 + 2)
            n = 0
            for b in range(2):
                for dst, value in ((q_lo[b][96:97, :], 0.0), (k_hi[b][96:97, :], 1.0), (k_lo[b][96:97, :], 0.0), (vaug[b][:, :, HD:P], 1.0)):
                    nc.gpsimd.memset(dst.bitcast(F32), value).then_inc(mla_constants, 1)
                    n += 1
                    pool.wait_ge(mla_constants, n)

        mla_constants = sem("mla_constants")

        def mla_prepare_act(act, n, b, turn):
            q_hi, q_lo, k_hi, k_lo, vaug = mla.bufs
            q, kv = flat(pjA), flat(pjB)
            act.wait_ge(q_ready, n + 1)
            nc.scalar.activation(q_hi[b][0:HD, :], q[0:HD, :], ACT.Copy, scale=MLA_SCALE).then_inc(mla.hi_done, 1)

            def keys():
                act.wait_ge(unit_done, n + (U_HEAD + 3))
                nc.scalar.activation(k_hi[b][0:HD, :], kv[0:HD, :], ACT.Copy).then_inc(mla.hi_done, 1)

            def values():
                if not (isinstance(n, int) and n == 0):
                    act.wait_ge(mla.vt_ready, n)
                nc.scalar.activation(mla_vT[:, :], kv[HD:P, :], ACT.Copy).then_inc(mla.vT_done, 1)

            def rope():
                act.wait_ge(mla.rope_done, n * 3 + 3)
                nc.scalar.activation(q_hi[b][CR, :], rope_x[CR, :], ACT.Copy).then_inc(mla.hi_done, 1)
            return {1: keys, 3: rope, 4: values}

        def mla_prepare_dve(dve, n, b):
            q_hi, q_lo, k_hi, k_lo, vaug = mla.bufs
            q, kv = flat(pjA), flat(pjB)
            dve.wait_ge(q_ready, n + 1)
            if not (isinstance(n, int) and n == 0):
                dve.wait_ge(mla.lo_done, n * 3)
            nc.vector.tensor_tensor(rope_x[CR, :], q[CR, :], cos_sin[CR, :], ALU.mult).then_inc(mla.rope_done, 1)
            nc.vector.tensor_tensor(rope_y[CR, :], q[SR, :], cos_sin[SR, :], ALU.mult).then_inc(mla.rope_done, 1)
            dve.wait_ge(mla.rope_done, n * 3 + 2)
            nc.vector.tensor_tensor(rope_x[CR, :], rope_x[CR, :], rope_y[CR, :], ALU.add).then_inc(mla.rope_done, 1)
            dve.wait_ge(mla.hi_done, n * 3 + 1)
            nc.vector.scalar_tensor_tensor(q_lo[b][0:HD, :], q[0:HD, :], MLA_SCALE, q_hi[b][0:HD, :].bitcast(F32),
                                           ALU.mult, ALU.subtract).then_inc(mla.lo_done, 1)
            dve.wait_ge(mla.hi_done, n * 3 + 2)
            nc.vector.tensor_tensor(k_lo[b][0:HD, :], kv[0:HD, :], k_hi[b][0:HD, :].bitcast(F32), ALU.subtract).then_inc(mla.lo_done, 1)
            dve.wait_ge(mla.hi_done, n * 3 + 3)
            dve.wait_ge(mla.rope_done, n * 3 + 3)
            nc.vector.tensor_tensor(q_lo[b][CR, :], rope_x[CR, :], q_hi[b][CR, :].bitcast(F32), ALU.subtract).then_inc(mla.lo_done, 1)

        m2_hi, m2_lo, mo_added = sem("mix2_hi"), sem("mix2_lo"), sem("mo_added")
        p_in, p_hi_done, p_lo_done = sem("p_in"), sem("p_hi_done"), sem("p_lo_done")
        pg_read, pp_read, ple_added = sem("ple_gate_read"), sem("emb_read"), sem("ple_added")
        ple_mul, pp_ready = sem("ple_mul"), sem("emb_ready")
        p_raw = at("p_raw", R_S, [P, 2, T])
        p_hi, p_lo = at("p_hi", R_S + 8192, [P, 2, T], F32R), at("p_lo", R_S + 16384, [P, 2, T], F32R)
        emb = at("emb", R_M, [P, DT, T])
        result = at("result", R_H, [P, DT, T])

        def emb_unit(pe, e):
            kts = (e % 4 * 2, e % 4 * 2 + 1)
            last = project(pe, (U_PLE + e // 4) % 2, kts, p_hi, p_lo, (pjA, pjB)[e % 2], done=e % 4 == 3)
            if e % 4 < 3:
                last.then_inc(pp_ready, 1)

        def ple_pe(pe):
            pe.wait_ge(p_lo_done, 1)
            for e in range(DT):
                if e % 4 == 0:
                    pe.wait_ge(w_split, U_PLE + e // 4 + 3)
                if e < 2:
                    pe.wait_ge(mo_added, DT - 1 + e + 2)
                else:
                    pe.wait_ge(pp_read, e - 1)
                emb_unit(pe, e)
                if e == 1:
                    norm_sum_pe(pe, N4, DT + 1, ssq).then_inc(N4["ms"], 1)
                if e == 3:
                    norm_spread_pe(pe, N4, diag, 4).then_inc(N4["bc"], 1)

            def arrived(i):
                if i == 0:
                    pe.wait_ge(pp_read, DT)
                N4.wait(pe, "lo", i + 1)
            project_tiles(pe, ((U_GATE, pjA),), range(DT), h_hi, h_lo, arrived)
            pe.wait_ge(w_split, U_GATE + 1 + 3)
            project(pe, (U_GATE + 1) % 2, range(DT), h_hi, h_lo, pjB)
            halved_pe(pe, U_GATE, range(DT), h_hi, h_lo, pg_read, 0, (lambda: half_sum_pe(pe, N5, DT + 1, 0), lambda: half_spread_pe(pe, N5, 0)))
            half_sum_pe(pe, N5, N_HALVED + 1, 1)
            half_spread_pe(pe, N5, 1)

        def emb_act(act):
            for e in range(DT):
                act.wait_ge(unit_done if e % 4 == 3 else pp_ready, U_PLE + e // 4 + 3 if e % 4 == 3 else e - e // 4 + 1)
                nc.scalar.activation(emb[:, e, :], flat((pjA, pjB)[e % 2]), ACT.Copy).then_inc(pp_read, 1)
                if e == 1:
                    norm_root(act, N4, D)
                if e >= 4:
                    norm_split_act(act, N4, (e - 4,), hi_tile)

        def ple_act(act):
            def gate(src, c, j, n):
                act.wait_ge(unit_done, n + (U_GATE + 3))
                act.wait_ge(ple_added, n + 1)
                nc.scalar.activation(tmp[j][:, c], src, ACT.Sigmoid).then_inc(pg_read, 1)
            halved_act(act, ple_added, 2, N5, {0: lambda: half_root(act, N5, 0)}, gate)
            half_root(act, N5, 1)

        def ple_dve(dve):
            dve.wait_ge(N4["lo"], N4.base["lo"] + DT)

            def gated(i, c, n, j):
                tile, product = flat(x[:, bass.ds(i, 1), c]), tmp[j][:, c]
                dve.wait_ge(pg_read, n + 1)
                nc.vector.tensor_tensor(product, flat(emb[:, bass.ds(i, 1), c]), product, ALU.mult).then_inc(ple_mul, 1)
                dve.wait_ge(ple_mul, n + 1)
                nc.vector.tensor_tensor(tile, product, tile, ALU.add).then_inc(ple_added, 1)

            def scale(half, tiles):
                for k in tiles:
                    nc.vector.scalar_tensor_tensor(result[:, k, cols(half)], x[:, k, cols(half)], vec[:, V_FN + k:V_FN + k + 1],
                                                   PS[:, 4 + half, :], ALU.mult, ALU.mult).then_inc(N5["h"], 1)

            def after1():
                N5.wait(dve, "bc", 1)
                scale(0, range(3))
            halved_dve(dve, U_GATE, ple_added, N5, {0: lambda: half_diag(dve, N5, 0), 1: after1, 2: lambda: scale(0, range(3, 6)),
                                                    3: lambda: scale(0, range(6, DT))}, gated)
            half_diag(dve, N5, 1)
            N5.wait(dve, "bc", 2)
            scale(1, range(DT))

        stage = at("const_stage", R_M, [P, N_CONST])
        pos_i = at("pos_i", R_S + 8192, [P, T], I32)
        ang = [at(f"ang{i}", R_S + 12288 + 4096 * i, [P, T]) for i in range(4)]

        def setup_dve(dve):
            dve.wait_ge(consts_in, 16)
            for dst, k, n in ((ident[:, :], K_ID, P), (ones[:, :], K_ONE, P), (head_mean[:, :], K_BLK, P),
                              (ident_bf[:, :], K_ID, P), (masks[:, :, :].rearrange("p a n -> p (a n)"), K_MASK, 1024),
                              (att_mask[:, :], K_ATT, P), (small_const[:, :], K_CNT, 40)):
                nc.vector.tensor_copy(dst, stage[:, k:k + n]).then_inc(setup_done, 1)

        N_SETUP = 7

        ROPE_STEPS = 11

        def rope_dve(dve):
            r = slice(64, 128)
            two_pi = 2 * np.pi
            c1 = 6.28125
            c2 = float(np.floor((two_pi - c1) * 2 ** 20) / 2 ** 20)
            c3 = float(two_pi - c1 - c2)
            magic = 1.5 * 2 ** 23
            freq, sign = small_const[r, 32:33], small_const[SR, 33:34]
            a, turns, s = ang[0][r, :], ang[1][r, :], ang[2]
            lim = 3.14159
            steps = [lambda: nc.vector.tensor_copy(a, pos_i[r, :]),
                     lambda: nc.vector.tensor_scalar(a, a, freq, None, ALU.mult),
                     lambda: nc.vector.tensor_scalar(turns, a, float(1 / two_pi), magic, ALU.mult, ALU.add),
                     lambda: nc.vector.tensor_scalar(turns, turns, magic, None, ALU.subtract),
                     lambda: nc.vector.scalar_tensor_tensor(a, turns, -c1, a, ALU.mult, ALU.add),
                     lambda: nc.vector.scalar_tensor_tensor(a, turns, -c2, a, ALU.mult, ALU.add),
                     lambda: nc.vector.scalar_tensor_tensor(a, turns, -c3, a, ALU.mult, ALU.add),
                     lambda: nc.vector.tensor_scalar(a, a, lim, -lim, ALU.min, ALU.max),
                     lambda: nc.vector.tensor_tensor(s[CR, :], s[CR, :], s[CR, :], ALU.mult),
                     lambda: nc.vector.tensor_scalar(cos_sin[CR, :], s[CR, :], -2.0, 1.0, ALU.mult, ALU.add),
                     lambda: nc.vector.tensor_scalar(cos_sin[SR, :], s[SR, :], sign, None, ALU.mult)]

            def run(k):
                if k == 0:
                    dve.wait_ge(pos_in, 16)
                    dve.wait_ge(setup_done, N_SETUP)
                else:
                    dve.wait_ge(rope_s, k)
                if k == 8:
                    dve.wait_ge(rope_a, 2)
                steps[k]().then_inc(rope_s, 1)
            return run

        def rope_act(act):
            act.wait_ge(rope_s, 8)
            nc.scalar.activation(ang[2][CR, :], ang[0][CR, :], ACT.Sin, scale=0.5).then_inc(rope_a, 1)
            nc.scalar.activation(ang[2][SR, :], ang[0][SR, :], ACT.Sin).then_inc(rope_a, 1)

        second_sq = at("second_sq", R_M + 16384, [P, T])
        first_sq = (sq, second_sq)


        def first_total_dve(dve, half, k):
            i = half * DT + k
            c = cols(half)
            N1.wait(dve, "sq", i + 1)
            part = first_sq[k % 2]
            if k == 0:
                nc.vector.tensor_copy(ssq[:, c], part[:, c]).then_inc(N1["ssq"], 1)
            else:
                N1.wait(dve, "ssq", i)
                nc.vector.tensor_tensor(ssq[:, c], ssq[:, c], part[:, c], ALU.add).then_inc(N1["ssq"], 1)

        def first_norm_dve(dve):
            for k in range(DT):
                first_total_dve(dve, 0, k)
            dve.wait_ge(vecs_in, 16)
            dve.wait_ge(setup_done, N_SETUP)
            half_diag(dve, N1, 0)
            N1.wait(dve, "bc", 1)
            for k in range(DT + 1):
                half_split_dve(dve, N1, 0, k, gain_of(V_LN1))
                if k < DT:
                    first_total_dve(dve, 1, k)
            half_diag(dve, N1, 1)
            N1.wait(dve, "bc", 2)
            for k in range(DT + 1):
                half_split_dve(dve, N1, 1, k, gain_of(V_LN1))

        def first_norm_act(act):
            def square(half, k):
                i = half * DT + k
                act.wait_ge(x_in[half * 4 + k // 2], 16)
                if k >= 2:
                    N1.wait(act, "ssq", i - 1)
                nc.scalar.activation(first_sq[k % 2][:, cols(half)], x[:, k, cols(half)], ACT.Square).then_inc(N1["sq"], 1)
            for k in range(DT):
                square(0, k)
            act.wait_ge(setup_done, N_SETUP)
            half_root(act, N1, 0)
            for k in range(DT):
                square(1, k)
                half_split_act(act, N1, 0, k)
            half_root(act, N1, 1)
            for k in range(DT):
                half_split_act(act, N1, 1, k)

        def first_norm_pe(pe):
            half_sum_pe(pe, N1, DT, 0)
            half_spread_pe(pe, N1, 0)

            def arrived(half, k):
                if (half, k) == (1, 0):
                    half_sum_pe(pe, N1, 2 * DT, 1)
                    half_spread_pe(pe, N1, 1)
                N1.wait(pe, "lo", half * DT + k + 1)
            project_by_half(pe, ((U_SMALL, pjA), (U_FV[0], FV_BANKS[0])), h_hi, h_lo, arrived, (True, False))

        block = ctx.enter_context(nc.Block())

        @block.sync
        def _(sp):
            sp.dma_start(stage[:, :], consts).then_inc(consts_in, 16)
            sp.dma_start(vec[:, :], vecs).then_inc(vecs_in, 16)
            sp.wait_ge(x_in[3], 16)
            sp.dma_start(pos_i[:, :], pos).then_inc(pos_in, 16)

            def load(u, s):
                sp.wait_ge(w_split, u + 1)
                sp.dma_start(raw[s][:, :, :].rearrange("p k n -> p (k n)"), wpack[u, :, :] if isinstance(u, int) else
                             wpack[bass.ds(u, 1), :, :].rearrange("o p n -> (o p) n")).then_inc(w_loaded[s], 16)
            with sp.Fori(0, N_UNITS // 2) as it:
                for s in range(2):
                    load(it * 2 + s, s)
            if N_UNITS % 2:
                load(N_UNITS - 1, 0)
            for half in range(2):
                for i in range(DT // 2):
                    N5.wait(sp, "h", half * DT + 2 * i + 2)
                    k = 2 * i
                    sp.dma_start(outT[k * P:(k + 2) * P, cols(half)].rearrange("(k p) t -> p k t", p=P), result[:, k:k + 2, cols(half)])\
                        .then_inc(out_stored, 16)
            sp.wait_ge(out_stored, 16 * DT)

        @block.gpsimd
        def _(pool):
            pool.sem_inc(w_split, 2)
            nc.gpsimd.memset(zero[:, :], 0.0).then_inc(zero_set, 1)
            pool.wait_ge(zero_set, 1)
            no_change = zero[:, :].rearrange("p (a n) -> p a n", a=1).to_broadcast([P, DT, P])

            def split(u, s, loads, kts=slice(0, DT)):
                pool.wait_ge(w_loaded[s], loads)
                pool.wait_ge(unit_done, u + 1)
                nc.gpsimd.tensor_tensor(w_hi[s][:, kts, :], raw[s][:, kts, :], no_change[:, kts, :], ALU.add).then_inc(w_hi_done, 1)
                pool.wait_ge(w_hi_done, u + 1)
                nc.gpsimd.tensor_tensor(w_lo[s][:, kts, :], raw[s][:, kts, :], w_hi[s][:, kts, :].bitcast(F32), ALU.subtract)\
                    .then_inc(w_split, 1)

            def units(first, end, kts=DT):
                k = slice(0, kts)
                with pool.Fori(0, (end - first) // 2) as it:
                    for j in range(2):
                        split(it * 2 + (first + j), (first + j) % 2, it * 16 + ((first + j) // 2 * 16 + 16), k)
                if (end - first) % 2:
                    split(end - 1, (end - 1) % 2, (end - 1) // 2 * 16 + 16, k)

            def heads(A, first):
                def step(n, b, turn):
                    u = first + b + 1
                    split(turn * 2 + u, u % 2, turn * 16 + (u // 2 * 16 + 16))
                    if not (isinstance(n, int) and n == 0):
                        for g in range(N_PIECES):
                            low_pool(pool, A, n - 1, g)
                steps(pool, A, step)
                for g in range(N_PIECES):
                    low_pool(pool, A, A.heads - 1, g)
            units(0, U_FQK + 1)
            fox_constants_pool(pool)
            heads(fox, U_FQK)
            units(U_FQK + FOX_H + 1, U_DN[-1])
            units(U_DN[-1], U_MIN, MLP_CHUNKS[-1])
            units(U_MIN, U_HEAD + 1)
            mla_constants_pool(pool)
            heads(mla, U_HEAD)
            units(U_HEAD + MLA_H + 1, N_UNITS)

        @block.scalar
        def _(act):
            act.sem_inc(fox.pv_done, 4)
            act.sem_inc(fox.pv_hi, 2)
            act.sem_inc(fox.p_lo_done, 2)
            act.sem_inc(mla.pv_done, 4)
            act.sem_inc(mla.pv_hi, 2)
            act.sem_inc(mla.p_lo_done, 2)
            act.sem_inc(gate_read, 1)
            for i in range(DT):
                c = cols(i // 4)
                k = i % 4 * 2
                act.dma_start(x[:, k:k + 2, c], xT[k * P:(k + 2) * P, c].rearrange("(k p) t -> p k t", p=P)).then_inc(x_in[i], 16)
            first_norm_act(act)
            small_act(act)
            fox_values_act(act, 0)
            rope_act(act)
            fox_values_act(act, 1)
            act.preload_act_table_set(LN_EXP)
            steps(act, fox, lambda n, b, turn: step_act(act, fox, n, b, turn, fox_prepare_act))
            last_act(act, fox)
            rest_act(act)
            gla_act(act)
            halved_norm_act(act, wo_added, 0, N2)
            mlp_act(act)
            mla_in_act(act)
            mla_setup_act(act)
            act.preload_act_table_set(LN_EXP)
            steps(act, mla, lambda n, b, turn: step_act(act, mla, n, b, turn, mla_prepare_act))
            last_act(act, mla, lambda k: mix_hi_act(k, m2_hi))
            act.wait_ge(mla.norm_done, 2 * MLA_H)
            mix_hi_act(DT - 1, m2_hi)
            act.dma_start(p_raw[:, :, :], pT.rearrange("(k p) t -> p k t", p=P)).then_inc(p_in, 16)
            act.wait_ge(p_in, 16)
            nc.scalar.activation(tau(p_hi), tau(p_raw), ACT.Copy).then_inc(p_hi_done, 1)
            residual_squares(act, mo_added, 0, N4)
            emb_act(act)
            norm_split_act(act, N4, range(4, DT), hi_tile)
            ple_act(act)

        @block.vector
        def _(dve):
            for s, credit in ((up_read, 1), (dn_added, 2), (a_split_lo, 1), (ple_added, 2), (mo_added, 2)):
                dve.sem_inc(s, credit)
            rope_step = rope_dve(dve)
            setup_dve(dve)
            first_norm_dve(dve)
            small_dve(dve)
            for k in range(ROPE_STEPS):
                rope_step(k)
            steps(dve, fox, lambda n, b, turn: step_dve(dve, fox, n, b, turn, fox_prepare_dve, 4, False))
            for half in range(2):
                norm_half_dve(dve, fox, FOX_H - 1, 1, half, 4 + FOX_H // 2 - 1, False)
            gla_dve(dve)
            dve.wait_ge(x_back, 16 * DT)
            halved_norm_dve(dve, U_WO, wo_added, N2, gain_of(V_LN2))
            mlp_dve(dve)
            mla_in_dve(dve)
            mla_setup_dve(dve)
            steps(dve, mla, lambda n, b, turn: step_dve(dve, mla, n, b, turn, mla_prepare_dve, 0, True))
            norm_half_dve(dve, mla, MLA_H - 1, 1, 0, MLA_H // 2 - 1, True)
            for k in range(2):
                mix_lo_dve(dve, k, k, m2_hi, m2_lo)
            norm_half_dve(dve, mla, MLA_H - 1, 1, 1, MLA_H // 2 - 1, True)
            for k in range(2, DT - 1):
                mix_lo_dve(dve, k, k, m2_hi, m2_lo)
            mix_lo_dve(dve, DT - 1, DT - 1, m2_hi, m2_lo)
            dve.wait_ge(p_hi_done, 1)
            nc.vector.tensor_tensor(tau(p_lo), tau(p_raw), tau(p_hi).bitcast(F32), ALU.subtract).then_inc(p_lo_done, 1)
            residual_dve(dve, U_MO, mo_added, 0, N4)
            norm_spread(dve, N4)
            norm_split_dve(dve, N4, DT, lambda k: x[:, k, :], lambda k: None, hi_tile, lo_tile)
            ple_dve(dve)

        @block.tensor
        def _(pe):
            pe.sem_inc(unit_done, 2)
            pe.wait_ge(setup_done, N_SETUP)
            first_norm_pe(pe)
            fox_values_pe(pe)
            steps(pe, fox, lambda n, b, turn: step_pe(pe, fox, n, b, turn, fox_project, fox_vT))
            last_pe(pe, fox)
            rest_pe(pe)
            gla_pe(pe)
            def mix_part(i):
                if i == 0:
                    pe.wait_ge(g_o, 2)
                if i == 1:
                    for c in range(2):
                        gla_mean_pe(pe, c)
                pe.wait_ge(m_lo, i + 1)
            project_tiles(pe, ((U_WO, pjA), (U_WO + 1, pjB)), MIX_ORDER, h_hi, mix_lo, mix_part)
            halved_norm_pe(pe, U_WO, range(DT), h_hi, mix_lo, wo_added, 0, N2, U_GU[0])
            mlp_pe(pe)
            mla_in_pe(pe)
            pe.wait_ge(z_read, DT)
            steps(pe, mla, lambda n, b, turn: step_pe(pe, mla, n, b, turn, mla_project, mla_vT))
            last_pe(pe, mla)
            project_tiles(pe, ((U_MO, pjA),), range(DT), h_hi, mix_lo, lambda i: pe.wait_ge(m2_lo, i + 1))
            pe.wait_ge(w_split, U_MO + 1 + 3)
            project(pe, (U_MO + 1) % 2, range(DT), h_hi, mix_lo, pjB)
            units_pe(pe, U_MO + 2, DT - 2, range(DT), h_hi, mix_lo, lambda it, j: pe.wait_ge(mo_added, it * 2 + (j + 3)))
            ple_pe(pe)


def shape_constants():
    c = np.zeros((P, N_CONST), np.float32)
    i = np.arange(P)
    c[:, K_ID:K_ID + P] = np.eye(P)
    c[:, K_ONE:K_ONE + P] = 1.0
    c[:, K_BLK:K_BLK + P] = (i[:, None] // HD == i[None, :] // HD) / HD
    later = i[None, :] > i[:, None]
    chunk_later = i[None, :] // CHUNK > i[:, None] // CHUNK
    for k, m in ((0, later), (2, chunk_later)):
        by_query = c[:, K_MASK + 256 * k:K_MASK + 256 * (k + 1)]
        by_query[:, 0:P], by_query[:, P:] = m * NEG, NEG
        by_key = c[:, K_MASK + 256 * (k + 1):K_MASK + 256 * (k + 2)]
        by_key[:, 0:P], by_key[:, P:] = NEG, m.T * NEG
    c[:, K_ATT:K_ATT + P] = (i[:, None] // CHUNK == i[None, :] // CHUNK) & (i[:, None] <= i[None, :])
    t = np.arange(16)
    for tile, row, w in ((0, 0, 2), (0, HD, 4), (1, 0, 8), (1, HD, 16)):
        c[row:row + HD, K_CNT + 16 * tile:K_CNT + 16 * tile + 16] = 1.0 / np.minimum(t + 1, w)
    half = ROPE // 2
    c[:, K_FREQ] = (np.float32(ROPE_THETA) ** (-np.arange(0, ROPE, 2, dtype=np.float32) / np.float32(ROPE)))[i % half]
    c[:, K_SIGN] = np.where(i % ROPE < half, -1.0, 1.0)
    c[:, K_EPS] = EPS
    c[:, K_EPS + 1] = 1.0
    return c


def halved_tile(i):
    return i if i < DT else i - (DT - 2)


def pack_units(w_in, w_o, w_gu, w_down, mla_in, w_q_b, w_kv_b, mla_out, ple_gate, ple_proj):
    units = np.zeros((N_UNITS, P, DT, P), np.float32)

    def put(u, w, cols, kt0=0, to=0, rows=slice(None)):
        part = w[rows][:, cols]
        k = part.shape[0] // P
        units[u, :, kt0:kt0 + k, to:to + part.shape[1]] = part.reshape(k, P, -1).transpose(1, 0, 2)

    def tile(c0, n=P):
        return slice(c0, c0 + n)

    put(U_SMALL, w_in, tile(C_GA, 16))
    put(U_SMALL, w_in, tile(C_FF, FOX_H), to=32)
    for i in range(FOX_H // 2):
        put(U_FV[i], w_in, tile(C_FV + P * i))
    for h in range(FOX_H):
        put(U_FQK + h if h else U_FQK0, w_in, tile(C_FQ + HD * h, HD))
        put(U_FQK + h if h else U_FQK0, w_in, tile(C_FK + HD * h, HD), to=HD)
    for i in range(N_REST):
        put(U_REST + i, w_in, tile(P * i))
    for i in range(N_HALVED):
        put(U_WO + i, w_o, tile(P * halved_tile(i)))
        put(U_GATE + i, ple_gate, tile(P * halved_tile(i)))
    f0 = 0
    for c, n in enumerate(MLP_CHUNKS):
        for f in range(n):
            put(U_GU[c] + 2 * f, w_gu, tile(P * (f0 + f)))
            put(U_GU[c] + 2 * f + 1, w_gu, tile(FF + P * (f0 + f)))
        for i in range(DT if c < len(MLP_CHUNKS) - 1 else N_HALVED):
            put(U_DN[c] + i, w_down, tile(P * halved_tile(i)), rows=slice(P * f0, P * (f0 + n)))
        f0 += n
    for i in range(5):
        put(U_MIN + i, mla_in, tile(P * i))
    half = ROPE // 2
    k0 = QL + KVL
    put(U_MIN + 5, mla_in, tile(k0, ROPE), to=64)
    put(U_MIN + 5, mla_in, tile(k0 + half, half), to=96)
    put(U_MIN + 5, mla_in, tile(k0, half), to=96 + half)
    for i in range(DT):
        put(U_Z + i, mla_in, tile(k0 + ROPE + P * i))
    for h in range(MLA_H):
        q0 = (NOPE + ROPE) * h
        put(U_HEAD + h, w_q_b, tile(q0, NOPE + ROPE))
        put(U_HEAD + h, w_q_b, tile(q0 + NOPE + half, half), to=96)
        put(U_HEAD + h, w_q_b, tile(q0 + NOPE, half), to=96 + half)
        put(U_HEAD + h, w_kv_b, tile(P * h), kt0=3)
    for i in range(DT):
        put(U_MO + i, mla_out, tile(P * i))
        put(U_PLE + i // 4, ple_proj, tile(P * i), kt0=i % 4 * 2)
    return units.reshape(N_UNITS, P, DT * P)


def pack_vectors(inputs):
    v = np.zeros((P, N_VEC), np.float32)
    for col, name in ((V_LN1, "ln1"), (V_LN2, "ln2"), (V_LNF, "ln_f"), (V_FN, "final_norm_2"), (V_NG, "norm_g_2"), (V_GN, "gla_gn"), (V_BA, "b_a"),
                      (V_PS, "pool_scale"), (V_QN, "mla_q_norm_2"), (V_KVN, "mla_kv_norm_2")):
        a = np.asarray(inputs[name]).reshape(-1, P)
        v[:, col:col + a.shape[0]] = a.T
    v[32:32 + FOX_H, V_BF] = np.asarray(inputs["b_f"])[0]
    w = np.asarray(inputs["w_pool"])[0]
    for g in range(4):
        r = HD * (g % 2)
        v[r:r + HD, V_WPOOL + P * (g // 2) + r:V_WPOOL + P * (g // 2) + r + HD] = w[g]
    v[0:16, V_WAUP:V_WAUP + GLA_W] = np.asarray(inputs["w_a_up"])[0]
    return v


def kernel(**inputs):
    import concourse.bacc as bacc
    from concourse.bass_utils import run_bass_kernel_spmd

    def first(name):
        return np.asarray(inputs[name])[0]

    arrays = {
        "wpack": pack_units(first("w_in"), first("w_o"), first("w_gu"), first("w_down"), first("mla_w_in_2"),
                            first("mla_w_q_b_2"), first("mla_w_kv_b_2"), first("mla_w_out_2"), first("ple_gate_2"),
                            first("ple_proj_2")),
        "xT": np.ascontiguousarray(first("x").T),
        "pT": np.ascontiguousarray(np.asarray(inputs["p_2"])[0, 0].T),
        "vecs": pack_vectors(inputs),
        "consts": shape_constants(),
        "pos": np.ascontiguousarray(np.broadcast_to(np.asarray(inputs["positions_2"]), (P, T))),
    }
    nc = bacc.Bacc("TRN2", target_bir_lowering=False, num_devices=1)
    args = [nc.dram_tensor(f"in_{n}", a.shape, mybir.dt.from_np(a.dtype), kind="ExternalInput").ap() for n, a in arrays.items()]
    out = nc.dram_tensor("out", (D, T), F32, kind="ExternalOutput").ap()
    f_rows = nc.dram_tensor("f_rows", (2, FOX_H, T), F32).ap()
    build(nc, *args, out, f_rows)
    r = run_bass_kernel_spmd(nc, [{f"in_{n}": a for n, a in arrays.items()}], core_ids=[0])
    return np.ascontiguousarray(r.results[0]["out"].T).reshape(1, T, D)
```
